# Optimizing a Trainium2 kernel written in Bass

```python
import math
import jax, jax.numpy as jnp
from jax import lax
import numpy as np

D_MODEL = 1024
BATCH = 1
SEQ = 512
DEPTH = 2
DEC_BATCH = 8
DEC_SEQ = 8
PAST_LEN = 4096
PAGE_SIZE = 128

POOL_WIDTH = D_MODEL // 2
POOL_WINDOWS = (2, 4, 8, 16)
POOL_GROUPS = len(POOL_WINDOWS)
POOL_GROUP_DIM = POOL_WIDTH // POOL_GROUPS
POOL_BUF = max(POOL_WINDOWS) - 1
RET_WIDTH = D_MODEL - POOL_WIDTH
RET_HEADS = 4
RET_HEAD_DIM = RET_WIDTH // RET_HEADS
RET_CHUNK = 128
ROPE_BASE = 10000.0
IN_WIDTH = POOL_WIDTH + 4 * RET_WIDTH
N_EXPERT_GROUPS = 4
EXPERTS_PER_GROUP = 4
N_EXPERTS = N_EXPERT_GROUPS * EXPERTS_PER_GROUP
EXPERT_TOP_K = 2
D_EXPERT = D_MODEL // 4
RMS_EPS = 1e-6
GN_EPS = 1e-5

kernel_name = "hybrid_pool_retention_hmoe_step"

def rmsnorm(x, g):
    xf = x.astype(jnp.float32)
    y = xf * lax.rsqrt(jnp.mean(xf * xf, axis=-1, keepdims=True) + RMS_EPS)
    return (y * g.astype(jnp.float32)).astype(x.dtype)

def pool_mix(u, prev, n_prev, w_grp, scale):
    B, L, P = u.shape
    full = jnp.concatenate([prev, u], axis=1).astype(jnp.float32)
    c = lax.cumsum(full, axis=1)
    c = jnp.concatenate([jnp.zeros((B, 1, P), jnp.float32), c], axis=1)
    t_idx = jnp.arange(L)
    uf = u.astype(jnp.float32)
    outs = []
    for j, w in enumerate(POOL_WINDOWS):
        sl = slice(j * POOL_GROUP_DIM, (j + 1) * POOL_GROUP_DIM)
        s = c[:, POOL_BUF + 1:, sl] - c[:, POOL_BUF + 1 - w:POOL_BUF + 1 - w + L, sl]
        cnt = jnp.minimum(w, n_prev + t_idx + 1).astype(jnp.float32)
        outs.append(s / cnt[None, :, None] - uf[..., sl])
    d = jnp.concatenate(outs, axis=-1).reshape(B, L, POOL_GROUPS, POOL_GROUP_DIM)
    y = jnp.einsum('blgc,gce->blge', d, w_grp.astype(jnp.float32)).reshape(B, L, P)
    return y * scale.astype(jnp.float32)

def rope(x, pos):
    half = x.shape[-1] // 2
    inv = ROPE_BASE ** (-jnp.arange(half, dtype=jnp.float32) / half)
    ang = pos.astype(jnp.float32)[:, None] * inv[None, :]
    cos = jnp.cos(ang)[None, :, None, :]
    sin = jnp.sin(ang)[None, :, None, :]
    x1, x2 = x[..., :half], x[..., half:]
    return jnp.concatenate([x1 * cos - x2 * sin, x1 * sin + x2 * cos], axis=-1)

def retention(q, k, v, s0):
    B, H, L, D = q.shape
    C = RET_CHUNK if L % RET_CHUNK == 0 else L
    n = L // C
    log_g = jnp.log(1.0 - 2.0 ** (-5.0 - jnp.arange(H, dtype=jnp.float32)))
    i = jnp.arange(C, dtype=jnp.float32)
    diff = i[:, None] - i[None, :]
    decay_mat = jnp.where(diff[None] >= 0,
                          jnp.exp(jnp.maximum(diff, 0.0)[None] * log_g[:, None, None]), 0.0)
    q_decay = jnp.exp((i + 1.0)[None, :] * log_g[:, None])[..., None]
    k_decay = jnp.exp((C - 1.0 - i)[None, :] * log_g[:, None])[..., None]
    chunk_decay = jnp.exp(C * log_g)[:, None, None]

    def to_chunks(a):
        return a.reshape(B, H, n, C, D).transpose(2, 0, 1, 3, 4)

    def step(s, qkv):
        qc, kc, vc = qkv
        scores = jnp.einsum('bhid,bhjd->bhij', qc, kc) * decay_mat
        o = (jnp.einsum('bhij,bhjd->bhid', scores, vc)
             + jnp.einsum('bhid,bhde->bhie', qc * q_decay, s))
        s_new = s * chunk_decay + jnp.einsum('bhjd,bhje->bhde', kc * k_decay, vc)
        return s_new, o

    s_fin, o = lax.scan(step, s0, (to_chunks(q), to_chunks(k), to_chunks(v)))
    o = o.transpose(1, 2, 0, 3, 4).reshape(B, H, L, D)
    return o, s_fin

def mixer_block(x, pool_prev, n_prev, ret_s0, pos, norm_g, w_in, w_pool, pool_scale, gn_g, w_out):
    B, L, _ = x.shape
    h = rmsnorm(x, norm_g)
    z = h @ w_in
    P, R = POOL_WIDTH, RET_WIDTH
    u, q, k, v, g = jnp.split(z, [P, P + R, P + 2 * R, P + 3 * R], axis=-1)
    pool_out = pool_mix(u, pool_prev, n_prev, w_pool, pool_scale)
    new_buf = jnp.concatenate([pool_prev, u.astype(pool_prev.dtype)], axis=1)[:, -POOL_BUF:]
    shp = (B, L, RET_HEADS, RET_HEAD_DIM)
    qh = rope(q.reshape(shp).astype(jnp.float32), pos)
    kh = rope(k.reshape(shp).astype(jnp.float32), pos) * (RET_HEAD_DIM ** -0.5)
    vh = v.reshape(shp).astype(jnp.float32)
    o, s_fin = retention(qh.transpose(0, 2, 1, 3), kh.transpose(0, 2, 1, 3),
                         vh.transpose(0, 2, 1, 3), ret_s0.astype(jnp.float32))
    o = o.transpose(0, 2, 1, 3)
    mu = jnp.mean(o, axis=-1, keepdims=True)
    var = jnp.mean(jnp.square(o - mu), axis=-1, keepdims=True)
    o = ((o - mu) * lax.rsqrt(var + GN_EPS)).reshape(B, L, R) * gn_g.astype(jnp.float32)
    ret_out = jax.nn.silu(g.astype(jnp.float32)) * o
    mix = jnp.concatenate([pool_out, ret_out], axis=-1).astype(x.dtype) @ w_out
    return x + mix, new_buf, s_fin.astype(ret_s0.dtype)

def hier_moe(x, norm_g, w_rg, b_rg, w_re, b_re, w_gate, w_up, w_down):
    B, L, D = x.shape
    hf = rmsnorm(x, norm_g).reshape(B * L, D)
    T = B * L
    grp_logits = (hf @ w_rg).astype(jnp.float32) + b_rg.astype(jnp.float32)
    grp_prob = jax.nn.softmax(grp_logits, axis=-1)
    _, g_sel = lax.top_k(grp_logits, 1)
    exp_logits = ((hf @ w_re).astype(jnp.float32) + b_re.astype(jnp.float32)).reshape(
        T, N_EXPERT_GROUPS, EXPERTS_PER_GROUP)
    in_grp = jnp.take_along_axis(exp_logits, g_sel[:, :, None], axis=1)[:, 0]
    top_v, top_i = lax.top_k(in_grp, EXPERT_TOP_K)
    top_w = jax.nn.softmax(top_v, axis=-1) * jnp.take_along_axis(grp_prob, g_sel, axis=1)
    expert_idx = g_sel * EXPERTS_PER_GROUP + top_i
    gates = jnp.sum(jax.nn.one_hot(expert_idx, N_EXPERTS, dtype=jnp.float32) * top_w[..., None], axis=1)
    y = jnp.zeros((T, D), jnp.float32)
    for e in range(N_EXPERTS):
        act = jax.nn.silu((hf @ w_gate[e]).astype(jnp.float32)) * (hf @ w_up[e]).astype(jnp.float32)
        y = y + (act * gates[:, e:e + 1]).astype(x.dtype) @ w_down[e]
    return x + y.reshape(B, L, D).astype(x.dtype)

def setup_inputs(seed: int = 0) -> dict:
    key = jax.random.key(seed)
    ks = jax.random.split(key, 20)
    f32 = jnp.float32
    nrm = lambda k, s, sc: jax.random.normal(k, s, f32) * sc
    return {
        "x_prompt": nrm(ks[0], (BATCH, SEQ, D_MODEL), 1.0),
        "x_sample": nrm(ks[1], (DEC_BATCH, DEC_SEQ, D_MODEL), 1.0),
        "cache_pool": nrm(ks[2], (DEPTH, DEC_BATCH, POOL_BUF, POOL_WIDTH), 1.0),
        "state_ret": nrm(ks[3], (DEPTH, DEC_BATCH, RET_HEADS, RET_HEAD_DIM, RET_HEAD_DIM), 0.5),
        "norm_mix": 1.0 + nrm(ks[4], (DEPTH, D_MODEL), 0.02),
        "w_in": nrm(ks[5], (DEPTH, D_MODEL, IN_WIDTH), D_MODEL ** -0.5),
        "w_pool": nrm(ks[6], (DEPTH, POOL_GROUPS, POOL_GROUP_DIM, POOL_GROUP_DIM), POOL_GROUP_DIM ** -0.5),
        "pool_scale": 1.0 + nrm(ks[7], (DEPTH, POOL_WIDTH), 0.1),
        "ret_gn": 1.0 + nrm(ks[8], (DEPTH, RET_WIDTH), 0.02),
        "w_out": nrm(ks[9], (DEPTH, D_MODEL, D_MODEL), D_MODEL ** -0.5),
        "norm_ffn": 1.0 + nrm(ks[10], (DEPTH, D_MODEL), 0.02),
        "w_router_group": nrm(ks[11], (DEPTH, D_MODEL, N_EXPERT_GROUPS), D_MODEL ** -0.5),
        "b_router_group": nrm(ks[12], (DEPTH, N_EXPERT_GROUPS), 0.01),
        "w_router_expert": nrm(ks[13], (DEPTH, D_MODEL, N_EXPERTS), D_MODEL ** -0.5),
        "b_router_expert": nrm(ks[14], (DEPTH, N_EXPERTS), 0.01),
        "w_gate": nrm(ks[15], (DEPTH, N_EXPERTS, D_MODEL, D_EXPERT), D_MODEL ** -0.5),
        "w_up": nrm(ks[16], (DEPTH, N_EXPERTS, D_MODEL, D_EXPERT), D_MODEL ** -0.5),
        "w_down": nrm(ks[17], (DEPTH, N_EXPERTS, D_EXPERT, D_MODEL), D_EXPERT ** -0.5),
        "norm_final": 1.0 + nrm(ks[18], (D_MODEL,), 0.02),
    }

def reference(x_prompt, x_sample, cache_pool, state_ret, norm_mix, w_in, w_pool, pool_scale,
              ret_gn, w_out, norm_ffn, w_router_group, b_router_group, w_router_expert,
              b_router_expert, w_gate, w_up, w_down, norm_final):
    yp, ys = x_prompt, x_sample
    Bp, Lp, _ = x_prompt.shape
    Ls = x_sample.shape[1]
    pos_p = jnp.arange(Lp)
    pos_s = PAST_LEN + jnp.arange(Ls)
    n_prev_s = min(POOL_BUF, PAST_LEN)
    pool_p, ret_p, pool_s, ret_s = [], [], [], []
    for l in range(DEPTH):
        zero_buf = jnp.zeros((Bp, POOL_BUF, POOL_WIDTH), x_prompt.dtype)
        zero_state = jnp.zeros((Bp, RET_HEADS, RET_HEAD_DIM, RET_HEAD_DIM), x_prompt.dtype)
        mix_w = (norm_mix[l], w_in[l], w_pool[l], pool_scale[l], ret_gn[l], w_out[l])
        yp, bp, sp = mixer_block(yp, zero_buf, 0, zero_state, pos_p, *mix_w)
        ys, bs, ss = mixer_block(ys, cache_pool[l], n_prev_s, state_ret[l], pos_s, *mix_w)
        moe_w = (norm_ffn[l], w_router_group[l], b_router_group[l], w_router_expert[l],
                 b_router_expert[l], w_gate[l], w_up[l], w_down[l])
        yp = hier_moe(yp, *moe_w)
        ys = hier_moe(ys, *moe_w)
        pool_p.append(bp); ret_p.append(sp); pool_s.append(bs); ret_s.append(ss)
    y_prompt = rmsnorm(yp, norm_final)
    y_sample = rmsnorm(ys, norm_final)
    return (y_prompt, y_sample, jnp.stack(pool_p), jnp.stack(ret_p), jnp.stack(pool_s), jnp.stack(ret_s))


_drawn_inputs = setup_inputs


def setup_inputs(seed=0):
    import zlib

    import numpy as np

    out = dict(_drawn_inputs(seed))
    spreads = {}
    factors = {'ret_gn': 3.214, 'b_router_group': 2.782, 'b_router_expert': 11.819, 'norm_final': 8.385}
    for name, (base, spread) in spreads.items():
        noise = np.random.default_rng([zlib.crc32(name.encode()), seed]).standard_normal(out[name].shape)
        drawn = base * np.exp(spread * noise) if base else spread * noise
        out[name] = __import__('jax').numpy.asarray(drawn.astype(out[name].dtype))
    for name, factor in factors.items():
        out[name] = (out[name] * factor).astype(out[name].dtype)
    return out
```

```python
from contextlib import ExitStack

import numpy as np

import concourse.bass as bass
from concourse import mybir

ALU = mybir.AluOpType
ACT = mybir.ActivationFunctionType
AX = mybir.AxisListType
F32 = mybir.dt.float32
F32R = mybir.dt.float32r
BF16 = mybir.dt.bfloat16
I32 = mybir.dt.int32
U32 = mybir.dt.uint32

P = 128
D = 1024
SEQ, DECB, DECS, PAST = 512, 8, 8, 4096
NL = 2
KC = D // P
NT = 5
LAST = NT - 1
NSAMP = DECB * DECS
TOK = NT * P
PW = 512
NH = 4
HALF = 64
BUF = 15
IN_W = 5 * PW
NE, NG, EPG = 16, 4, 4
F = 256
UW = 16 + SEQ + DECB * 24
WIN_STEPS, WOUT_STEPS = 5 * KC, 2 * KC
W_STEPS = WIN_STEPS + WOUT_STEPS
RAW, SPL = 3, 4
LOOP0, LOOP1 = 1, 13
EPS_RMS, EPS_GN = 1e-6, 1e-5
OUT_OF_RANGE = 1000000.0


def constant_tables():
    f = np.float32
    p = np.arange(P)
    pos = np.zeros((P, NT), f)
    for t in range(LAST):
        pos[:, t] = t * P + p
    pos[:, LAST] = PAST + p % DECS
    inv = f(10000.0) ** (-(np.arange(HALF, dtype=f)) / f(HALF))
    ang = (pos[:, :, None] * inv.astype(f)[None, None, :]).astype(f)
    log_g = np.log(f(1.0) - f(2.0) ** (-5.0 - np.arange(NH, dtype=f))).astype(f)
    scale = f(P) ** f(-0.5)

    def decay(chunk):
        i, j = p[None, :], p[:, None]
        same = (i // chunk == j // chunk) & (i >= j)
        e = np.exp(np.maximum(i - j, 0).astype(f)[:, None, :] * log_g[None, :, None])
        return np.where(same[:, None, :], e, 0).astype(f) * scale

    def qdecay(chunk):
        row = np.exp(((p % chunk) + 1.0).astype(f)[None, :] * log_g[:, None])
        return np.broadcast_to(row[None], (P, NH, P))

    def kdecay(chunk):
        return np.exp((chunk - 1.0 - (p % chunk)).astype(f)[:, None] * log_g[None]) * scale

    invc = np.zeros((NH, 16), f)
    for g, w in enumerate((2, 4, 8, 16)):
        invc[g] = 1.0 / np.minimum(w, np.arange(16) + 1)
    seq_mask = (p[:, None] // DECS == np.arange(DECB)[None]) & (p[:, None] < NSAMP)
    valid = np.ones((P, NT), f)
    valid[NSAMP:, LAST] = 0
    parts = {
        "cos": np.cos(ang), "sin": np.sin(ang), "nsin": -np.sin(ang),
        "decay": np.stack([decay(P), decay(DECS)], 1),
        "qdec": np.stack([qdecay(P), qdecay(DECS)], 1),
        "kdec": np.stack([kdecay(P), kdecay(DECS)], 1),
        "seqm": seq_mask, "inv": np.broadcast_to(invc[None], (P, NH, 16)),
        "ident": np.eye(P),
        "rank4": np.broadcast_to(np.array([4, 3, 2, 1], f), (P, NT, 4)),
        "iota": np.broadcast_to(np.arange(NE, dtype=f), (P, NT, NE)),
        "valid": valid, "drop": (1 - valid) * OUT_OF_RANGE,
    }
    at, cols, n = {}, [], 0
    for k, a in parts.items():
        a = np.asarray(a, f).reshape(P, -1)
        at[k] = (n, n + a.shape[1])
        n += a.shape[1]
        cols.append(a)
    tri = np.concatenate([(p[:, None] < p[None, :]), np.ones((P, P))], 1)
    pair = (np.arange(2)[None, :, None] * TOK + np.arange(NT)[None, None, :] * P + p[:, None, None])
    ints = np.concatenate([pair.reshape(P, 2 * NT), np.full((P, NT * NE), 4096)], 1)
    chunk = np.exp(f(P) * log_g), np.exp(f(DECS) * log_g)
    return at, np.concatenate(cols, 1).astype(f), tri.astype(f), ints.astype(np.uint32), chunk


def build(nc, a, o):
    at, _, _, _, chunk_decay = constant_tables()
    ncst = max(v[1] for v in at.values())
    ctx = ExitStack()
    with ctx:
        top = [((nc.sbuf_base + 63) // 64) * 64]

        def place(nbytes):
            off = top[0]
            top[0] += (nbytes + 31) // 32 * 32
            assert top[0] <= nc.SBUF_PARTITION_SIZE_BYTES, top[0]
            return off

        def tile(name, shape, dt=F32, off=None):
            size = int(np.prod(shape[1:])) * (2 if dt == BF16 else 4)
            return nc.alloc_sbuf_tensor_at(name, shape, dt, offset=place(size) if off is None else off)

        cst = tile("cst", [P, ncst])
        tri = tile("tri", [P, 2 * P], BF16)
        ints = tile("ints", [P, 2 * NT + NT * NE], U32)
        x = tile("x", [P, NT, D])
        gain = tile("gain", [P, D])
        wpool = tile("wpool", [P, NH, P])
        pscale = tile("pscale", [P, NH])
        gnrow = tile("gnrow", [P, PW])
        cpn = tile("cpn", [DECB * BUF, PW])
        wr = tile("wr", [P, KC, 20])
        wrh = tile("wrh", [P, KC, 20], F32R)
        wrl = tile("wrl", [P, KC, 20], F32R)
        rbias = tile("rbias", [P, 20])
        wh = [tile(f"wh{i}", [P, PW], F32R) for i in range(SPL)]
        wl = [tile(f"wl{i}", [P, PW], F32R) for i in range(SPL)]
        e0 = place(24 * 1024)
        shared = place(48 * 1024)
        slot_at = [e0, shared, shared + 24 * 1024]
        wgu = [tile(f"wgu{s}", [P, KC, 2 * F], off=slot_at[s]) for s in range(3)]
        wdn = [tile(f"wdn{s}", [P, 2, D], off=slot_at[s] + 16 * 1024) for s in range(3)]
        z = tile("z", [P, NT, 4, PW], off=shared)
        raw = [tile(f"raw{i}", [P, PW], off=shared + 40 * 1024 + 2048 * i) for i in range(RAW)]
        region = place(40 * 1024)
        hT = tile("hT", [P, KC, TOK], F32R, off=region)
        lT = tile("lT", [P, KC, TOK], F32R, off=region + 20 * 1024)
        hg = [tile(f"hg{i}", [P, D], off=region + 4096 * i) for i in range(3)]
        y = [tile(f"y{i}", [P, D], off=region + 4096 * (3 + i)) for i in range(3)]
        hgT = [tile(f"hgT{i}", [P, KC, P], off=region + 4096 * (6 + i)) for i in range(3)]
        act = tile("act", [P, F], off=region + 4096 * 9)
        actT = tile("actT", [P, 2, P], off=region + 4096 * 9 + 1024)
        pidx = tile("pidx", [P, NT * NE], U32, off=region + 4096 * 9 + 2048)
        tidx = tile("tidx", [P, NT * NE], U32, off=region + 4096 * 9 + 2048 + 320)
        tmpf = tile("tmpf", [P, NT * NE], off=region + 4096 * 9 + 2048 + 640)
        r12 = place(12 * 1024)
        xn = [tile(f"xn{i}", [P, D], off=r12 + 4096 * i) for i in range(2)]
        unat = tile("unat", [P, NT, PW], off=r12)
        qT = tile("qT", [P, NH, P], off=r12)
        kT = tile("kT", [P, NH, P], off=r12 + 2048)
        qdT = tile("qdT", [P, NH, P], off=r12 + 2048 * 2)
        scT = tile("scT", [P, NH, P], off=r12 + 2048 * 3)
        kd = tile("kd", [P, NH, P], off=r12 + 2048 * 4)
        on = tile("on", [P, NH, P], off=r12 + 2048 * 5)
        rt = [r12 + 8192]

        def route(name, shape, dt=F32):
            off = rt[0]
            rt[0] += (int(np.prod(shape[1:])) * (2 if dt == BF16 else 4) + 31) // 32 * 32
            assert rt[0] <= r12 + 12 * 1024
            return tile(name, shape, dt, off)

        lg = route("lg", [P, NT, 20])
        gd = route("gd", [P, NT, 4])
        gex = route("gex", [P, NT, 4])
        key = route("key", [P, NT, 4])
        ohg = route("ohg", [P, NT, 4])
        prod = route("prod", [P, NT, NG, EPG])
        ing = route("ing", [P, NT, EPG])
        oh = [route(f"oh{k}", [P, NT, EPG]) for k in range(2)]
        both = [route(f"both{k}", [P, NT, NE]) for k in range(2)]
        taken = route("taken", [P, NT, NE], BF16)
        where = route("where", [P, NT * NE])
        picked = route("picked", [P, NT, NE])
        small = route("small", [P, 16, NT])
        pgate = tile("pgate", [P, 2, NT])
        slot_u = tile("slot_u", [P, 2, NT], U32)
        gidx = tile("gidx", [P, 1], U32)
        sidx = tile("sidx", [P, 1], U32)
        most_f = tile("most_f", [P, 1])
        most = tile("most", [P, 1], I32)
        ss = tile("ss", [P, NT])
        rms = tile("rms", [P, NT])
        rstd = tile("rstd", [P, NT])
        bnst = tile("bnst", [P, NH, 6])
        mv = tile("mv", [P, NH, 2])
        gnrt = tile("gnrt", [P, NH])
        gnrs = tile("gnrs", [P, NH])
        eps = tile("eps", [P, 2])
        s0 = [tile(f"s0{i}", [P, DECB, P]) for i in range(2)]
        st = tile("st", [P, NH, P])
        uT = tile("uT", [P, UW])
        dT = tile("dT", [P, TOK])
        edge = tile("edge", [P, 16])
        wa = place(2 * UW * 4)
        winA = tile("winA", [P, UW], off=wa)
        winB = tile("winB", [P, UW], off=wa + UW * 4)
        ropA = tile("ropA", [P, NH, 2, HALF], off=wa)
        ropB = tile("ropB", [P, NH, 2, HALF], off=wa + 2048)
        vb = tile("vb", [P, DECB, P], off=wa)

        ps = [ctx.enter_context(nc.psum_tensor(f"ps{i}", [P, 512], F32)) for i in range(8)]
        xn_d = nc.dram_tensor("xn_d", (TOK, D), F32).ap()
        y_d = nc.dram_tensor("y_d", (2 * TOK, D), F32).ap()
        tab_d = nc.dram_tensor("tab_d", (TOK * NE, 1), U32).ap()

        def sem(name):
            return ctx.enter_context(nc.semaphore(name))

        cst_ld = sem("cst_ld"); x_ld = [sem(f"x_ld{t}") for t in range(NT)]; gain_ld = sem("gain_ld")
        small_ld = sem("small_ld"); raw_ld = [sem(f"raw_ld{i}") for i in range(RAW)]
        s0_ld = [sem(f"s0_ld{i}") for i in range(2)]; gu_ld = [sem(f"gu_ld{i}") for i in range(3)]
        dn_ld = [sem(f"dn_ld{i}") for i in range(3)]; gat = [sem(f"gat{i}") for i in range(3)]
        comb_ld = [sem(f"comb_ld{i}") for i in range(6)]
        tab_init = sem("tab_init"); slot_sc = sem("slot_sc"); idx_ld = sem("idx_ld")
        xn_st = [sem(f"xn_st{i}") for i in range(2)]; upool_st = sem("upool_st"); st_st = sem("st_st")
        s0_st = [sem(f"s0_st{i}") for i in range(2)]; y_sc = [sem(f"y_sc{i}") for i in range(3)]
        out_st = sem("out_st")
        ready0 = sem("ready0"); sq_done = sem("sq_done"); rms_done = sem("rms_done"); xn_done = sem("xn_done")
        tr_done = sem("tr_done"); hi_done = sem("hi_done"); lo_done = sem("lo_done")
        whi = sem("whi"); wlo = sem("wlo"); wpe = sem("wpe"); zmm = sem("zmm")
        zfree = [sem(f"zfree{i}") for i in range(8)]
        xmm = sem("xmm"); xw = sem("xw"); sg_done = sem("sg_done")
        ut_done = sem("ut_done"); uT_done = sem("uT_done"); win_done = sem("win_done"); d_done = sem("d_done")
        yp_done = sem("yp_done"); phi = sem("phi"); plo = sem("plo")
        rope = sem("rope"); kd_done = sem("kd_done"); qk_tr = sem("qk_tr"); qk_ev = sem("qk_ev"); qd_done = sem("qd_done")
        sc_mm = sem("sc_mm"); sc_ev = sem("sc_ev"); o_mm = sem("o_mm"); kv_mm = sem("kv_mm"); s_upd = sem("s_upd")
        st_ready = sem("st_ready"); o_ev = sem("o_ev"); o_back = sem("o_back"); gn_st = sem("gn_st"); gn_rt = sem("gn_rt")
        gn_free = sem("gn_free"); on_done = sem("on_done"); on_tr = sem("on_tr"); ohi = sem("ohi"); olo = sem("olo")
        vb_done = sem("vb_done"); skv_mm = sem("skv_mm"); s_new = sem("s_new")
        wr_hi = sem("wr_hi"); wr_lo = sem("wr_lo"); lg_mm = sem("lg_mm"); gdone = sem("gdone"); gexp = sem("gexp")
        dv_done = sem("dv_done"); dvexp = sem("dvexp"); taken_done = sem("taken_done"); pos_mm = sem("pos_mm")
        slots_done = sem("slots_done"); tidx_done = sem("tidx_done"); hg_clear = sem("hg_clear"); most_done = sem("most_done")
        gu_mm = sem("gu_mm"); t_mm = sem("t_mm")
        hgA = sem("hgA"); hgV = sem("hgV"); silu_done = sem("silu_done"); act_done = sem("act_done")
        at_mm = sem("at_mm"); actT_done = sem("actT_done"); dn_mm = sem("dn_mm"); yA = sem("yA"); yV = sem("yV")
        comb = sem("comb")
        ov = [{k: sem(f"ov{L}_{k}") for k in ("ld", "g", "t", "h", "gu", "s", "a", "at", "aT", "d", "y", "sc")}
              for L in range(NL)]
        dve_chain = sem("dve_chain"); act_chain = sem("act_chain"); pool_chain = sem("pool_chain")

        def c(name, *shape):
            v = cst[:, at[name][0]:at[name][1]]
            if len(shape) == 1:
                return v.rearrange("p (a b) -> p a b", a=shape[0])
            if len(shape) == 2:
                return v.rearrange("p (a b c) -> p a b c", a=shape[0], b=shape[1])
            return v

        ident = c("ident")
        OFFS = {"q": 0, "k": 1, "v": 2, "g": 3}

        def zq(t, name):
            return z[:, t, OFFS[name], :]

        def heads(ap):
            return ap.rearrange("p (h d) -> p h d", h=NH)

        def over(ap, n, dim=1):
            v = ap.unsqueeze(dim)
            shape = list(v.shape)
            shape[dim] = n
            return v.to_broadcast(shape)

        ZUSES = [len(range(b, 25, 8)) for b in range(8)]
        EUSES = [len(range(s, NE, 3)) for s in range(3)]

        def z_there(eng, L, g, t):
            m = 5 * g + t
            eng.wait_ge(zfree[m % 8], L * ZUSES[m % 8] + m // 8 + 1)

        def slot_count(L, s, e):
            if isinstance(e, int):
                return L * EUSES[s] + e // 3 + 1
            raise AssertionError

        def step_done(eng, S):
            L, s = divmod(S, W_STEPS)
            g, k = divmod(s, KC)
            if k < KC - 1:
                eng.wait_ge(wpe, (W_STEPS * L // KC + g) * (KC - 1) + k + 1)
            elif g < 5:
                eng.wait_ge(zmm, 5 * NT * L + NT * (g + 1))
            else:
                eng.wait_ge(xmm, 2 * NT * L + NT * (g - 4))

        block = ctx.enter_context(nc.Block())

        @block.sync
        def _(sp):
            sp.dma_start(cst[:, :], a["cst"]).then_inc(cst_ld, 16)
            sp.dma_start(ints[:, :], a["ints"]).then_inc(cst_ld, 16)
            sp.dma_start(tri[:, :], a["tri"]).then_inc(cst_ld, 16)
            for t in range(LAST):
                sp.dma_start(x[:, t, :], a["x_prompt"][0, t * P:(t + 1) * P, :]).then_inc(x_ld[t], 16)
            sp.dma_start(x[0:NSAMP, LAST, :], a["x_sample"].rearrange("b s d -> (b s) d")).then_inc(x_ld[LAST], 16)

            def load_gain(n):
                if n:
                    sp.wait_ge(xn_done, 5 * n)
                src = a["norm_final"] if n == 2 * NL else a[("norm_mix", "norm_ffn")[n % 2]][n // 2]
                sp.dma_start(gain[:, :], src.partition_broadcast(P)).then_inc(gain_ld, 16)

            def load_raw(L, s):
                S = W_STEPS * L + s
                if S >= RAW:
                    sp.wait_ge(wlo, S - RAW + 1)
                if s < RAW and L:
                    sp.wait_ge(dn_mm, NE * L - 1)
                if s < WIN_STEPS:
                    g, k = divmod(s, KC)
                    src = a["w_in"][L, k * P:(k + 1) * P, g * PW:(g + 1) * PW]
                else:
                    n, k = divmod(s - WIN_STEPS, KC)
                    src = a["w_out"][L, k * P:(k + 1) * P, n * PW:(n + 1) * PW]
                sp.dma_start(raw[S % RAW][:, :], src).then_inc(raw_ld[S % RAW], 16)

            def load_expert(L, e, s, d):
                if d or L:
                    sp.wait_ge(gu_mm, NE * L + e - 2 if d else NE * L)
                sp.dma_start(wgu[s][:, :, 0:F], a["w_gate"][L, e].rearrange("(k p) f -> p k f", p=P)).then_inc(gu_ld[s], 16)
                sp.dma_start(wgu[s][:, :, F:2 * F], a["w_up"][L, e].rearrange("(k p) f -> p k f", p=P)).then_inc(gu_ld[s], 16)
                if d or L:
                    sp.wait_ge(dn_mm, NE * L + e - 2 if d else NE * L)
                sp.dma_start(wdn[s][:, :, :], a["w_down"][L, e].rearrange("(k p) d -> p k d", p=P)).then_inc(dn_ld[s], 16)

            def overflow(L):
                v = ov[L]
                sp.wait_ge(most_done, L + 1)
                n = sp.value_load(most[0:1, 0:1], min_val=0, max_val=2 * TOK)
                with sp.If(n > P):
                    sp.wait_ge(dn_mm, NE * (L + 1))
                    sp.sem_inc(v["d"], 1)
                    with sp.Fori(1, NT) as turn:
                        with sp.Fori(0, NE) as e:
                            sp.wait_ge(v["d"], turn * NE + e - NE + 1)
                            sp.dma_start(wgu[0][:, :, 0:F], a["w_gate"][L, e].rearrange("(k p) f -> p k f", p=P)).then_inc(v["ld"], 16)
                            sp.dma_start(wgu[0][:, :, F:2 * F], a["w_up"][L, e].rearrange("(k p) f -> p k f", p=P)).then_inc(v["ld"], 16)
                            sp.dma_start(wdn[0][:, :, :], a["w_down"][L, e].rearrange("(k p) d -> p k d", p=P)).then_inc(v["ld"], 16)
                    sp.wait_ge(v["sc"], 16 * (NT - 1) * NE)
                with sp.Else():
                    sp.wait_ge(most_done, L + 1)

            load_gain(0)
            for L in range(NL):
                if L:
                    sp.wait_ge(comb, 2 * NT * (L - 1) + 1)
                sp.dma_start(wpool[:, :, :], a["w_pool"][L].rearrange("g c e -> c g e")).then_inc(small_ld, 16)
                sp.dma_start(pscale[:, :], a["pool_scale"][L].rearrange("(g e) -> e g", g=NH),
                             allow_slow_non_contiguous=True).then_inc(small_ld, 16)
                sp.dma_start(gnrow[:, :], a["ret_gn"][L].partition_broadcast(P)).then_inc(small_ld, 16)
                sp.dma_start(cpn[:, :], a["cache_pool"][L].rearrange("b r c -> (b r) c")).then_inc(small_ld, 16)
                sp.dma_start(wr[:, :, 0:4], a["w_router_group"][L].rearrange("(k p) n -> p k n", p=P)).then_inc(small_ld, 16)
                sp.dma_start(wr[:, :, 4:20], a["w_router_expert"][L].rearrange("(k p) n -> p k n", p=P)).then_inc(small_ld, 16)
                sp.dma_start(rbias[:, 0:4], a["b_router_group"][L].partition_broadcast(P)).then_inc(small_ld, 16)
                sp.dma_start(rbias[:, 4:20], a["b_router_expert"][L].partition_broadcast(P)).then_inc(small_ld, 16)
                sp.dma_start(o["new_pool_sample"][L, :, 0:BUF - DECS, :], a["cache_pool"][L, :, DECS:BUF, :]).then_inc(out_st, 16)
                for s in range(WIN_STEPS):
                    load_raw(L, s)
                    if s == 10:
                        load_gain(2 * L + 1)
                        load_expert(L, 0, 0, False)
                    if s == 20:
                        for t in (3, LAST):
                            z_there(sp, L, 0, t)
                        sp.dma_start(o["new_pool_prompt"][L, 0], unat[P - BUF:P, 3, :]).then_inc(upool_st, 16)
                        sp.dma_start(o["new_pool_sample"][L, :, BUF - DECS:BUF, :].rearrange("b s c -> b s c"),
                                     unat[0:NSAMP, LAST, :]).then_inc(upool_st, 16)
                for s in range(WIN_STEPS, W_STEPS):
                    load_raw(L, s)
                step_done(sp, W_STEPS * (L + 1) - 1)
                load_expert(L, 1, 1, False)
                load_expert(L, 2, 2, False)
                load_gain(2 * L + 2)
                load_expert(L, 3, 0, True)
                with sp.Fori(0, (NE - 4) // 3) as i:
                    for j in range(3):
                        load_expert(L, i * 3 + (4 + j), (1 + j) % 3, True)
                overflow(L)
                for s in range(3):
                    sp.wait_ge(y_sc[s], 16 * EUSES[s] * (L + 1))
                for i in range(2 * NT):
                    k, t = divmod(i, NT)
                    if i >= 6:
                        sp.wait_ge(comb, 2 * NT * L + i - 5)
                    n = P if t < LAST else NSAMP
                    sp.dma_start((hg + y)[i % 6][0:n, :], y_d[k * TOK + t * P:k * TOK + t * P + n, :]).then_inc(comb_ld[i % 6], 16)
            sp.wait_ge(out_st, 16 * NL)
            sp.wait_ge(upool_st, 32 * NL)
            sp.wait_ge(st_st, 16 * NL)
            for i in range(2):
                sp.wait_ge(s0_st[i], 32 * NL)

        @block.gpsimd
        def _(pool):
            chain = [0]

            def link(ins):
                chain[0] += 1
                ins.then_inc(pool_chain, 1)
                pool.wait_ge(pool_chain, chain[0])

            pool.memset(eps[:, 0:1], EPS_RMS).then_inc(ready0, 1)
            pool.memset(eps[:, 1:2], EPS_GN).then_inc(ready0, 1)
            pool.memset(uT[:, :], 0.0).then_inc(ready0, 1)
            pool.memset(dT[:, SEQ + NSAMP:TOK], 0.0).then_inc(ready0, 1)
            pool.wait_ge(cst_ld, 48)

            def gather(e):
                s = e % 3
                pool.indirect_dma_start(out=hg[s][:, :], out_offset=None, in_=xn_d,
                                        in_offset=bass.IndirectOffsetOnAxis(ap=tidx[:, e:e + 1], axis=0),
                                        bounds_check=TOK - 1, oob_is_err=False).then_inc(gat[s], 16)

            def scatter(L, e):
                s = e % 3
                pool.wait_ge(yA, NE * L + e + 1)
                pool.wait_ge(yV, NE * L + e + 1)
                pool.indirect_dma_start(out=y_d, out_offset=bass.IndirectOffsetOnAxis(ap=pidx[:, e:e + 1], axis=0),
                                        in_=y[s][:, :], in_offset=None,
                                        bounds_check=2 * TOK - 1, oob_is_err=False).then_inc(y_sc[s], 16)

            for L in range(NL):
                pool.dma_start(tab_d.rearrange("(j p e) o -> p j (e o)", j=NT, p=P),
                               ints[:, 2 * NT:].rearrange("p (j e) -> p j e", j=NT)).then_inc(tab_init, 16)
                for i in range(2):
                    if L:
                        pool.wait_ge(s0_st[i], 32 * L)
                    pool.dma_start(s0[i][:, :, :], a["state_ret"][L, :, i].rearrange("b d e -> d b e")).then_inc(s0_ld[i], 16)
                w = 0
                for g in range(NH):
                    pool.wait_ge(uT_done, 3 * (NH * L + g + 1))
                    if g or L:
                        pool.wait_ge(d_done, NH * L + g)
                    src = uT
                    for r in range(g + 1):
                        dst = (winA, winB)[r % 2]
                        n = 1 << r
                        lo = 2 * n - 1
                        pool.tensor_tensor(dst[:, lo:UW], src[:, lo:UW], src[:, lo - n:UW - n], ALU.add).then_inc(win_done, 1)
                        w += 1
                        pool.wait_ge(win_done, 10 * L + w)
                        src = dst
                pool.wait_ge(d_done, NH * (L + 1))
                for t in range(NT):
                    for qk in (0, 1):
                        z_there(pool, L, 1 + qk, t)
                        v = z[:, t, qk, :].rearrange("p (h s d) -> p h s d", h=NH, s=2)
                        cs, sn, ns = (c(n, NT)[:, t, :] for n in ("cos", "sin", "nsin"))
                        cosb = cs.unsqueeze(1).unsqueeze(1).to_broadcast([P, NH, 2, HALF])
                        pool.tensor_tensor(ropA[:, :, :, :], v, cosb, ALU.mult)
                        pool.tensor_tensor(ropB[:, :, 0, :], v[:, :, 1, :], over(ns, NH), ALU.mult)
                        link(pool.tensor_tensor(ropB[:, :, 1, :], v[:, :, 0, :], over(sn, NH), ALU.mult))
                        last = pool.tensor_tensor(v, ropA[:, :, :, :], ropB[:, :, :, :], ALU.add)
                        if qk == 0:
                            link(last)
                    last.then_inc(rope, 1)
                    pool.wait_ge(rope, NT * L + t + 1)
                for h in range(NH):
                    pool.wait_ge(s_new, NH * L + h + 1)
                    pool.dma_start(o["new_ret_sample"][L, :, h].rearrange("b d e -> d b e"), s0[h % 2][:, :, :]).then_inc(s0_st[h % 2], 16)
                    if h < 2:
                        pool.wait_ge(s0_st[h % 2], 32 * L + 16)
                        pool.dma_start(s0[h % 2][:, :, :], a["state_ret"][L, :, h + 2].rearrange("b d e -> d b e")).then_inc(s0_ld[h % 2], 16)
                pool.wait_ge(lg_mm, L + 1)
                for s in range(3):
                    pool.memset(hg[s][:, :], 0.0).then_inc(hg_clear, 1)
                pool.wait_ge(slots_done, L + 1)
                pool.wait_ge(tab_init, 16 * (L + 1))
                for i in range(2 * NT):
                    pool.indirect_dma_start(out=tab_d, out_offset=bass.IndirectOffsetOnAxis(ap=slot_u[:, i // NT, i % NT:i % NT + 1], axis=0),
                                            in_=ints[:, i:i + 1], in_offset=None,
                                            bounds_check=TOK * NE - 1, oob_is_err=False).then_inc(slot_sc, 16)
                pool.wait_ge(slot_sc, 16 * 2 * NT * (L + 1))
                pool.dma_start(pidx[:, :].rearrange("p (j e) -> p j e", j=NT),
                               tab_d.rearrange("(j p e) o -> p j (e o)", j=NT, p=P)).then_inc(idx_ld, 16)
                pool.wait_ge(tidx_done, L + 1)
                pool.wait_ge(hg_clear, 3 * (L + 1))
                for i in range(2):
                    n = (3, 2)[i]
                    pool.wait_ge(xn_st[i], 16 * n * (L + 1))
                for e in range(3):
                    gather(e)
                for e in range(NE):
                    scatter(L, e)
                    if e:
                        pool.wait_ge(y_sc[(e - 1) % 3], 16 * slot_count(L, (e - 1) % 3, e - 1))
                    if e + 3 < NE:
                        pool.wait_ge(t_mm, NE * L + e + 1)
                        gather(e + 3)
                v = ov[L]
                pool.wait_ge(most_done, L + 1)
                n = pool.value_load(most[0:1, 0:1], min_val=0, max_val=2 * TOK)
                with pool.If(n > P):
                    pool.wait_ge(t_mm, NE * (L + 1))
                    for s in range(3):
                        pool.wait_ge(y_sc[s], 16 * EUSES[s] * (L + 1))
                    with pool.Fori(1, NT) as turn:
                        with pool.Fori(0, NE) as e:
                            col = turn * NE + e
                            pool.tensor_copy(gidx[:, :], tidx[:, bass.ds(col, 1)])
                            pool.drain()
                            pool.indirect_dma_start(out=hg[0][:, :], out_offset=None, in_=xn_d,
                                                    in_offset=bass.IndirectOffsetOnAxis(ap=gidx[:, 0:1], axis=0),
                                                    bounds_check=TOK - 1, oob_is_err=False).then_inc(v["g"], 16)
                            pool.wait_ge(v["y"], col - NE + 1)
                            pool.tensor_copy(sidx[:, :], pidx[:, bass.ds(col, 1)])
                            pool.drain()
                            pool.indirect_dma_start(out=y_d, out_offset=bass.IndirectOffsetOnAxis(ap=sidx[:, 0:1], axis=0),
                                                    in_=y[0][:, :], in_offset=None,
                                                    bounds_check=2 * TOK - 1, oob_is_err=False).then_inc(v["sc"], 16)
                            pool.wait_ge(v["sc"], 16 * (col - NE + 1))
                with pool.Else():
                    pool.wait_ge(t_mm, NE * (L + 1))
                pool.wait_ge(t_mm, NE * (L + 1))

        def o_hi(eng, L, t):
            eng.wait_ge(on_tr, NT * L + t + 1)
            eng.activation(hT[:, NH:KC, t * P:(t + 1) * P], heads(ps[7][:, :]), ACT.Copy).then_inc(ohi, 1)

        @block.scalar
        def _(sc):
            chain = [0]

            def norm_squares(n):
                for t in range(NT):
                    if n == 0:
                        sc.wait_ge(x_ld[t], 16)
                        sc.wait_ge(ready0, 5)
                    elif n % 2:
                        sc.wait_ge(xw, 10 * (n // 2) + NT + t + 1)
                    else:
                        sc.wait_ge(comb, 10 * (n // 2 - 1) + NT + t + 1)
                    if n >= 2 and t < 2 and n % 2 == 0:
                        sc.wait_ge(xn_st[t], 16 * (3, 2)[t] * (n // 2))
                    if t >= 2:
                        sc.wait_ge(sq_done, NT * n + t - 1)
                    sc.activation(xn[t % 2][:, :], x[:, t, :], ACT.Square, accum_out=ss[:, t:t + 1]).then_inc(sq_done, 1)
                sc.wait_ge(sq_done, NT * (n + 1))
                sc.activation(rms[:, :], ss[:, :], ACT.Sqrt, bias=eps[:, 0:1], scale=1.0 / D).then_inc(rms_done, 1)

            def norm_hi(n):
                for t in range(NT):
                    if n % 2:
                        sc.wait_ge(xn_done, NT * n + t + 1)
                        sc.dma_start(xn_d[t * P:(t + 1) * P, :], xn[t % 2][:, :]).then_inc(xn_st[t % 2], 16)
                    for half in range(2):
                        i = 2 * t + half
                        sc.wait_ge(tr_done, 10 * n + i + 1)
                        sc.activation(hT[:, 4 * half:4 * half + 4, t * P:(t + 1) * P], ps[i % 4][:, :].rearrange("p (k c) -> p k c", k=4),
                                      ACT.Copy).then_inc(hi_done, 1)

            def w_hi(L, s):
                S = W_STEPS * L + s
                sc.wait_ge(raw_ld[S % RAW], 16 * (S // RAW + 1))
                if S >= SPL:
                    step_done(sc, S - SPL)
                sc.activation(wh[S % SPL][:, :], raw[S % RAW][:, :], ACT.Copy).then_inc(whi, 1)

            def z_evac(L, g, tiles):
                for t in tiles:
                    m = 5 * g + t
                    sc.wait_ge(zmm, 25 * L + m + 1)
                    dst = unat[:, t, :] if g == 0 else z[:, t, g - 1, :]
                    sc.activation(dst, ps[m % 8][:, :], ACT.Silu if g == 4 else ACT.Copy).then_inc(zfree[m % 8], 1)

            def expert(L, e, s, nxt, prev):
                X = NE * L + e
                sc.wait_ge(gu_mm, X + 1)
                if not (isinstance(X, int) and X == 0):
                    sc.wait_ge(at_mm, X)
                sc.activation(act[:, :], ps[0][:, 0:F], ACT.Silu).then_inc(silu_done, 1)
                if nxt:
                    sc.wait_ge(t_mm, X + 2)
                    sc.activation(hgT[(s + 1) % 3][:, 0:4, :], ps[1][:, :].rearrange("p (k c) -> p k c", k=4), ACT.Copy).then_inc(hgA, 1)
                if prev:
                    y_evac(L, e - 1, (s + 2) % 3)
                sc.wait_ge(at_mm, X + 1)
                sc.activation(actT[:, :, :], ps[5][:, 0:F].rearrange("p (k c) -> p k c", k=2), ACT.Copy).then_inc(actT_done, 1)

            def y_evac(L, e, s):
                sc.wait_ge(dn_mm, NE * L + e + 1)
                if isinstance(e, int) and e == NE - 1:
                    sc.wait_ge(y_sc[s], 16 * (slot_count(L, s, e) - 1))
                sc.activation(y[s][:, 0:512], ps[3][:, :], ACT.Copy).then_inc(yA, 1)

            for L in range(NL):
                norm_squares(2 * L)
                norm_hi(2 * L)
                for s in range(WIN_STEPS):
                    w_hi(L, s)
                    if s % KC == 3 and s > KC:
                        z_evac(L, s // KC - 1, (0, 2, 4))
                z_evac(L, 4, range(NT))
                for s in range(WIN_STEPS, WIN_STEPS + SPL):
                    w_hi(L, s)
                sc.wait_ge(small_ld, 128 * (L + 1))
                for g in range(NH):
                    if g or L:
                        sc.wait_ge(d_done, NH * L + g)
                    if g == 0 and L == 0:
                        sc.wait_ge(ready0, 5)
                    sc.wait_ge(ut_done, NH * L + g + 1)
                    A, B = ps[2 * (g % 2)], ps[2 * (g % 2) + 1]
                    samp = uT[:, 16 + SEQ:].rearrange("p (b w) -> p b w", b=DECB)
                    sc.activation(uT[:, 16:16 + SEQ], A[:, :], ACT.Copy).then_inc(uT_done, 1)
                    sc.activation(samp[:, :, 16:24], B[:, 0:NSAMP].rearrange("p (b s) -> p b s", b=DECB), ACT.Copy).then_inc(uT_done, 1)
                    sc.activation(samp[:, :, 1:16], B[:, P:P + DECB * BUF].rearrange("p (b s) -> p b s", b=DECB), ACT.Copy).then_inc(uT_done, 1)
                    sc.wait_ge(yp_done, NH * L + g + 1)
                    sc.activation(hT[:, g, 0:SEQ], ps[4][:, :], ACT.Copy, scale=pscale[:, g:g + 1]).then_inc(phi, 1)
                    sc.activation(hT[:, g, SEQ:TOK], ps[5][:, 0:P], ACT.Copy, scale=pscale[:, g:g + 1]).then_inc(phi, 1)
                sc.wait_ge(upool_st, 32 * (L + 1))
                for t in range(NT):
                    sc.wait_ge(qk_tr, NT * L + t + 1)
                    sc.activation(qT[:, :, :], heads(ps[0][:, :]), ACT.Copy).then_inc(qk_ev, 1)
                    sc.activation(kT[:, :, :], heads(ps[1][:, :]), ACT.Copy).then_inc(qk_ev, 1)
                    if t:
                        o_hi(sc, L, t - 1)
                    if t == LAST:
                        sc.wait_ge(st_ready, LAST * (L + 1))
                        sc.dma_start(o["new_ret_prompt"][L, 0].rearrange("h d e -> d h e"), st[:, :, :]).then_inc(st_st, 16)
                        sc.wait_ge(o_mm, NT * L + NT)
                        sc.activation(scT[:, :, :], heads(ps[6][:, :]), ACT.Copy).then_inc(o_ev, 1)
                    sc.wait_ge(gn_st, NT * L + t + 1)
                    sc.activation(gnrt[:, :], mv[:, :, 1], ACT.Sqrt, bias=eps[:, 1:2], scale=1.0).then_inc(gn_rt, 1)
                o_hi(sc, L, LAST)
                for s in range(WIN_STEPS + SPL, W_STEPS):
                    w_hi(L, s)
                norm_squares(2 * L + 1)
                norm_hi(2 * L + 1)
                sc.wait_ge(gdone, L + 1)
                sc.activation(gex[:, :, :], gd[:, :, :], ACT.Exp).then_inc(gexp, 1)
                sc.wait_ge(dv_done, L + 1)
                sc.activation(small[:, 5, :], small[:, 4, :], ACT.Exp).then_inc(dvexp, 1)
                sc.wait_ge(t_mm, NE * L + 1)
                sc.activation(hgT[0][:, 0:4, :], ps[1][:, :].rearrange("p (k c) -> p k c", k=4), ACT.Copy).then_inc(hgA, 1)
                expert(L, 0, 0, True, False)
                with sc.Fori(0, (LOOP1 - LOOP0) // 3) as i:
                    for j in range(3):
                        expert(L, i * 3 + (1 + j), (1 + j) % 3, True, True)
                for e in range(LOOP1, NE):
                    expert(L, e, e % 3, e < NE - 1, True)
                y_evac(L, NE - 1, (NE - 1) % 3)
                v = ov[L]
                sc.wait_ge(most_done, L + 1)
                n = sc.value_load(most[0:1, 0:1], min_val=0, max_val=2 * TOK)
                with sc.If(n > P):
                    with sc.Fori(1, (NT - 1) * NE + 1) as i:
                        sc.wait_ge(v["t"], i)
                        for half in range(2):
                            sc.activation(hgT[0][:, 4 * half:4 * half + 4, :], ps[1 + half][:, :].rearrange("p (k c) -> p k c", k=4), ACT.Copy).then_inc(v["h"], 1)
                        sc.wait_ge(v["gu"], i)
                        sc.activation(act[:, :], ps[0][:, 0:F], ACT.Silu).then_inc(v["s"], 1)
                        sc.wait_ge(v["at"], i)
                        sc.activation(actT[:, :, :], ps[5][:, 0:F].rearrange("p (k c) -> p k c", k=2), ACT.Copy).then_inc(v["aT"], 1)
                        sc.wait_ge(v["d"], i + 1)
                        sc.activation(y[0][:, 0:512], ps[3][:, :], ACT.Copy)
                        sc.activation(y[0][:, 512:D], ps[4][:, :], ACT.Copy).then_inc(v["y"], 1)
                with sc.Else():
                    sc.wait_ge(dn_mm, NE * (L + 1))
                sc.wait_ge(dn_mm, NE * (L + 1))
            norm_squares(2 * NL)
            for t in range(NT):
                sc.wait_ge(xn_done, NT * 2 * NL + t + 1)
                if t < LAST:
                    sc.dma_start(o["y_prompt"][0, t * P:(t + 1) * P, :], xn[t % 2][:, :]).then_inc(xn_st[t % 2], 16)
                else:
                    sc.dma_start(o["y_sample"].rearrange("b s d -> (b s) d"), xn[t % 2][0:NSAMP, :]).then_inc(xn_st[t % 2], 16)
            for i in range(2):
                sc.wait_ge(xn_st[i], 16 * (3, 2)[i] * (NL + 1))

        def pool_mix(pe, L, g):
            pe.wait_ge(d_done, NH * L + g + 1)
            if g:
                pe.wait_ge(plo, 8 * L + 2 * g)
            pe.matmul(ps[4][:, :], wpool[:, g, :], dT[:, 0:SEQ], start=True, stop=True)
            pe.matmul(ps[5][:, 0:P], wpool[:, g, :], dT[:, SEQ:TOK], start=True, stop=True).then_inc(yp_done, 1)

        def on_t(pe, L, t):
            pe.wait_ge(on_done, NT * L + t + 1)
            if t:
                pe.wait_ge(olo, NT * L + t)
            for h in range(NH):
                last = pe.transpose(ps[7][:, h * P:(h + 1) * P], on[:, h, :], ident)
            last.then_inc(on_tr, 1)

        @block.tensor
        def _(pe):
            def transposes(n):
                pe.wait_ge(cst_ld, 48)
                for t in range(NT):
                    pe.wait_ge(xn_done, NT * n + t + 1)
                    for half in range(2):
                        i = 2 * t + half
                        if i >= 4:
                            pe.wait_ge(lo_done, 10 * n + i - 3)
                        for k in range(4):
                            last = pe.transpose(ps[i % 4][:, k * P:(k + 1) * P], xn[t % 2][:, (4 * half + k) * P:(4 * half + k + 1) * P], ident)
                        last.then_inc(tr_done, 1)

            def three(out, hi_l, lo_l, hi_r, lo_r, first, final):
                pe.matmul(out, hi_l, hi_r, start=first, stop=False)
                pe.matmul(out, hi_l, lo_r, start=False, stop=False)
                return pe.matmul(out, lo_l, hi_r, start=False, stop=final)

            def gu(s):
                for k in range(KC):
                    last = pe.matmul(ps[0][:, :], hgT[s][:, k, :], wgu[s][:, k, :], start=(k == 0), stop=(k == KC - 1))
                return last

            def rows_t(s):
                for k in range(KC):
                    last = pe.transpose(ps[1 + k // 4][:, (k % 4) * P:(k % 4 + 1) * P], hg[s][:, k * P:(k + 1) * P], ident)
                return last

            def down(s):
                for n in range(2):
                    for k in range(2):
                        last = pe.matmul(ps[3 + n][:, :], actT[:, k, :], wdn[s][:, k, n * 512:(n + 1) * 512], start=(k == 0), stop=(k == 1))
                return last

            def act_t():
                for k in range(2):
                    last = pe.transpose(ps[5][:, k * P:(k + 1) * P], act[:, k * P:(k + 1) * P], ident)
                return last

            def expert(L, e, s, waits, nxt, prev):
                X = NE * L + e
                gu_at, dn_at, gat_at = waits
                pe.wait_ge(hgA, X + 1)
                pe.wait_ge(hgV, X + 1)
                pe.wait_ge(gu_ld[s], gu_at)
                if prev:
                    pe.wait_ge(act_done, X)
                gu(s).then_inc(gu_mm, 1)
                if nxt:
                    pe.wait_ge(gat[(s + 1) % 3], gat_at)
                    rows_t((s + 1) % 3).then_inc(t_mm, 1)
                if prev:
                    run_down(L, e - 1, (s + 2) % 3, dn_at)
                pe.wait_ge(act_done, X + 1)
                act_t().then_inc(at_mm, 1)

            def run_down(L, e, s, dn_at, first=False):
                X = NE * L + e
                pe.wait_ge(actT_done, X + 1)
                pe.wait_ge(dn_ld[s], dn_at)
                if not (isinstance(e, int) and e == 0):
                    pe.wait_ge(yA, X)
                    pe.wait_ge(yV, X)
                down(s).then_inc(dn_mm, 1)

            for L in range(NL):
                transposes(2 * L)
                pe.wait_ge(lo_done, 10 * (2 * L + 1))
                for s in range(WIN_STEPS):
                    g, k = divmod(s, KC)
                    S = W_STEPS * L + s
                    pe.wait_ge(wlo, S + 1)
                    for t in range(NT):
                        m = 5 * g + t
                        if k == 0 and m >= 8:
                            z_there(pe, L, (m - 8) // 5, (m - 8) % 5)
                        last = three(ps[m % 8][:, :], hT[:, k, t * P:(t + 1) * P], lT[:, k, t * P:(t + 1) * P],
                                     wh[S % SPL][:, :], wl[S % SPL][:, :], k == 0, k == KC - 1)
                        if k == KC - 1:
                            last.then_inc(zmm, 1)
                    if k < KC - 1:
                        last.then_inc(wpe, 1)
                for g in range(4):
                    for t in range(NT):
                        z_there(pe, L, g + 1, t)
                for t in range(NT):
                    z_there(pe, L, 0, t)
                pe.wait_ge(small_ld, 128 * (L + 1))
                for g in range(NH):
                    A, B = ps[2 * (g % 2)], ps[2 * (g % 2) + 1]
                    if g >= 2:
                        pe.wait_ge(uT_done, 3 * (NH * L + g - 1))
                    for t in range(LAST):
                        pe.transpose(A[:, t * P:(t + 1) * P], unat[:, t, g * P:(g + 1) * P], ident)
                    pe.transpose(B[:, 0:P], unat[:, LAST, g * P:(g + 1) * P], ident)
                    pe.transpose(B[:, P:P + DECB * BUF], cpn[:, g * P:(g + 1) * P], ident[0:DECB * BUF, 0:DECB * BUF]).then_inc(ut_done, 1)
                    if g:
                        pool_mix(pe, L, g - 1)
                pool_mix(pe, L, NH - 1)
                pe.wait_ge(plo, 8 * (L + 1))
                pe.wait_ge(uT_done, 12 * (L + 1))
                for t in range(NT):
                    T = NT * L + t
                    pe.wait_ge(rope, T + 1)
                    if t:
                        pe.wait_ge(qk_ev, 2 * T)
                        pe.wait_ge(qd_done, T)
                    for h in range(NH):
                        pe.transpose(ps[0][:, h * P:(h + 1) * P], zq(t, "q")[:, h * P:(h + 1) * P], ident)
                    for h in range(NH):
                        last = pe.transpose(ps[1][:, h * P:(h + 1) * P], zq(t, "k")[:, h * P:(h + 1) * P], ident)
                    last.then_inc(qk_tr, 1)
                    pe.wait_ge(qk_ev, 2 * T + 2)
                    if t:
                        pe.wait_ge(sc_ev, T)
                    for h in range(NH):
                        last = pe.matmul(ps[2][:, h * P:(h + 1) * P], kT[:, h, :], qT[:, h, :], start=True, stop=True)
                    last.then_inc(sc_mm, 1)
                    if t:
                        on_t(pe, L, t - 1)
                    pe.wait_ge(sc_ev, T + 1)
                    pe.wait_ge(qd_done, T + 1)
                    for tt in (t,):
                        z_there(pe, L, 3, tt)
                    if t < LAST:
                        if t:
                            pe.wait_ge(gn_free, T)
                            pe.wait_ge(st_ready, 4 * L + t)
                        for h in range(NH):
                            out = ps[3][:, h * P:(h + 1) * P]
                            last = pe.matmul(out, scT[:, h, :], zq(t, "v")[:, h * P:(h + 1) * P], start=True, stop=(t == 0))
                            if t:
                                last = pe.matmul(out, qdT[:, h, :], st[:, h, :], start=False, stop=True)
                        last.then_inc(o_mm, 1)
                        pe.wait_ge(kd_done, T + 1)
                        for h in range(NH):
                            last = pe.matmul(ps[4][:, h * P:(h + 1) * P], kd[:, h, :], zq(t, "v")[:, h * P:(h + 1) * P], start=True, stop=True)
                        last.then_inc(kv_mm, 1)
                    else:
                        for h in range(NH):
                            out = ps[6][:, h * P:(h + 1) * P]
                            pe.wait_ge(s0_ld[h % 2], 16 * (2 * L + h // 2 + 1))
                            pe.matmul(out, zq(t, "v")[:, h * P:(h + 1) * P], scT[:, h, :], start=True, stop=False)
                            for b in range(DECB):
                                last = pe.matmul(out[:, b * DECS:(b + 1) * DECS], s0[h % 2][:, b, :], qdT[:, h, b * DECS:(b + 1) * DECS],
                                                 start=False, stop=(b == DECB - 1))
                            if h == NH - 1:
                                last.then_inc(o_mm, 1)
                            pe.wait_ge(vb_done, NH * L + h + 1)
                            if h:
                                pe.wait_ge(s_new, NH * L + h)
                            else:
                                pe.wait_ge(st_ready, 4 * L + 4)
                                pe.wait_ge(kd_done, T + 1)
                            for n in range(2):
                                last = pe.matmul(ps[4 + n][:, :], kd[:, h, :], vb[:, 4 * n:4 * n + 4, :], start=True, stop=True)
                            last.then_inc(skv_mm, 1)
                        pe.wait_ge(o_ev, L + 1)
                        pe.wait_ge(gn_free, T)
                        for h in range(NH):
                            last = pe.transpose(ps[3][:, h * P:(h + 1) * P], scT[:, h, :], ident)
                        last.then_inc(o_back, 1)
                on_t(pe, L, LAST)
                pe.wait_ge(phi, 8 * (L + 1))
                pe.wait_ge(olo, NT * (L + 1))
                pe.wait_ge(s_new, NH * (L + 1))
                for s in range(WIN_STEPS, W_STEPS):
                    n, k = divmod(s - WIN_STEPS, KC)
                    S = W_STEPS * L + s
                    pe.wait_ge(wlo, S + 1)
                    for t in range(NT):
                        m = 5 * n + t
                        if k == 0 and m >= 8:
                            pe.wait_ge(xw, 10 * L + m - 7)
                        last = three(ps[m % 8][:, :], hT[:, k, t * P:(t + 1) * P], lT[:, k, t * P:(t + 1) * P],
                                     wh[S % SPL][:, :], wl[S % SPL][:, :], k == 0, k == KC - 1)
                        if k == KC - 1:
                            last.then_inc(xmm, 1)
                    if k < KC - 1:
                        last.then_inc(wpe, 1)
                transposes(2 * L + 1)
                pe.wait_ge(lo_done, 10 * (2 * L + 2))
                pe.wait_ge(wr_lo, L + 1)
                for t in range(NT):
                    for k in range(KC):
                        last = three(ps[4][:, 32 * t:32 * t + 20], hT[:, k, t * P:(t + 1) * P], lT[:, k, t * P:(t + 1) * P],
                                     wrh[:, k, :], wrl[:, k, :], k == 0, k == KC - 1)
                last.then_inc(lg_mm, 1)
                pe.wait_ge(taken_done, L + 1)
                for t in range(NT):
                    for u in range(t + 1):
                        pe.matmul(ps[5][:, t * NE:(t + 1) * NE], tri[:, 0:P] if u == t else tri[:, P:2 * P], taken[:, u, :],
                                  start=(u == 0), stop=(u == t))
                for u in range(NT):
                    last = pe.matmul(ps[5][:, 96:96 + NE], tri[:, P:2 * P], taken[:, u, :], start=(u == 0), stop=(u == NT - 1))
                last.then_inc(pos_mm, 1)
                def uses(s):
                    return L * EUSES[s]
                pe.wait_ge(gat[0], 16 * (uses(0) + 1))
                rows_t(0).then_inc(t_mm, 1)
                expert(L, 0, 0, (32 * (uses(0) + 1), None, 16 * (uses(1) + 1)), True, False)
                with pe.Fori(0, (LOOP1 - LOOP0) // 3) as i:
                    for j in range(3):
                        s = (1 + j) % 3
                        n = uses(s) + i + 1 + (j == 2)
                        p = uses((s + 2) % 3) + i + 1
                        q = uses((s + 1) % 3) + i + 1 + (j >= 1)
                        expert(L, i * 3 + (1 + j), s, (n * 32, p * 16, q * 16), True, True)
                for e in range(LOOP1, NE):
                    s = e % 3
                    expert(L, e, s, (32 * slot_count(L, s, e), 16 * slot_count(L, (s + 2) % 3, e - 1),
                                     16 * slot_count(L, (s + 1) % 3, e + 1) if e < NE - 1 else None), e < NE - 1, True)
                run_down(L, NE - 1, (NE - 1) % 3, 16 * slot_count(L, (NE - 1) % 3, NE - 1))
                v = ov[L]
                pe.wait_ge(most_done, L + 1)
                n = pe.value_load(most[0:1, 0:1], min_val=0, max_val=2 * TOK)
                with pe.If(n > P):
                    pe.wait_ge(yA, NE * (L + 1))
                    pe.wait_ge(yV, NE * (L + 1))
                    with pe.Fori(1, (NT - 1) * NE + 1) as i:
                        pe.wait_ge(v["g"], 16 * i)
                        rows_t(0).then_inc(v["t"], 1)
                        pe.wait_ge(v["h"], 2 * i)
                        pe.wait_ge(v["ld"], 48 * i)
                        gu(0).then_inc(v["gu"], 1)
                        pe.wait_ge(v["a"], i)
                        act_t().then_inc(v["at"], 1)
                        pe.wait_ge(v["aT"], i)
                        down(0).then_inc(v["d"], 1)
                        pe.wait_ge(v["y"], i)
                with pe.Else():
                    pe.wait_ge(yA, NE * (L + 1))
                pe.wait_ge(yV, NE * (L + 1))

        def o_lo(ve, L, t):
            ve.wait_ge(ohi, NT * L + t + 1)
            dst = (slice(None), slice(NH, KC), slice(t * P, (t + 1) * P))
            ve.tensor_tensor(lT[dst], heads(ps[7][:, :]), hT[dst].bitcast(F32), ALU.subtract).then_inc(olo, 1)

        def x_add(ve, L, n, t):
            m = 5 * n + t
            ve.wait_ge(xmm, 10 * L + m + 1)
            v = x[:, t, n * 512:(n + 1) * 512]
            ve.tensor_tensor(v, v, ps[m % 8][:, :], ALU.add).then_inc(xw, 1)

        def routing(ve, L, link):
            def col(i):
                return small[:, i, :]

            def wide(ap, n):
                return ap.unsqueeze(2).to_broadcast([P, NT, n])

            def first_of(vals, best, hot):
                link(ve.tensor_tensor(key[:, :, :], vals, wide(best, 4), ALU.is_ge))
                link(ve.tensor_tensor(key[:, :, :], key[:, :, :], c("rank4", NT), ALU.mult))
                link(ve.tensor_reduce(col(9), key[:, :, :], AX.X, ALU.max))
                link(ve.tensor_tensor(hot, key[:, :, :], wide(col(9), 4), ALU.is_equal))

            ve.wait_ge(lg_mm, L + 1)
            link(ve.tensor_tensor(lg[:, :, :], ps[4][:, 0:32 * NT].rearrange("p (t n) -> p t n", t=NT)[:, :, 0:20],
                                  over(rbias[:, :], NT), ALU.add))
            G = lg[:, :, 0:4]
            link(ve.tensor_reduce(col(0), G, AX.X, ALU.max))
            ve.tensor_tensor(gd[:, :, :], G, wide(col(0), 4), ALU.subtract).then_inc(gdone, 1)
            first_of(G, col(0), ohg[:, :, :])
            link(ve.tensor_tensor(prod[:, :, :, :], lg[:, :, 4:20].rearrange("p t (g j) -> p t g j", g=NG),
                                  ohg[:, :, :].unsqueeze(3).to_broadcast([P, NT, NG, EPG]), ALU.mult))
            link(ve.tensor_reduce(ing[:, :, :], prod[:, :, :, :].rearrange("p t g j -> p t j g"), AX.X, ALU.add))
            link(ve.tensor_reduce(col(1), ing[:, :, :], AX.X, ALU.max))
            first_of(ing[:, :, :], col(1), oh[0][:, :, :])
            link(ve.scalar_tensor_tensor(out=ing[:, :, :], in0=oh[0][:, :, :], scalar=-3.0e38, in1=ing[:, :, :], op0=ALU.mult, op1=ALU.add))
            link(ve.tensor_reduce(col(2), ing[:, :, :], AX.X, ALU.max))
            ve.tensor_tensor(col(4), col(2), col(1), ALU.subtract).then_inc(dv_done, 1)
            first_of(ing[:, :, :], col(2), oh[1][:, :, :])
            for k in range(2):
                last = ve.tensor_tensor(both[k][:, :, :].rearrange("p t (g j) -> p t g j", g=NG),
                                        ohg[:, :, :].unsqueeze(3).to_broadcast([P, NT, NG, EPG]),
                                        over(oh[k][:, :, :], NG, 2), ALU.mult)
            link(last)
            link(ve.tensor_tensor(picked[:, :, :], both[0][:, :, :], both[1][:, :, :], ALU.add))
            ve.tensor_tensor(taken[:, :, :], picked[:, :, :], wide(c("valid"), NE), ALU.mult).then_inc(taken_done, 1)
            ve.wait_ge(gexp, L + 1)
            link(ve.tensor_reduce(col(6), gex[:, :, :], AX.X, ALU.add))
            ve.wait_ge(dvexp, L + 1)
            link(ve.tensor_scalar(col(7), col(5), 1.0, None, ALU.add))
            link(ve.tensor_tensor(col(8), col(6), col(7), ALU.mult))
            link(ve.reciprocal(pgate[:, 0, :], col(8)))
            link(ve.tensor_tensor(pgate[:, 1, :], pgate[:, 0, :], col(5), ALU.mult))
            ve.wait_ge(pos_mm, L + 1)
            link(ve.scalar_tensor_tensor(out=where[:, :], in0=ps[5][:, 0:NT * NE], scalar=float(NE), in1=c("iota"), op0=ALU.mult, op1=ALU.add))
            for k in range(2):
                link(ve.tensor_tensor(picked[:, :, :], both[k][:, :, :], where[:, :].rearrange("p (t e) -> p t e", t=NT), ALU.mult))
                link(ve.tensor_reduce(col(10 + k), picked[:, :, :], AX.X, ALU.add))
                last = ve.tensor_tensor(slot_u[:, k, :], col(10 + k), c("drop"), ALU.add)
            last.then_inc(slots_done, 1)
            link(ve.tensor_reduce(most_f[:, :], ps[5][:, 96:96 + NE], AX.X, ALU.max))
            ve.tensor_copy(most[:, :], most_f[:, :]).then_inc(most_done, 1)
            ve.wait_ge(idx_ld, 16 * (L + 1))
            link(ve.tensor_scalar(tmpf[:, :], pidx[:, :], float(TOK), -float(TOK), ALU.is_ge, ALU.mult))
            ve.tensor_tensor(tidx[:, :], tmpf[:, :], pidx[:, :], ALU.add).then_inc(tidx_done, 1)

        @block.vector
        def _(ve):
            chain = [0]

            def link(ins):
                chain[0] += 1
                ins.then_inc(dve_chain, 1)
                ve.wait_ge(dve_chain, chain[0])

            def norm_rows(n, lo=True):
                ve.wait_ge(rms_done, n + 1)
                link(ve.reciprocal(rstd[:, :], rms[:, :]))
                ve.wait_ge(gain_ld, 16 * (n + 1))
                for t in range(NT):
                    if t >= 2:
                        if lo:
                            ve.wait_ge(tr_done, 10 * n + 2 * (t - 1))
                        if n % 2 or not lo:
                            ve.wait_ge(xn_st[t % 2], 16 * ((3, 2)[t % 2] * (n // 2) + t // 2))
                    ve.scalar_tensor_tensor(out=xn[t % 2][:, :], in0=x[:, t, :], scalar=rstd[:, t:t + 1], in1=gain[:, :],
                                            op0=ALU.mult, op1=ALU.mult).then_inc(xn_done, 1)
                    if lo and t:
                        norm_lo(n, t - 1)
                if lo:
                    norm_lo(n, LAST)

            def norm_lo(n, t):
                for half in range(2):
                    i = 2 * t + half
                    ve.wait_ge(hi_done, 10 * n + i + 1)
                    dst = (slice(None), slice(4 * half, 4 * half + 4), slice(t * P, (t + 1) * P))
                    ve.tensor_tensor(lT[dst], ps[i % 4][:, :].rearrange("p (k c) -> p k c", k=4), hT[dst].bitcast(F32),
                                     ALU.subtract).then_inc(lo_done, 1)

            def w_lo(L, s):
                S = W_STEPS * L + s
                ve.wait_ge(whi, S + 1)
                ve.tensor_tensor(wl[S % SPL][:, :], raw[S % RAW][:, :], wh[S % SPL][:, :].bitcast(F32), ALU.subtract).then_inc(wlo, 1)

            def expert(L, e, s, nxt, prev):
                X = NE * L + e
                ve.wait_ge(silu_done, X + 1)
                ve.tensor_tensor(act[:, :], act[:, :], ps[0][:, F:2 * F], ALU.mult).then_inc(act_done, 1)
                if nxt:
                    ve.wait_ge(t_mm, X + 2)
                    ve.tensor_copy(hgT[(s + 1) % 3][:, 4:8, :], ps[2][:, :].rearrange("p (k c) -> p k c", k=4)).then_inc(hgV, 1)
                if prev:
                    y_evac(L, e - 1, (s + 2) % 3)

            def y_evac(L, e, s):
                ve.wait_ge(dn_mm, NE * L + e + 1)
                if isinstance(e, int) and e == NE - 1:
                    ve.wait_ge(y_sc[s], 16 * (slot_count(L, s, e) - 1))
                ve.tensor_copy(y[s][:, 512:D], ps[4][:, :]).then_inc(yV, 1)

            ve.memset(x[NSAMP:P, LAST, :], 0.0).then_inc(ready0, 1)
            for L in range(NL):
                if L == 0:
                    ve.wait_ge(cst_ld, 48)
                    ve.wait_ge(ready0, 5)
                norm_rows(2 * L)
                for s in range(WIN_STEPS):
                    w_lo(L, s)
                    if s % KC == 3 and s > KC:
                        g = s // KC - 1
                        for t in (1, 3):
                            m = 5 * g + t
                            ve.wait_ge(zmm, 25 * L + m + 1)
                            dst = unat[:, t, :] if g == 0 else z[:, t, g - 1, :]
                            ve.tensor_copy(dst, ps[m % 8][:, :]).then_inc(zfree[m % 8], 1)
                for s in range(WIN_STEPS, WIN_STEPS + SPL):
                    w_lo(L, s)
                ve.wait_ge(small_ld, 128 * (L + 1))
                link(ve.tensor_copy(wrh[:, :, :], wr[:, :, :]))
                ve.tensor_tensor(wrl[:, :, :], wr[:, :, :], wrh[:, :, :].bitcast(F32), ALU.subtract).then_inc(wr_lo, 1)
                w = 0
                for g in range(NH):
                    w += g + 1
                    ve.wait_ge(win_done, 10 * L + w)
                    if g or L:
                        ve.wait_ge(yp_done, NH * L + g)
                    win = (winA, winB)[g % 2]
                    inv = 1.0 / (2 << g)
                    link(ve.tensor_tensor(edge[:, :], win[:, 16:32], c("inv", NH)[:, g, :], ALU.mult))
                    ve.tensor_tensor(dT[:, 0:16], edge[:, :], uT[:, 16:32], ALU.subtract)
                    ve.scalar_tensor_tensor(out=dT[:, 16:SEQ], in0=win[:, 32:16 + SEQ], scalar=inv, in1=uT[:, 32:16 + SEQ],
                                            op0=ALU.mult, op1=ALU.subtract)
                    ws = win[:, 16 + SEQ:].rearrange("p (b w) -> p b w", b=DECB)[:, :, 16:24]
                    us = uT[:, 16 + SEQ:].rearrange("p (b w) -> p b w", b=DECB)[:, :, 16:24]
                    ve.scalar_tensor_tensor(out=dT[:, SEQ:SEQ + NSAMP].rearrange("p (b s) -> p b s", b=DECB), in0=ws, scalar=inv, in1=us,
                                            op0=ALU.mult, op1=ALU.subtract).then_inc(d_done, 1)
                    ve.wait_ge(phi, 8 * L + 2 * g + 1)
                    ve.scalar_tensor_tensor(out=lT[:, g, 0:SEQ], in0=ps[4][:, :], scalar=pscale[:, g:g + 1], in1=hT[:, g, 0:SEQ].bitcast(F32),
                                            op0=ALU.mult, op1=ALU.subtract).then_inc(plo, 1)
                    ve.wait_ge(phi, 8 * L + 2 * g + 2)
                    ve.scalar_tensor_tensor(out=lT[:, g, SEQ:TOK], in0=ps[5][:, 0:P], scalar=pscale[:, g:g + 1], in1=hT[:, g, SEQ:TOK].bitcast(F32),
                                            op0=ALU.mult, op1=ALU.subtract).then_inc(plo, 1)
                for t in range(NT):
                    z_there(ve, L, 4, t)
                    last = ve.tensor_tensor(z[:, t, 3, :], z[:, t, 3, :], gnrow[:, :], ALU.mult)
                last.then_inc(sg_done, 1)
                ve.wait_ge(sg_done, L + 1)
                ve.wait_ge(upool_st, 32 * (L + 1))
                for t in range(NT):
                    T = NT * L + t
                    kind = 1 if t == LAST else 0
                    ve.wait_ge(rope, T + 1)
                    if 1 <= t:
                        ve.wait_ge(kv_mm, 4 * L + t)
                    ve.tensor_tensor(kd[:, :, :], heads(zq(t, "k")), c("kdec", 2)[:, kind, :].unsqueeze(2).to_broadcast([P, NH, P]),
                                     ALU.mult).then_inc(kd_done, 1)
                    ve.wait_ge(qk_ev, 2 * T + 1)
                    if t:
                        ve.wait_ge(o_mm, T)
                    ve.tensor_tensor(qdT[:, :, :], heads(ps[0][:, :]), c("qdec", 2, NH)[:, kind, :, :], ALU.mult).then_inc(qd_done, 1)
                    if t:
                        o_lo(ve, L, t - 1)
                    ve.wait_ge(sc_mm, T + 1)
                    ve.tensor_tensor(scT[:, :, :], heads(ps[2][:, :]), c("decay", 2, NH)[:, kind, :, :], ALU.mult).then_inc(sc_ev, 1)
                    if t < LAST:
                        ve.wait_ge(kv_mm, 4 * L + t + 1)
                        if t == 0 and L:
                            ve.wait_ge(st_st, 16 * L)
                        for h in range(NH):
                            if t == 0:
                                last = ve.tensor_copy(st[:, h, :], ps[4][:, h * P:(h + 1) * P])
                            else:
                                last = ve.scalar_tensor_tensor(out=st[:, h, :], in0=st[:, h, :], scalar=float(chunk_decay[0][h]),
                                                               in1=ps[4][:, h * P:(h + 1) * P], op0=ALU.mult, op1=ALU.add)
                        last.then_inc(st_ready, 1)
                        ve.wait_ge(st_ready, 4 * L + t + 1)
                    else:
                        for h in range(NH):
                            if h:
                                ve.wait_ge(skv_mm, NH * L + h)
                            ve.tensor_tensor(vb[:, :, :], over(zq(t, "v")[:, h * P:(h + 1) * P], DECB),
                                             c("seqm").unsqueeze(2).to_broadcast([P, DECB, P]), ALU.mult).then_inc(vb_done, 1)
                            ve.wait_ge(skv_mm, NH * L + h + 1)
                            for n in range(2):
                                v = s0[h % 2][:, 4 * n:4 * n + 4, :]
                                last = ve.scalar_tensor_tensor(out=v, in0=v, scalar=float(chunk_decay[1][h]),
                                                               in1=ps[4 + n][:, :].rearrange("p (b e) -> p b e", b=4), op0=ALU.mult, op1=ALU.add)
                            last.then_inc(s_new, 1)
                        ve.wait_ge(o_back, L + 1)
                    ve.wait_ge(o_mm, T + 1)
                    for h in range(NH):
                        last = ve.bn_stats(bnst[:, h, :], ps[3][:, h * P:(h + 1) * P])
                    link(last)
                    for h in range(NH):
                        last = ve.bn_aggr(mv[:, h, :], bnst[:, h, :])
                    last.then_inc(gn_st, 1)
                    ve.wait_ge(gn_rt, T + 1)
                    link(ve.reciprocal(gnrs[:, :], gnrt[:, :]))
                    if t:
                        ve.wait_ge(on_tr, T)
                    for h in range(NH):
                        last = ve.tensor_scalar(on[:, h, :], ps[3][:, h * P:(h + 1) * P], mv[:, h, 0:1], gnrs[:, h:h + 1], ALU.subtract, ALU.mult)
                    last.then_inc(gn_free, 1)
                    ve.wait_ge(gn_free, T + 1)
                    ve.tensor_tensor(on[:, :, :], on[:, :, :], heads(zq(t, "g")), ALU.mult).then_inc(on_done, 1)
                o_lo(ve, L, LAST)
                for s in range(WIN_STEPS + SPL, W_STEPS):
                    w_lo(L, s)
                    if s == WIN_STEPS + KC + 3:
                        for t in range(NT):
                            x_add(ve, L, 0, t)
                for t in range(NT):
                    x_add(ve, L, 1, t)
                norm_rows(2 * L + 1)
                routing(ve, L, link)
                ve.wait_ge(t_mm, NE * L + 1)
                ve.tensor_copy(hgT[0][:, 4:8, :], ps[2][:, :].rearrange("p (k c) -> p k c", k=4)).then_inc(hgV, 1)
                expert(L, 0, 0, True, False)
                with ve.Fori(0, (LOOP1 - LOOP0) // 3) as i:
                    for j in range(3):
                        expert(L, i * 3 + (1 + j), (1 + j) % 3, True, True)
                for e in range(LOOP1, NE):
                    expert(L, e, e % 3, e < NE - 1, True)
                y_evac(L, NE - 1, (NE - 1) % 3)
                v = ov[L]
                ve.wait_ge(most_done, L + 1)
                n = ve.value_load(most[0:1, 0:1], min_val=0, max_val=2 * TOK)
                with ve.If(n > P):
                    with ve.Fori(1, (NT - 1) * NE + 1) as i:
                        ve.wait_ge(v["s"], i)
                        ve.tensor_tensor(act[:, :], act[:, :], ps[0][:, F:2 * F], ALU.mult).then_inc(v["a"], 1)
                with ve.Else():
                    ve.wait_ge(dn_mm, NE * (L + 1))
                for i in range(2 * NT):
                    k, t = divmod(i, NT)
                    n = P if t < LAST else NSAMP
                    per = 2 if i % 6 < 4 else 1
                    ve.wait_ge(comb_ld[i % 6], 16 * (per * L + i // 6 + 1))
                    if k:
                        ve.wait_ge(comb, 10 * L + t + 1)
                    ve.scalar_tensor_tensor(out=x[0:n, t, :], in0=(hg + y)[i % 6][0:n, :], scalar=pgate[0:n, k, t:t + 1], in1=x[0:n, t, :],
                                            op0=ALU.mult, op1=ALU.add).then_inc(comb, 1)
            norm_rows(2 * NL, lo=False)



_INS = ["x_prompt", "x_sample", "cache_pool", "state_ret", "norm_mix", "w_in", "w_pool", "pool_scale", "ret_gn", "w_out",
        "norm_ffn", "w_router_group", "b_router_group", "w_router_expert", "b_router_expert", "w_gate", "w_up", "w_down",
        "norm_final"]
_OUTS = [("y_prompt", (1, SEQ, D)), ("y_sample", (DECB, DECS, D)), ("new_pool_prompt", (NL, 1, BUF, PW)),
         ("new_ret_prompt", (NL, 1, NH, P, P)), ("new_pool_sample", (NL, DECB, BUF, PW)), ("new_ret_sample", (NL, DECB, NH, P, P))]


def kernel(**inputs):
    import concourse.bacc as bacc
    from concourse.bass_utils import run_bass_kernel_spmd as run
    import ml_dtypes

    nc = bacc.Bacc("TRN2", target_bir_lowering=False, num_devices=1)
    arrays, aps = {}, {}
    _, cst, tri, ints, _ = constant_tables()
    host = {k: np.ascontiguousarray(inputs[k]) for k in _INS}
    host.update(cst=cst, tri=tri.astype(ml_dtypes.bfloat16), ints=ints)
    for k, v in host.items():
        arrays[f"in_{k}"] = v
        aps[k] = nc.dram_tensor(f"in_{k}", v.shape, mybir.dt.from_np(v.dtype), kind="ExternalInput").ap()
    outs = {k: nc.dram_tensor(f"out_{k}", s, F32, kind="ExternalOutput").ap() for k, s in _OUTS}
    build(nc, aps, outs)
    r = run(nc, [arrays], core_ids=[0])
    return tuple(r.results[0][f"out_{k}"] for k, _ in _OUTS)
```

```python
from contextlib import ExitStack

import numpy as np

import concourse.bass as bass
from concourse import mybir

ALU = mybir.AluOpType
ACT = mybir.ActivationFunctionType
AX = mybir.AxisListType
F32 = mybir.dt.float32
F32R = mybir.dt.float32r
BF16 = mybir.dt.bfloat16
I32 = mybir.dt.int32
U32 = mybir.dt.uint32

P = 128
D = 1024
SEQ, DECB, DECS, PAST = 512, 8, 8, 4096
NL = 2
KC = D // P
NT = 5
LAST = NT - 1
NSAMP = DECB * DECS
TOK = NT * P
PW = 512
NH = 4
HALF = 64
BUF = 15
IN_W = 5 * PW
NE, NG, EPG = 16, 4, 4
F = 256
UW = 16 + SEQ + DECB * 24
WIN_STEPS, WOUT_STEPS = 5 * KC, 2 * KC
W_STEPS = WIN_STEPS + WOUT_STEPS
RAW, SPL = 3, 4
LOOP0, LOOP1 = 4, 13
EPS_RMS, EPS_GN = 1e-6, 1e-5
OUT_OF_RANGE = 1000000.0


def constant_tables():
    f = np.float32
    p = np.arange(P)
    pos = np.zeros((P, NT), f)
    for t in range(LAST):
        pos[:, t] = t * P + p
    pos[:, LAST] = PAST + p % DECS
    inv = f(10000.0) ** (-(np.arange(HALF, dtype=f)) / f(HALF))
    ang = (pos[:, :, None] * inv.astype(f)[None, None, :]).astype(f)
    log_g = np.log(f(1.0) - f(2.0) ** (-5.0 - np.arange(NH, dtype=f))).astype(f)
    scale = f(P) ** f(-0.5)

    def decay(chunk):
        i, j = p[None, :], p[:, None]
        same = (i // chunk == j // chunk) & (i >= j)
        e = np.exp(np.maximum(i - j, 0).astype(f)[:, None, :] * log_g[None, :, None])
        return np.where(same[:, None, :], e, 0).astype(f) * scale

    def qdecay(chunk):
        row = np.exp(((p % chunk) + 1.0).astype(f)[None, :] * log_g[:, None])
        return np.broadcast_to(row[None], (P, NH, P))

    def kdecay(chunk):
        return np.exp((chunk - 1.0 - (p % chunk)).astype(f)[:, None] * log_g[None]) * scale

    invc = np.zeros((NH, 16), f)
    for g, w in enumerate((2, 4, 8, 16)):
        invc[g] = 1.0 / np.minimum(w, np.arange(16) + 1)
    seq_mask = (p[:, None] // DECS == np.arange(DECB)[None]) & (p[:, None] < NSAMP)
    valid = np.ones((P, NT), f)
    valid[NSAMP:, LAST] = 0
    parts = {
        "cos": np.cos(ang), "sin": np.sin(ang), "nsin": -np.sin(ang),
        "decay": np.stack([decay(P), decay(DECS)], 1),
        "qdec": np.stack([qdecay(P), qdecay(DECS)], 1),
        "kdec": np.stack([kdecay(P), kdecay(DECS)], 1),
        "seqm": seq_mask, "inv": np.broadcast_to(invc[None], (P, NH, 16)),
        "ident": np.eye(P),
        "rank4": np.broadcast_to(np.array([4, 3, 2, 1], f), (P, NT, 4)),
        "iota": np.broadcast_to(np.arange(NE, dtype=f), (P, NT, NE)),
        "valid": valid, "drop": (1 - valid) * OUT_OF_RANGE,
    }
    at, cols, n = {}, [], 0
    for k, a in parts.items():
        a = np.asarray(a, f).reshape(P, -1)
        at[k] = (n, n + a.shape[1])
        n += a.shape[1]
        cols.append(a)
    tri = np.concatenate([(p[:, None] < p[None, :]), np.ones((P, P))], 1)
    pair = (np.arange(2)[None, :, None] * TOK + np.arange(NT)[None, None, :] * P + p[:, None, None])
    ints = np.concatenate([pair.reshape(P, 2 * NT), np.full((P, NT * NE), 4096)], 1)
    chunk = np.exp(f(P) * log_g), np.exp(f(DECS) * log_g)
    return at, np.concatenate(cols, 1).astype(f), tri.astype(f), ints.astype(np.uint32), chunk


def build(nc, a, o):
    at, _, _, _, chunk_decay = constant_tables()
    ncst = max(v[1] for v in at.values())
    ctx = ExitStack()
    with ctx:
        top = [((nc.sbuf_base + 63) // 64) * 64]

        def place(nbytes):
            off = top[0]
            top[0] += (nbytes + 31) // 32 * 32
            assert top[0] <= nc.SBUF_PARTITION_SIZE_BYTES, top[0]
            return off

        def tile(name, shape, dt=F32, off=None):
            size = int(np.prod(shape[1:])) * (2 if dt == BF16 else 4)
            return nc.alloc_sbuf_tensor_at(name, shape, dt, offset=place(size) if off is None else off)

        cst = tile("cst", [P, ncst])
        tri = tile("tri", [P, 2 * P], BF16)
        ints = tile("ints", [P, 2 * NT + NT * NE], U32)
        x = tile("x", [P, NT, D])
        gain = tile("gain", [P, D])
        wpool = tile("wpool", [P, NH, P])
        pscale = tile("pscale", [P, NH])
        gnrow = tile("gnrow", [P, PW])
        cpn = tile("cpn", [DECB * BUF, PW])
        wr = tile("wr", [P, KC, 20])
        wrh = tile("wrh", [P, KC, 20], F32R)
        wrl = tile("wrl", [P, KC, 20], F32R)
        rbias = tile("rbias", [P, 20])
        wring = place(4096 * SPL)
        wh = [tile(f"wh{i}", [P, PW], F32R, off=wring + 2048 * i) for i in range(SPL)]
        wl = [tile(f"wl{i}", [P, PW], F32R, off=wring + 2048 * (SPL + i)) for i in range(SPL)]
        e0 = place(24 * 1024)
        shared = place(48 * 1024)
        slot_at = [e0, shared, shared + 24 * 1024]
        wgu = [tile(f"wgu{s}", [P, KC, 2 * F], off=slot_at[s]) for s in range(3)]
        wdn = [tile(f"wdn{s}", [P, 2, D], off=slot_at[s] + 16 * 1024) for s in range(3)]
        gul = [tile(f"gul{s}", [P, KC, 2 * F], F32R, off=slot_at[s]) for s in range(3)]
        dnl = [tile(f"dnl{s}", [P, 2, D], F32R, off=slot_at[s] + 16 * 1024) for s in range(3)]
        z = tile("z", [P, NT, 4, PW], off=shared)
        raw = [tile(f"raw{i}", [P, PW], off=shared + 40 * 1024 + 2048 * i) for i in range(RAW)]
        region = place(40 * 1024)
        hT = tile("hT", [P, KC, TOK], F32R, off=region)
        lT = tile("lT", [P, KC, TOK], F32R, off=region + 20 * 1024)
        hg = [tile(f"hg{i}", [P, D], off=region + 4096 * i) for i in range(3)]
        y = [tile(f"y{i}", [P, D], off=region + 4096 * (3 + i)) for i in range(3)]
        hgTh = tile("hgTh", [P, KC, P], F32R, off=region + 4096 * 6)
        hgTl = tile("hgTl", [P, KC, P], F32R, off=region + 4096 * 7)
        act = tile("act", [P, F], off=region + 4096 * 9)
        actTh = tile("actTh", [P, 2, P], F32R, off=region + 4096 * 9 + 1024)
        actTl = tile("actTl", [P, 2, P], F32R, off=region + 4096 * 9 + 2048)
        pidx = tile("pidx", [P, NT * NE], U32, off=region + 4096 * 9 + 3072)
        tidx = tile("tidx", [P, NT * NE], U32, off=region + 4096 * 9 + 3072 + 320)
        tmpf = tile("tmpf", [P, NT * NE], off=region + 4096 * 9 + 3072 + 640)
        hgT = tile("hgT", [P, KC, P], off=region + 4096 * 6)
        actT = tile("actT", [P, 2, P], off=region + 4096 * 9 + 1024)
        back = hg + y + [tile(f"back{i}", [P, D], off=region + 4096 * (6 + i)) for i in range(3)]
        r12 = place(12 * 1024)
        xn = [tile(f"xn{i}", [P, D], off=r12 + 4096 * i) for i in range(2)]
        eh = [tile(f"eh{i}", [P, 2 * PW], F32R, off=wring + 4096 * i if i < 4 else r12 + 4096 * (i - 4)) for i in range(6)]
        unat = tile("unat", [P, NT, PW], off=r12)
        qT = tile("qT", [P, NH, P], off=r12)
        kT = tile("kT", [P, NH, P], off=r12 + 2048)
        qdT = tile("qdT", [P, NH, P], off=r12 + 2048 * 2)
        scT = tile("scT", [P, NH, P], off=r12 + 2048 * 3)
        kd = tile("kd", [P, NH, P], off=r12 + 2048 * 4)
        on = tile("on", [P, NH, P], off=r12 + 2048 * 5)
        rt = [r12 + 8192]

        def route(name, shape, dt=F32):
            off = rt[0]
            rt[0] += (int(np.prod(shape[1:])) * (2 if dt == BF16 else 4) + 31) // 32 * 32
            assert rt[0] <= r12 + 12 * 1024
            return tile(name, shape, dt, off)

        lg = route("lg", [P, NT, 20])
        gd = route("gd", [P, NT, 4])
        gex = route("gex", [P, NT, 4])
        key = route("key", [P, NT, 4])
        ohg = route("ohg", [P, NT, 4])
        prod = route("prod", [P, NT, NG, EPG])
        ing = route("ing", [P, NT, EPG])
        oh = [route(f"oh{k}", [P, NT, EPG]) for k in range(2)]
        both = [route(f"both{k}", [P, NT, NE]) for k in range(2)]
        taken = route("taken", [P, NT, NE], BF16)
        where = route("where", [P, NT * NE])
        picked = route("picked", [P, NT, NE])
        small = route("small", [P, 16, NT])
        pgate = tile("pgate", [P, 2, NT])
        slot_u = tile("slot_u", [P, 2, NT], U32)
        gidx = tile("gidx", [P, 1], U32)
        sidx = tile("sidx", [P, 1], U32)
        most_f = tile("most_f", [P, 1])
        most = tile("most", [P, 1], I32)
        ss = tile("ss", [P, NT])
        rms = tile("rms", [P, NT])
        rstd = tile("rstd", [P, NT])
        bnst = tile("bnst", [P, NH, 6])
        mv = tile("mv", [P, NH, 2])
        gnrt = tile("gnrt", [P, NH])
        gnrs = tile("gnrs", [P, NH])
        eps = tile("eps", [P, 2])
        s0 = [tile(f"s0{i}", [P, DECB, P]) for i in range(2)]
        st = tile("st", [P, NH, P])
        uT = tile("uT", [P, UW])
        dT = tile("dT", [P, TOK])
        edge = tile("edge", [P, 16])
        wa = place(2 * UW * 4)
        winA = tile("winA", [P, UW], off=wa)
        winB = tile("winB", [P, UW], off=wa + UW * 4)
        ropA = tile("ropA", [P, NH, 2, HALF], off=wa)
        ropB = tile("ropB", [P, NH, 2, HALF], off=wa + 2048)
        vb = tile("vb", [P, DECB, P], off=wa)

        ps = [ctx.enter_context(nc.psum_tensor(f"ps{i}", [P, 512], F32)) for i in range(8)]
        xn_d = nc.dram_tensor("xn_d", (TOK, D), F32).ap()
        y_d = nc.dram_tensor("y_d", (2 * TOK, D), F32).ap()
        tab_d = nc.dram_tensor("tab_d", (TOK * NE, 1), U32).ap()

        def sem(name):
            return ctx.enter_context(nc.semaphore(name))

        cst_ld = sem("cst_ld"); x_ld = [sem(f"x_ld{t}") for t in range(NT)]; gain_ld = sem("gain_ld")
        small_ld = sem("small_ld"); raw_ld = [sem(f"raw_ld{i}") for i in range(RAW)]
        s0_ld = [sem(f"s0_ld{i}") for i in range(2)]; gu_ld = [sem(f"gu_ld{i}") for i in range(3)]
        dn_ld = [sem(f"dn_ld{i}") for i in range(3)]; gat = [sem(f"gat{i}") for i in range(3)]
        comb_ld = [sem(f"comb_ld{i}") for i in range(9)]
        tab_init = sem("tab_init"); slot_sc = sem("slot_sc"); idx_ld = sem("idx_ld")
        xn_st = [sem(f"xn_st{i}") for i in range(2)]; upool_st = sem("upool_st"); st_st = sem("st_st")
        s0_st = [sem(f"s0_st{i}") for i in range(2)]; y_sc = [sem(f"y_sc{i}") for i in range(3)]
        out_st = sem("out_st")
        ready0 = sem("ready0"); sq_done = sem("sq_done"); rms_done = sem("rms_done"); xn_done = sem("xn_done")
        tr_done = sem("tr_done"); hi_done = sem("hi_done"); lo_done = sem("lo_done")
        whi = sem("whi"); wlo = sem("wlo"); wpe = sem("wpe"); zmm = sem("zmm")
        zfree = [sem(f"zfree{i}") for i in range(8)]
        xmm = sem("xmm"); xw = sem("xw"); sg_done = sem("sg_done")
        ut_done = sem("ut_done"); uT_done = sem("uT_done"); win_done = sem("win_done"); d_done = sem("d_done")
        yp_done = sem("yp_done"); phi = sem("phi"); plo = sem("plo")
        rope = sem("rope"); kd_done = sem("kd_done"); qk_tr = sem("qk_tr"); qk_ev = sem("qk_ev"); qd_done = sem("qd_done")
        sc_mm = sem("sc_mm"); sc_ev = sem("sc_ev"); o_mm = sem("o_mm"); kv_mm = sem("kv_mm"); s_upd = sem("s_upd")
        st_ready = sem("st_ready"); o_ev = sem("o_ev"); o_back = sem("o_back"); gn_st = sem("gn_st"); gn_rt = sem("gn_rt")
        gn_free = sem("gn_free"); on_done = sem("on_done"); on_tr = sem("on_tr"); ohi = sem("ohi"); olo = sem("olo")
        vb_done = sem("vb_done"); skv_mm = sem("skv_mm"); s_new = sem("s_new")
        wr_hi = sem("wr_hi"); wr_lo = sem("wr_lo"); lg_mm = sem("lg_mm"); gdone = sem("gdone"); gexp = sem("gexp")
        dv_done = sem("dv_done"); dvexp = sem("dvexp"); taken_done = sem("taken_done"); pos_mm = sem("pos_mm")
        slots_done = sem("slots_done"); tidx_done = sem("tidx_done"); hg_clear = sem("hg_clear"); most_done = sem("most_done")
        ghi = sem("ghi"); glo = sem("glo"); gpe = sem("gpe")
        dhi = sem("dhi"); dlo = sem("dlo"); dpe = sem("dpe")
        t_mm = sem("t_mm"); hg_hi = sem("hg_hi"); hg_lo = sem("hg_lo"); silu_done = sem("silu_done")
        act_done = sem("act_done"); at_mm = sem("at_mm"); at_hi = sem("at_hi"); at_lo = sem("at_lo")
        yA = sem("yA"); yV = sem("yV")
        comb = sem("comb")
        ov = [{k: sem(f"ov{L}_{k}") for k in ("ld", "g", "t", "h", "gu", "s", "a", "at", "aT", "d", "y", "sc")}
              for L in range(NL)]
        dve_chain = sem("dve_chain"); act_chain = sem("act_chain"); pool_chain = sem("pool_chain")

        def c(name, *shape):
            v = cst[:, at[name][0]:at[name][1]]
            if len(shape) == 1:
                return v.rearrange("p (a b) -> p a b", a=shape[0])
            if len(shape) == 2:
                return v.rearrange("p (a b c) -> p a b c", a=shape[0], b=shape[1])
            return v

        ident = c("ident")
        OFFS = {"q": 0, "k": 1, "v": 2, "g": 3}

        def zq(t, name):
            return z[:, t, OFFS[name], :]

        def heads(ap):
            return ap.rearrange("p (h d) -> p h d", h=NH)

        def over(ap, n, dim=1):
            v = ap.unsqueeze(dim)
            shape = list(v.shape)
            shape[dim] = n
            return v.to_broadcast(shape)

        ZUSES = [len(range(b, 25, 8)) for b in range(8)]
        EUSES = [len(range(s, NE, 3)) for s in range(3)]

        def z_there(eng, L, g, t):
            m = 5 * g + t
            eng.wait_ge(zfree[m % 8], L * ZUSES[m % 8] + m // 8 + 1)

        def used(L, s, n):
            return n + (L * EUSES[s] + 1)

        def pair(ap, k):
            return ap[:, 2 * k:2 * k + 2, :].rearrange("p a b -> p (a b)")

        def experts(eng, body):
            def at(e):
                body(e, e % 3, tuple((e + d) // 3 for d in (-1, 0, 1)))
            for e in range(LOOP0):
                at(e)
            with eng.Fori(0, (LOOP1 - LOOP0) // 3) as i:
                for j in range(3):
                    body(i * 3 + (LOOP0 + j), (LOOP0 + j) % 3, tuple(i + (LOOP0 + j + d) // 3 for d in (-1, 0, 1)))
            for e in range(LOOP1, NE):
                at(e)

        def first(e):
            return isinstance(e, int) and e == 0

        def final(e):
            return isinstance(e, int) and e == NE - 1

        def step_done(eng, S):
            L, s = divmod(S, W_STEPS)
            g, k = divmod(s, KC)
            if k < KC - 1:
                eng.wait_ge(wpe, (W_STEPS * L // KC + g) * (KC - 1) + k + 1)
            elif g < 5:
                eng.wait_ge(zmm, 5 * NT * L + NT * (g + 1))
            else:
                eng.wait_ge(xmm, 2 * NT * L + NT * (g - 4))

        block = ctx.enter_context(nc.Block())

        @block.sync
        def _(sp):
            sp.dma_start(cst[:, :], a["cst"]).then_inc(cst_ld, 16)
            sp.dma_start(ints[:, :], a["ints"]).then_inc(cst_ld, 16)
            sp.dma_start(tri[:, :], a["tri"]).then_inc(cst_ld, 16)
            for t in range(LAST):
                sp.dma_start(x[:, t, :], a["x_prompt"][0, t * P:(t + 1) * P, :]).then_inc(x_ld[t], 16)
            sp.dma_start(x[0:NSAMP, LAST, :], a["x_sample"].rearrange("b s d -> (b s) d")).then_inc(x_ld[LAST], 16)

            def load_gain(n):
                if n:
                    sp.wait_ge(xn_done, 5 * n)
                src = a["norm_final"] if n == 2 * NL else a[("norm_mix", "norm_ffn")[n % 2]][n // 2]
                sp.dma_start(gain[:, :], src.partition_broadcast(P)).then_inc(gain_ld, 16)

            def load_raw(L, s):
                S = W_STEPS * L + s
                if S >= RAW:
                    sp.wait_ge(wlo, S - RAW + 1)
                if s < RAW and L:
                    sp.wait_ge(dpe, 2 * (NE * L - 1))
                if s < WIN_STEPS:
                    g, k = divmod(s, KC)
                    src = a["w_in"][L, k * P:(k + 1) * P, g * PW:(g + 1) * PW]
                else:
                    n, k = divmod(s - WIN_STEPS, KC)
                    src = a["w_out"][L, k * P:(k + 1) * P, n * PW:(n + 1) * PW]
                sp.dma_start(raw[S % RAW][:, :], src).then_inc(raw_ld[S % RAW], 16)

            def load_gu(L, e, s, wait=True):
                if wait:
                    sp.wait_ge(gpe, e * 4 + 4 * (NE * L - 2))
                sp.dma_start(wgu[s][:, :, 0:F], a["w_gate"][L, e].rearrange("(k p) f -> p k f", p=P)).then_inc(gu_ld[s], 16)
                sp.dma_start(wgu[s][:, :, F:2 * F], a["w_up"][L, e].rearrange("(k p) f -> p k f", p=P)).then_inc(gu_ld[s], 16)

            def load_dn(L, e, s, wait=True):
                if wait and not (isinstance(e, int) and NE * L + e == 2):
                    sp.wait_ge(dpe, e * 2 + 2 * (NE * L - 2))
                sp.dma_start(wdn[s][:, :, :], a["w_down"][L, e].rearrange("(k p) d -> p k d", p=P)).then_inc(dn_ld[s], 16)

            def overflow(L):
                v = ov[L]
                sp.wait_ge(most_done, L + 1)
                n = sp.value_load(most[0:1, 0:1], min_val=0, max_val=2 * TOK)
                with sp.If(n > P):
                    sp.wait_ge(dpe, 2 * NE * (L + 1))
                    sp.sem_inc(v["d"], 1)
                    with sp.Fori(1, NT) as turn:
                        with sp.Fori(0, NE) as e:
                            sp.wait_ge(v["d"], turn * NE + e - NE + 1)
                            sp.dma_start(wgu[0][:, :, 0:F], a["w_gate"][L, e].rearrange("(k p) f -> p k f", p=P)).then_inc(v["ld"], 16)
                            sp.dma_start(wgu[0][:, :, F:2 * F], a["w_up"][L, e].rearrange("(k p) f -> p k f", p=P)).then_inc(v["ld"], 16)
                            sp.dma_start(wdn[0][:, :, :], a["w_down"][L, e].rearrange("(k p) d -> p k d", p=P)).then_inc(v["ld"], 16)
                    sp.wait_ge(v["sc"], 16 * (NT - 1) * NE)
                with sp.Else():
                    sp.wait_ge(most_done, L + 1)

            load_gain(0)
            for L in range(NL):
                if L:
                    sp.wait_ge(comb, 2 * NT * (L - 1) + 1)
                sp.dma_start(wpool[:, :, :], a["w_pool"][L].rearrange("g c e -> c g e")).then_inc(small_ld, 16)
                sp.dma_start(pscale[:, :], a["pool_scale"][L].rearrange("(g e) -> e g", g=NH),
                             allow_slow_non_contiguous=True).then_inc(small_ld, 16)
                sp.dma_start(gnrow[:, :], a["ret_gn"][L].partition_broadcast(P)).then_inc(small_ld, 16)
                sp.dma_start(cpn[:, :], a["cache_pool"][L].rearrange("b r c -> (b r) c")).then_inc(small_ld, 16)
                sp.dma_start(wr[:, :, 0:4], a["w_router_group"][L].rearrange("(k p) n -> p k n", p=P)).then_inc(small_ld, 16)
                sp.dma_start(wr[:, :, 4:20], a["w_router_expert"][L].rearrange("(k p) n -> p k n", p=P)).then_inc(small_ld, 16)
                sp.dma_start(rbias[:, 0:4], a["b_router_group"][L].partition_broadcast(P)).then_inc(small_ld, 16)
                sp.dma_start(rbias[:, 4:20], a["b_router_expert"][L].partition_broadcast(P)).then_inc(small_ld, 16)
                sp.dma_start(o["new_pool_sample"][L, :, 0:BUF - DECS, :], a["cache_pool"][L, :, DECS:BUF, :]).then_inc(out_st, 16)
                for s in range(WIN_STEPS):
                    load_raw(L, s)
                    if s == 10:
                        load_gain(2 * L + 1)
                        if L:
                            sp.wait_ge(dpe, 2 * NE * L)
                        load_gu(L, 0, 0, False)
                        load_dn(L, 0, 0, False)
                    if s == 20:
                        for t in (3, LAST):
                            z_there(sp, L, 0, t)
                        sp.dma_start(o["new_pool_prompt"][L, 0], unat[P - BUF:P, 3, :]).then_inc(upool_st, 16)
                        sp.dma_start(o["new_pool_sample"][L, :, BUF - DECS:BUF, :].rearrange("b s c -> b s c"),
                                     unat[0:NSAMP, LAST, :]).then_inc(upool_st, 16)
                for s in range(WIN_STEPS, W_STEPS):
                    load_raw(L, s)
                step_done(sp, W_STEPS * (L + 1) - 1)
                load_gu(L, 1, 1, False)
                load_gu(L, 2, 2, False)
                load_dn(L, 1, 1, False)
                load_gain(2 * L + 2)
                for j in range(3):
                    load_gu(L, 3 + j, j)
                    load_dn(L, 2 + j, (2 + j) % 3)
                with sp.Fori(0, (NE - 7) // 3) as i:
                    for j in range(3):
                        load_gu(L, i * 3 + (6 + j), j)
                        load_dn(L, i * 3 + (5 + j), (2 + j) % 3)
                load_gu(L, NE - 1, 0)
                load_dn(L, NE - 2, 2)
                load_dn(L, NE - 1, 0)
                overflow(L)
                for s in range(3):
                    sp.wait_ge(y_sc[s], 16 * EUSES[s] * (L + 1))
                for i in range(2 * NT):
                    k, t = divmod(i, NT)
                    if i >= 9:
                        sp.wait_ge(comb, 2 * NT * L + i - 8)
                    n = P if t < LAST else NSAMP
                    sp.dma_start(back[i % 9][0:n, :], y_d[k * TOK + t * P:k * TOK + t * P + n, :]).then_inc(comb_ld[i % 9], 16)
            sp.wait_ge(out_st, 16 * NL)
            sp.wait_ge(upool_st, 32 * NL)
            sp.wait_ge(st_st, 16 * NL)
            for i in range(2):
                sp.wait_ge(s0_st[i], 32 * NL)

        @block.gpsimd
        def _(pool):
            chain = [0]

            def link(ins):
                chain[0] += 1
                ins.then_inc(pool_chain, 1)
                pool.wait_ge(pool_chain, chain[0])

            pool.memset(eps[:, 0:1], EPS_RMS).then_inc(ready0, 1)
            pool.memset(eps[:, 1:2], EPS_GN).then_inc(ready0, 1)
            pool.memset(uT[:, :], 0.0).then_inc(ready0, 1)
            pool.memset(dT[:, SEQ + NSAMP:TOK], 0.0).then_inc(ready0, 1)
            pool.wait_ge(cst_ld, 48)

            def gather(e):
                s = e % 3
                pool.indirect_dma_start(out=hg[s][:, :], out_offset=None, in_=xn_d,
                                        in_offset=bass.IndirectOffsetOnAxis(ap=tidx[:, e:e + 1], axis=0),
                                        bounds_check=TOK - 1, oob_is_err=False).then_inc(gat[s], 16)

            def scatter(L, e):
                s = e % 3
                pool.wait_ge(yA, NE * L + e + 1)
                pool.wait_ge(yV, NE * L + e + 1)
                pool.indirect_dma_start(out=y_d, out_offset=bass.IndirectOffsetOnAxis(ap=pidx[:, e:e + 1], axis=0),
                                        in_=y[s][:, :], in_offset=None,
                                        bounds_check=2 * TOK - 1, oob_is_err=False).then_inc(y_sc[s], 16)

            for L in range(NL):
                pool.dma_start(tab_d.rearrange("(j p e) o -> p j (e o)", j=NT, p=P),
                               ints[:, 2 * NT:].rearrange("p (j e) -> p j e", j=NT)).then_inc(tab_init, 16)
                for i in range(2):
                    if L:
                        pool.wait_ge(s0_st[i], 32 * L)
                    pool.dma_start(s0[i][:, :, :], a["state_ret"][L, :, i].rearrange("b d e -> d b e")).then_inc(s0_ld[i], 16)
                w = 0
                for g in range(NH):
                    pool.wait_ge(uT_done, 3 * (NH * L + g + 1))
                    if g or L:
                        pool.wait_ge(d_done, NH * L + g)
                    src = uT
                    for r in range(g + 1):
                        dst = (winA, winB)[r % 2]
                        n = 1 << r
                        lo = 2 * n - 1
                        pool.tensor_tensor(dst[:, lo:UW], src[:, lo:UW], src[:, lo - n:UW - n], ALU.add).then_inc(win_done, 1)
                        w += 1
                        pool.wait_ge(win_done, 10 * L + w)
                        src = dst
                pool.wait_ge(d_done, NH * (L + 1))
                for t in range(NT):
                    for qk in (0, 1):
                        z_there(pool, L, 1 + qk, t)
                        v = z[:, t, qk, :].rearrange("p (h s d) -> p h s d", h=NH, s=2)
                        cs, sn, ns = (c(n, NT)[:, t, :] for n in ("cos", "sin", "nsin"))
                        cosb = cs.unsqueeze(1).unsqueeze(1).to_broadcast([P, NH, 2, HALF])
                        pool.tensor_tensor(ropA[:, :, :, :], v, cosb, ALU.mult)
                        pool.tensor_tensor(ropB[:, :, 0, :], v[:, :, 1, :], over(ns, NH), ALU.mult)
                        link(pool.tensor_tensor(ropB[:, :, 1, :], v[:, :, 0, :], over(sn, NH), ALU.mult))
                        last = pool.tensor_tensor(v, ropA[:, :, :, :], ropB[:, :, :, :], ALU.add)
                        if qk == 0:
                            link(last)
                    last.then_inc(rope, 1)
                    pool.wait_ge(rope, NT * L + t + 1)
                for h in range(NH):
                    pool.wait_ge(s_new, NH * L + h + 1)
                    pool.dma_start(o["new_ret_sample"][L, :, h].rearrange("b d e -> d b e"), s0[h % 2][:, :, :]).then_inc(s0_st[h % 2], 16)
                    if h < 2:
                        pool.wait_ge(s0_st[h % 2], 32 * L + 16)
                        pool.dma_start(s0[h % 2][:, :, :], a["state_ret"][L, :, h + 2].rearrange("b d e -> d b e")).then_inc(s0_ld[h % 2], 16)
                pool.wait_ge(lg_mm, L + 1)
                for s in range(3):
                    pool.memset(hg[s][:, :], 0.0).then_inc(hg_clear, 1)
                pool.wait_ge(slots_done, L + 1)
                pool.wait_ge(tab_init, 16 * (L + 1))
                for i in range(2 * NT):
                    pool.indirect_dma_start(out=tab_d, out_offset=bass.IndirectOffsetOnAxis(ap=slot_u[:, i // NT, i % NT:i % NT + 1], axis=0),
                                            in_=ints[:, i:i + 1], in_offset=None,
                                            bounds_check=TOK * NE - 1, oob_is_err=False).then_inc(slot_sc, 16)
                pool.wait_ge(slot_sc, 16 * 2 * NT * (L + 1))
                pool.dma_start(pidx[:, :].rearrange("p (j e) -> p j e", j=NT),
                               tab_d.rearrange("(j p e) o -> p j (e o)", j=NT, p=P)).then_inc(idx_ld, 16)
                pool.wait_ge(tidx_done, L + 1)
                pool.wait_ge(hg_clear, 3 * (L + 1))
                for i in range(2):
                    n = (3, 2)[i]
                    pool.wait_ge(xn_st[i], 16 * n * (L + 1))
                for e in range(3):
                    gather(e)
                for e in range(NE):
                    if e + 3 < NE:
                        pool.wait_ge(t_mm, NE * L + e + 1)
                        gather(e + 3)
                    if e >= 2:
                        scatter(L, e - 2)
                scatter(L, NE - 2)
                scatter(L, NE - 1)
                v = ov[L]
                pool.wait_ge(most_done, L + 1)
                n = pool.value_load(most[0:1, 0:1], min_val=0, max_val=2 * TOK)
                with pool.If(n > P):
                    pool.wait_ge(t_mm, NE * (L + 1))
                    for s in range(3):
                        pool.wait_ge(y_sc[s], 16 * EUSES[s] * (L + 1))
                    with pool.Fori(1, NT) as turn:
                        with pool.Fori(0, NE) as e:
                            col = turn * NE + e
                            pool.tensor_copy(gidx[:, :], tidx[:, bass.ds(col, 1)])
                            pool.drain()
                            pool.indirect_dma_start(out=hg[0][:, :], out_offset=None, in_=xn_d,
                                                    in_offset=bass.IndirectOffsetOnAxis(ap=gidx[:, 0:1], axis=0),
                                                    bounds_check=TOK - 1, oob_is_err=False).then_inc(v["g"], 16)
                            pool.wait_ge(v["y"], col - NE + 1)
                            pool.tensor_copy(sidx[:, :], pidx[:, bass.ds(col, 1)])
                            pool.drain()
                            pool.indirect_dma_start(out=y_d, out_offset=bass.IndirectOffsetOnAxis(ap=sidx[:, 0:1], axis=0),
                                                    in_=y[0][:, :], in_offset=None,
                                                    bounds_check=2 * TOK - 1, oob_is_err=False).then_inc(v["sc"], 16)
                            pool.wait_ge(v["sc"], 16 * (col - NE + 1))
                with pool.Else():
                    pool.wait_ge(t_mm, NE * (L + 1))
                pool.wait_ge(t_mm, NE * (L + 1))

        def o_hi(eng, L, t):
            eng.wait_ge(on_tr, NT * L + t + 1)
            eng.activation(hT[:, NH:KC, t * P:(t + 1) * P], heads(ps[7][:, :]), ACT.Copy).then_inc(ohi, 1)

        @block.scalar
        def _(sc):
            chain = [0]

            def norm_squares(n):
                for t in range(NT):
                    if n == 0:
                        sc.wait_ge(x_ld[t], 16)
                        sc.wait_ge(ready0, 5)
                    elif n % 2:
                        sc.wait_ge(xw, 10 * (n // 2) + NT + t + 1)
                    else:
                        sc.wait_ge(comb, 10 * (n // 2 - 1) + NT + t + 1)
                    if n >= 2 and t < 2 and n % 2 == 0:
                        sc.wait_ge(xn_st[t], 16 * (3, 2)[t] * (n // 2))
                    if t >= 2:
                        sc.wait_ge(sq_done, NT * n + t - 1)
                    sc.activation(xn[t % 2][:, :], x[:, t, :], ACT.Square, accum_out=ss[:, t:t + 1]).then_inc(sq_done, 1)
                sc.wait_ge(sq_done, NT * (n + 1))
                sc.activation(rms[:, :], ss[:, :], ACT.Sqrt, bias=eps[:, 0:1], scale=1.0 / D).then_inc(rms_done, 1)

            def norm_hi(n):
                for t in range(NT):
                    if n % 2:
                        sc.wait_ge(xn_done, NT * n + t + 1)
                        sc.dma_start(xn_d[t * P:(t + 1) * P, :], xn[t % 2][:, :]).then_inc(xn_st[t % 2], 16)
                    for half in range(2):
                        i = 2 * t + half
                        sc.wait_ge(tr_done, 10 * n + i + 1)
                        sc.activation(hT[:, 4 * half:4 * half + 4, t * P:(t + 1) * P], ps[i % 4][:, :].rearrange("p (k c) -> p k c", k=4),
                                      ACT.Copy).then_inc(hi_done, 1)

            def w_hi(L, s):
                S = W_STEPS * L + s
                sc.wait_ge(raw_ld[S % RAW], 16 * (S // RAW + 1))
                if S >= SPL:
                    step_done(sc, S - SPL)
                sc.activation(wh[S % SPL][:, :], raw[S % RAW][:, :], ACT.Copy).then_inc(whi, 1)

            def z_evac(L, g, tiles):
                for t in tiles:
                    m = 5 * g + t
                    sc.wait_ge(zmm, 25 * L + m + 1)
                    dst = unat[:, t, :] if g == 0 else z[:, t, g - 1, :]
                    sc.activation(dst, ps[m % 8][:, :], ACT.Silu if g == 4 else ACT.Copy).then_inc(zfree[m % 8], 1)

            def gu_hi(L, e, s, n):
                X = NE * L + e
                sc.wait_ge(gu_ld[s], used(L, s, n) * 32)
                for p in range(4):
                    if not first(e):
                        sc.wait_ge(gpe, X * 4 + (p - 3))
                    sc.activation(eh[p][:, :], pair(wgu[s], p), ACT.Copy).then_inc(ghi, 1)

            def dn_hi(L, e, s, n):
                X = NE * L + e
                sc.wait_ge(dn_ld[s], used(L, s, n) * 16)
                for k in range(2):
                    if not first(e):
                        sc.wait_ge(dpe, X * 2 + (k - 1))
                    sc.activation(eh[4 + k][:, :], wdn[s][:, k, :], ACT.Copy).then_inc(dhi, 1)

            def rows_hi(L, e):
                for half in range(2):
                    sc.wait_ge(t_mm, NE * L + e + 1)
                    sc.activation(hgTh[:, 4 * half:4 * half + 4, :], ps[1 + half][:, :].rearrange("p (k c) -> p k c", k=4), ACT.Copy).then_inc(hg_hi, 1)

            def y_evac(L, e, s, n):
                sc.wait_ge(dpe, (NE * L + e) * 2 + 2)
                if L or not (isinstance(n, int) and n == 0):
                    sc.wait_ge(y_sc[s], (used(L, s, n) - 1) * 16)
                sc.activation(y[s][:, 0:512], ps[3][:, :], ACT.Copy).then_inc(yA, 1)

            def expert(L, e, s, n):
                X = NE * L + e
                if not first(e):
                    dn_hi(L, e - 1, (s + 2) % 3, n[0])
                if not final(e):
                    gu_hi(L, e + 1, (s + 1) % 3, n[2])
                sc.wait_ge(gpe, X * 4 + 4)
                sc.activation(act[:, :], ps[0][:, 0:F], ACT.Silu).then_inc(silu_done, 1)
                if not final(e):
                    rows_hi(L, e + 1)
                if not first(e):
                    y_evac(L, e - 1, (s + 2) % 3, n[0])
                sc.wait_ge(at_mm, X + 1)
                sc.activation(actTh[:, :, :], ps[5][:, 0:F].rearrange("p (k c) -> p k c", k=2), ACT.Copy).then_inc(at_hi, 1)

            for L in range(NL):
                norm_squares(2 * L)
                norm_hi(2 * L)
                for s in range(WIN_STEPS):
                    w_hi(L, s)
                    if s % KC == 3 and s > KC:
                        z_evac(L, s // KC - 1, (0, 2, 4))
                z_evac(L, 4, range(NT))
                for s in range(WIN_STEPS, WIN_STEPS + SPL):
                    w_hi(L, s)
                sc.wait_ge(small_ld, 128 * (L + 1))
                for g in range(NH):
                    if g or L:
                        sc.wait_ge(d_done, NH * L + g)
                    if g == 0 and L == 0:
                        sc.wait_ge(ready0, 5)
                    sc.wait_ge(ut_done, NH * L + g + 1)
                    A, B = ps[2 * (g % 2)], ps[2 * (g % 2) + 1]
                    samp = uT[:, 16 + SEQ:].rearrange("p (b w) -> p b w", b=DECB)
                    sc.activation(uT[:, 16:16 + SEQ], A[:, :], ACT.Copy).then_inc(uT_done, 1)
                    sc.activation(samp[:, :, 16:24], B[:, 0:NSAMP].rearrange("p (b s) -> p b s", b=DECB), ACT.Copy).then_inc(uT_done, 1)
                    sc.activation(samp[:, :, 1:16], B[:, P:P + DECB * BUF].rearrange("p (b s) -> p b s", b=DECB), ACT.Copy).then_inc(uT_done, 1)
                    sc.wait_ge(yp_done, NH * L + g + 1)
                    sc.activation(hT[:, g, 0:SEQ], ps[4][:, :], ACT.Copy, scale=pscale[:, g:g + 1]).then_inc(phi, 1)
                    sc.activation(hT[:, g, SEQ:TOK], ps[5][:, 0:P], ACT.Copy, scale=pscale[:, g:g + 1]).then_inc(phi, 1)
                sc.wait_ge(upool_st, 32 * (L + 1))
                for t in range(NT):
                    sc.wait_ge(qk_tr, NT * L + t + 1)
                    sc.activation(qT[:, :, :], heads(ps[0][:, :]), ACT.Copy).then_inc(qk_ev, 1)
                    sc.activation(kT[:, :, :], heads(ps[1][:, :]), ACT.Copy).then_inc(qk_ev, 1)
                    if t:
                        o_hi(sc, L, t - 1)
                    if t == LAST:
                        sc.wait_ge(st_ready, LAST * (L + 1))
                        sc.dma_start(o["new_ret_prompt"][L, 0].rearrange("h d e -> d h e"), st[:, :, :]).then_inc(st_st, 16)
                        sc.wait_ge(o_mm, NT * L + NT)
                        sc.activation(scT[:, :, :], heads(ps[6][:, :]), ACT.Copy).then_inc(o_ev, 1)
                    sc.wait_ge(gn_st, NT * L + t + 1)
                    sc.activation(gnrt[:, :], mv[:, :, 1], ACT.Sqrt, bias=eps[:, 1:2], scale=1.0).then_inc(gn_rt, 1)
                o_hi(sc, L, LAST)
                for s in range(WIN_STEPS + SPL, W_STEPS):
                    w_hi(L, s)
                norm_squares(2 * L + 1)
                norm_hi(2 * L + 1)
                gu_hi(L, 0, 0, 0)
                for i in range(2):
                    sc.wait_ge(xn_st[i], 16 * (3, 2)[i] * (L + 1))
                sc.wait_ge(gdone, L + 1)
                sc.activation(gex[:, :, :], gd[:, :, :], ACT.Exp).then_inc(gexp, 1)
                sc.wait_ge(dv_done, L + 1)
                sc.activation(small[:, 5, :], small[:, 4, :], ACT.Exp).then_inc(dvexp, 1)
                rows_hi(L, 0)
                experts(sc, lambda e, s, n: expert(L, e, s, n))
                dn_hi(L, NE - 1, (NE - 1) % 3, (NE - 1) // 3)
                y_evac(L, NE - 1, (NE - 1) % 3, (NE - 1) // 3)
                v = ov[L]
                sc.wait_ge(most_done, L + 1)
                n = sc.value_load(most[0:1, 0:1], min_val=0, max_val=2 * TOK)
                with sc.If(n > P):
                    with sc.Fori(1, (NT - 1) * NE + 1) as i:
                        sc.wait_ge(v["t"], i)
                        for half in range(2):
                            sc.activation(hgT[:, 4 * half:4 * half + 4, :], ps[1 + half][:, :].rearrange("p (k c) -> p k c", k=4), ACT.Copy).then_inc(v["h"], 1)
                        sc.wait_ge(v["gu"], i)
                        sc.activation(act[:, :], ps[0][:, 0:F], ACT.Silu).then_inc(v["s"], 1)
                        sc.wait_ge(v["at"], i)
                        sc.activation(actT[:, :, :], ps[5][:, 0:F].rearrange("p (k c) -> p k c", k=2), ACT.Copy).then_inc(v["aT"], 1)
                        sc.wait_ge(v["d"], i + 1)
                        sc.activation(y[0][:, 0:512], ps[3][:, :], ACT.Copy)
                        sc.activation(y[0][:, 512:D], ps[4][:, :], ACT.Copy).then_inc(v["y"], 1)
                with sc.Else():
                    sc.wait_ge(dpe, 2 * NE * (L + 1))
                sc.wait_ge(dpe, 2 * NE * (L + 1))
            norm_squares(2 * NL)
            for t in range(NT):
                sc.wait_ge(xn_done, NT * 2 * NL + t + 1)
                if t < LAST:
                    sc.dma_start(o["y_prompt"][0, t * P:(t + 1) * P, :], xn[t % 2][:, :]).then_inc(xn_st[t % 2], 16)
                else:
                    sc.dma_start(o["y_sample"].rearrange("b s d -> (b s) d"), xn[t % 2][0:NSAMP, :]).then_inc(xn_st[t % 2], 16)
            for i in range(2):
                sc.wait_ge(xn_st[i], 16 * (3, 2)[i] * (NL + 1))

        def pool_mix(pe, L, g):
            pe.wait_ge(d_done, NH * L + g + 1)
            if g:
                pe.wait_ge(plo, 8 * L + 2 * g)
            pe.matmul(ps[4][:, :], wpool[:, g, :], dT[:, 0:SEQ], start=True, stop=True)
            pe.matmul(ps[5][:, 0:P], wpool[:, g, :], dT[:, SEQ:TOK], start=True, stop=True).then_inc(yp_done, 1)

        def on_t(pe, L, t):
            pe.wait_ge(on_done, NT * L + t + 1)
            if t:
                pe.wait_ge(olo, NT * L + t)
            for h in range(NH):
                last = pe.transpose(ps[7][:, h * P:(h + 1) * P], on[:, h, :], ident)
            last.then_inc(on_tr, 1)

        @block.tensor
        def _(pe):
            def transposes(n):
                pe.wait_ge(cst_ld, 48)
                for t in range(NT):
                    pe.wait_ge(xn_done, NT * n + t + 1)
                    for half in range(2):
                        i = 2 * t + half
                        if i >= 4:
                            pe.wait_ge(lo_done, 10 * n + i - 3)
                        for k in range(4):
                            last = pe.transpose(ps[i % 4][:, k * P:(k + 1) * P], xn[t % 2][:, (4 * half + k) * P:(4 * half + k + 1) * P], ident)
                        last.then_inc(tr_done, 1)

            def three(out, hi_l, lo_l, hi_r, lo_r, first, final):
                pe.matmul(out, hi_l, hi_r, start=first, stop=False)
                pe.matmul(out, hi_l, lo_r, start=False, stop=False)
                return pe.matmul(out, lo_l, hi_r, start=False, stop=final)

            def rows_t(s):
                for k in range(KC):
                    last = pe.transpose(ps[1 + k // 4][:, (k % 4) * P:(k % 4 + 1) * P], hg[s][:, k * P:(k + 1) * P], ident)
                return last

            def act_t():
                for k in range(2):
                    last = pe.transpose(ps[5][:, k * P:(k + 1) * P], act[:, k * P:(k + 1) * P], ident)
                return last

            def expert(L, e, s, n):
                X = NE * L + e
                pe.wait_ge(hg_lo, X * 2 + 2)
                if not first(e):
                    pe.wait_ge(act_done, X)
                for p in range(4):
                    pe.wait_ge(glo, X * 4 + (p + 1))
                    for k in (2 * p, 2 * p + 1):
                        half = slice((k % 2) * PW, (k % 2 + 1) * PW)
                        last = three(ps[0][:, :], hgTh[:, k, :], hgTl[:, k, :], eh[p][:, half], gul[s][:, k, :],
                                     k == 0, k == KC - 1)
                    last.then_inc(gpe, 1)
                if not final(e):
                    q = (s + 1) % 3
                    pe.wait_ge(gat[q], used(L, q, n[2]) * 16)
                    rows_t(q).then_inc(t_mm, 1)
                if not first(e):
                    down(L, e - 1, (s + 2) % 3)
                pe.wait_ge(act_done, X + 1)
                act_t().then_inc(at_mm, 1)

            def down(L, e, s):
                X = NE * L + e
                pe.wait_ge(at_lo, X + 1)
                if not first(e):
                    pe.wait_ge(yA, X)
                    pe.wait_ge(yV, X)
                for k in range(2):
                    pe.wait_ge(dlo, X * 2 + (k + 1))
                    for m in range(2):
                        cols = slice(m * 512, (m + 1) * 512)
                        last = three(ps[3 + m][:, :], actTh[:, k, :], actTl[:, k, :], eh[4 + k][:, cols],
                                     dnl[s][:, k, cols], k == 0, k == 1)
                    last.then_inc(dpe, 1)

            for L in range(NL):
                transposes(2 * L)
                pe.wait_ge(lo_done, 10 * (2 * L + 1))
                for s in range(WIN_STEPS):
                    g, k = divmod(s, KC)
                    S = W_STEPS * L + s
                    pe.wait_ge(wlo, S + 1)
                    for t in range(NT):
                        m = 5 * g + t
                        if k == 0 and m >= 8:
                            z_there(pe, L, (m - 8) // 5, (m - 8) % 5)
                        last = three(ps[m % 8][:, :], hT[:, k, t * P:(t + 1) * P], lT[:, k, t * P:(t + 1) * P],
                                     wh[S % SPL][:, :], wl[S % SPL][:, :], k == 0, k == KC - 1)
                        if k == KC - 1:
                            last.then_inc(zmm, 1)
                    if k < KC - 1:
                        last.then_inc(wpe, 1)
                for g in range(4):
                    for t in range(NT):
                        z_there(pe, L, g + 1, t)
                for t in range(NT):
                    z_there(pe, L, 0, t)
                pe.wait_ge(small_ld, 128 * (L + 1))
                for g in range(NH):
                    A, B = ps[2 * (g % 2)], ps[2 * (g % 2) + 1]
                    if g >= 2:
                        pe.wait_ge(uT_done, 3 * (NH * L + g - 1))
                    for t in range(LAST):
                        pe.transpose(A[:, t * P:(t + 1) * P], unat[:, t, g * P:(g + 1) * P], ident)
                    pe.transpose(B[:, 0:P], unat[:, LAST, g * P:(g + 1) * P], ident)
                    pe.transpose(B[:, P:P + DECB * BUF], cpn[:, g * P:(g + 1) * P], ident[0:DECB * BUF, 0:DECB * BUF]).then_inc(ut_done, 1)
                    if g:
                        pool_mix(pe, L, g - 1)
                pool_mix(pe, L, NH - 1)
                pe.wait_ge(plo, 8 * (L + 1))
                pe.wait_ge(uT_done, 12 * (L + 1))
                for t in range(NT):
                    T = NT * L + t
                    pe.wait_ge(rope, T + 1)
                    if t:
                        pe.wait_ge(qk_ev, 2 * T)
                        pe.wait_ge(qd_done, T)
                    for h in range(NH):
                        pe.transpose(ps[0][:, h * P:(h + 1) * P], zq(t, "q")[:, h * P:(h + 1) * P], ident)
                    for h in range(NH):
                        last = pe.transpose(ps[1][:, h * P:(h + 1) * P], zq(t, "k")[:, h * P:(h + 1) * P], ident)
                    last.then_inc(qk_tr, 1)
                    pe.wait_ge(qk_ev, 2 * T + 2)
                    if t:
                        pe.wait_ge(sc_ev, T)
                    for h in range(NH):
                        last = pe.matmul(ps[2][:, h * P:(h + 1) * P], kT[:, h, :], qT[:, h, :], start=True, stop=True)
                    last.then_inc(sc_mm, 1)
                    if t:
                        on_t(pe, L, t - 1)
                    pe.wait_ge(sc_ev, T + 1)
                    pe.wait_ge(qd_done, T + 1)
                    for tt in (t,):
                        z_there(pe, L, 3, tt)
                    if t < LAST:
                        if t:
                            pe.wait_ge(gn_free, T)
                            pe.wait_ge(st_ready, 4 * L + t)
                        for h in range(NH):
                            out = ps[3][:, h * P:(h + 1) * P]
                            last = pe.matmul(out, scT[:, h, :], zq(t, "v")[:, h * P:(h + 1) * P], start=True, stop=(t == 0))
                            if t:
                                last = pe.matmul(out, qdT[:, h, :], st[:, h, :], start=False, stop=True)
                        last.then_inc(o_mm, 1)
                        pe.wait_ge(kd_done, T + 1)
                        for h in range(NH):
                            last = pe.matmul(ps[4][:, h * P:(h + 1) * P], kd[:, h, :], zq(t, "v")[:, h * P:(h + 1) * P], start=True, stop=True)
                        last.then_inc(kv_mm, 1)
                    else:
                        for h in range(NH):
                            out = ps[6][:, h * P:(h + 1) * P]
                            pe.wait_ge(s0_ld[h % 2], 16 * (2 * L + h // 2 + 1))
                            pe.matmul(out, zq(t, "v")[:, h * P:(h + 1) * P], scT[:, h, :], start=True, stop=False)
                            for b in range(DECB):
                                last = pe.matmul(out[:, b * DECS:(b + 1) * DECS], s0[h % 2][:, b, :], qdT[:, h, b * DECS:(b + 1) * DECS],
                                                 start=False, stop=(b == DECB - 1))
                            if h == NH - 1:
                                last.then_inc(o_mm, 1)
                            pe.wait_ge(vb_done, NH * L + h + 1)
                            if h:
                                pe.wait_ge(s_new, NH * L + h)
                            else:
                                pe.wait_ge(st_ready, 4 * L + 4)
                                pe.wait_ge(kd_done, T + 1)
                            for n in range(2):
                                last = pe.matmul(ps[4 + n][:, :], kd[:, h, :], vb[:, 4 * n:4 * n + 4, :], start=True, stop=True)
                            last.then_inc(skv_mm, 1)
                        pe.wait_ge(o_ev, L + 1)
                        pe.wait_ge(gn_free, T)
                        for h in range(NH):
                            last = pe.transpose(ps[3][:, h * P:(h + 1) * P], scT[:, h, :], ident)
                        last.then_inc(o_back, 1)
                on_t(pe, L, LAST)
                pe.wait_ge(phi, 8 * (L + 1))
                pe.wait_ge(olo, NT * (L + 1))
                pe.wait_ge(s_new, NH * (L + 1))
                for s in range(WIN_STEPS, W_STEPS):
                    n, k = divmod(s - WIN_STEPS, KC)
                    S = W_STEPS * L + s
                    pe.wait_ge(wlo, S + 1)
                    for t in range(NT):
                        m = 5 * n + t
                        if k == 0 and m >= 8:
                            pe.wait_ge(xw, 10 * L + m - 7)
                        last = three(ps[m % 8][:, :], hT[:, k, t * P:(t + 1) * P], lT[:, k, t * P:(t + 1) * P],
                                     wh[S % SPL][:, :], wl[S % SPL][:, :], k == 0, k == KC - 1)
                        if k == KC - 1:
                            last.then_inc(xmm, 1)
                    if k < KC - 1:
                        last.then_inc(wpe, 1)
                transposes(2 * L + 1)
                pe.wait_ge(lo_done, 10 * (2 * L + 2))
                pe.wait_ge(wr_lo, L + 1)
                for t in range(NT):
                    for k in range(KC):
                        last = three(ps[4][:, 32 * t:32 * t + 20], hT[:, k, t * P:(t + 1) * P], lT[:, k, t * P:(t + 1) * P],
                                     wrh[:, k, :], wrl[:, k, :], k == 0, k == KC - 1)
                last.then_inc(lg_mm, 1)
                pe.wait_ge(taken_done, L + 1)
                for t in range(NT):
                    for u in range(t + 1):
                        pe.matmul(ps[5][:, t * NE:(t + 1) * NE], tri[:, 0:P] if u == t else tri[:, P:2 * P], taken[:, u, :],
                                  start=(u == 0), stop=(u == t))
                for u in range(NT):
                    last = pe.matmul(ps[5][:, 96:96 + NE], tri[:, P:2 * P], taken[:, u, :], start=(u == 0), stop=(u == NT - 1))
                last.then_inc(pos_mm, 1)
                pe.wait_ge(gat[0], 16 * used(L, 0, 0))
                rows_t(0).then_inc(t_mm, 1)
                experts(pe, lambda e, s, n: expert(L, e, s, n))
                down(L, NE - 1, (NE - 1) % 3)
                v = ov[L]
                pe.wait_ge(most_done, L + 1)
                n = pe.value_load(most[0:1, 0:1], min_val=0, max_val=2 * TOK)
                with pe.If(n > P):
                    pe.wait_ge(yA, NE * (L + 1))
                    pe.wait_ge(yV, NE * (L + 1))
                    with pe.Fori(1, (NT - 1) * NE + 1) as i:
                        pe.wait_ge(v["g"], 16 * i)
                        rows_t(0).then_inc(v["t"], 1)
                        pe.wait_ge(v["h"], 2 * i)
                        pe.wait_ge(v["ld"], 48 * i)
                        for k in range(KC):
                            last = pe.matmul(ps[0][:, :], hgT[:, k, :], wgu[0][:, k, :], start=(k == 0), stop=(k == KC - 1))
                        last.then_inc(v["gu"], 1)
                        pe.wait_ge(v["a"], i)
                        act_t().then_inc(v["at"], 1)
                        pe.wait_ge(v["aT"], i)
                        for m in range(2):
                            for k in range(2):
                                last = pe.matmul(ps[3 + m][:, :], actT[:, k, :], wdn[0][:, k, m * 512:(m + 1) * 512], start=(k == 0), stop=(k == 1))
                        last.then_inc(v["d"], 1)
                        pe.wait_ge(v["y"], i)
                with pe.Else():
                    pe.wait_ge(yA, NE * (L + 1))
                pe.wait_ge(yV, NE * (L + 1))

        def o_lo(ve, L, t):
            ve.wait_ge(ohi, NT * L + t + 1)
            dst = (slice(None), slice(NH, KC), slice(t * P, (t + 1) * P))
            ve.tensor_tensor(lT[dst], heads(ps[7][:, :]), hT[dst].bitcast(F32), ALU.subtract).then_inc(olo, 1)

        def x_add(ve, L, n, t):
            m = 5 * n + t
            ve.wait_ge(xmm, 10 * L + m + 1)
            v = x[:, t, n * 512:(n + 1) * 512]
            ve.tensor_tensor(v, v, ps[m % 8][:, :], ALU.add).then_inc(xw, 1)

        def routing(ve, L, link, gu_lo):
            def col(i):
                return small[:, i, :]

            def wide(ap, n):
                return ap.unsqueeze(2).to_broadcast([P, NT, n])

            def first_of(vals, best, hot):
                link(ve.tensor_tensor(key[:, :, :], vals, wide(best, 4), ALU.is_ge))
                link(ve.tensor_tensor(key[:, :, :], key[:, :, :], c("rank4", NT), ALU.mult))
                link(ve.tensor_reduce(col(9), key[:, :, :], AX.X, ALU.max))
                link(ve.tensor_tensor(hot, key[:, :, :], wide(col(9), 4), ALU.is_equal))

            ve.wait_ge(lg_mm, L + 1)
            link(ve.tensor_tensor(lg[:, :, :], ps[4][:, 0:32 * NT].rearrange("p (t n) -> p t n", t=NT)[:, :, 0:20],
                                  over(rbias[:, :], NT), ALU.add))
            G = lg[:, :, 0:4]
            link(ve.tensor_reduce(col(0), G, AX.X, ALU.max))
            ve.tensor_tensor(gd[:, :, :], G, wide(col(0), 4), ALU.subtract).then_inc(gdone, 1)
            first_of(G, col(0), ohg[:, :, :])
            link(ve.tensor_tensor(prod[:, :, :, :], lg[:, :, 4:20].rearrange("p t (g j) -> p t g j", g=NG),
                                  ohg[:, :, :].unsqueeze(3).to_broadcast([P, NT, NG, EPG]), ALU.mult))
            link(ve.tensor_reduce(ing[:, :, :], prod[:, :, :, :].rearrange("p t g j -> p t j g"), AX.X, ALU.add))
            link(ve.tensor_reduce(col(1), ing[:, :, :], AX.X, ALU.max))
            first_of(ing[:, :, :], col(1), oh[0][:, :, :])
            link(ve.scalar_tensor_tensor(out=ing[:, :, :], in0=oh[0][:, :, :], scalar=-3.0e38, in1=ing[:, :, :], op0=ALU.mult, op1=ALU.add))
            link(ve.tensor_reduce(col(2), ing[:, :, :], AX.X, ALU.max))
            ve.tensor_tensor(col(4), col(2), col(1), ALU.subtract).then_inc(dv_done, 1)
            first_of(ing[:, :, :], col(2), oh[1][:, :, :])
            for k in range(2):
                last = ve.tensor_tensor(both[k][:, :, :].rearrange("p t (g j) -> p t g j", g=NG),
                                        ohg[:, :, :].unsqueeze(3).to_broadcast([P, NT, NG, EPG]),
                                        over(oh[k][:, :, :], NG, 2), ALU.mult)
            link(last)
            link(ve.tensor_tensor(picked[:, :, :], both[0][:, :, :], both[1][:, :, :], ALU.add))
            ve.tensor_tensor(taken[:, :, :], picked[:, :, :], wide(c("valid"), NE), ALU.mult).then_inc(taken_done, 1)
            ve.wait_ge(gexp, L + 1)
            link(ve.tensor_reduce(col(6), gex[:, :, :], AX.X, ALU.add))
            ve.wait_ge(dvexp, L + 1)
            link(ve.tensor_scalar(col(7), col(5), 1.0, None, ALU.add))
            link(ve.tensor_tensor(col(8), col(6), col(7), ALU.mult))
            link(ve.reciprocal(pgate[:, 0, :], col(8)))
            link(ve.tensor_tensor(pgate[:, 1, :], pgate[:, 0, :], col(5), ALU.mult))
            ve.wait_ge(pos_mm, L + 1)
            link(ve.scalar_tensor_tensor(out=where[:, :], in0=ps[5][:, 0:NT * NE], scalar=float(NE), in1=c("iota"), op0=ALU.mult, op1=ALU.add))
            for k in range(2):
                link(ve.tensor_tensor(picked[:, :, :], both[k][:, :, :], where[:, :].rearrange("p (t e) -> p t e", t=NT), ALU.mult))
                link(ve.tensor_reduce(col(10 + k), picked[:, :, :], AX.X, ALU.add))
                last = ve.tensor_tensor(slot_u[:, k, :], col(10 + k), c("drop"), ALU.add)
            last.then_inc(slots_done, 1)
            link(ve.tensor_reduce(most_f[:, :], ps[5][:, 96:96 + NE], AX.X, ALU.max))
            ve.tensor_copy(most[:, :], most_f[:, :]).then_inc(most_done, 1)
            gu_lo(L, 0, 0)
            ve.wait_ge(idx_ld, 16 * (L + 1))
            link(ve.tensor_scalar(tmpf[:, :], pidx[:, :], float(TOK), -float(TOK), ALU.is_ge, ALU.mult))
            ve.tensor_tensor(tidx[:, :], tmpf[:, :], pidx[:, :], ALU.add).then_inc(tidx_done, 1)

        @block.vector
        def _(ve):
            chain = [0]

            def link(ins):
                chain[0] += 1
                ins.then_inc(dve_chain, 1)
                ve.wait_ge(dve_chain, chain[0])

            def norm_rows(n, lo=True):
                ve.wait_ge(rms_done, n + 1)
                link(ve.reciprocal(rstd[:, :], rms[:, :]))
                ve.wait_ge(gain_ld, 16 * (n + 1))
                for t in range(NT):
                    if t >= 2:
                        if lo:
                            ve.wait_ge(tr_done, 10 * n + 2 * (t - 1))
                        if n % 2 or not lo:
                            ve.wait_ge(xn_st[t % 2], 16 * ((3, 2)[t % 2] * (n // 2) + t // 2))
                    ve.scalar_tensor_tensor(out=xn[t % 2][:, :], in0=x[:, t, :], scalar=rstd[:, t:t + 1], in1=gain[:, :],
                                            op0=ALU.mult, op1=ALU.mult).then_inc(xn_done, 1)
                    if lo and t:
                        norm_lo(n, t - 1)
                if lo:
                    norm_lo(n, LAST)

            def norm_lo(n, t):
                for half in range(2):
                    i = 2 * t + half
                    ve.wait_ge(hi_done, 10 * n + i + 1)
                    dst = (slice(None), slice(4 * half, 4 * half + 4), slice(t * P, (t + 1) * P))
                    ve.tensor_tensor(lT[dst], ps[i % 4][:, :].rearrange("p (k c) -> p k c", k=4), hT[dst].bitcast(F32),
                                     ALU.subtract).then_inc(lo_done, 1)

            def w_lo(L, s):
                S = W_STEPS * L + s
                ve.wait_ge(whi, S + 1)
                ve.tensor_tensor(wl[S % SPL][:, :], raw[S % RAW][:, :], wh[S % SPL][:, :].bitcast(F32), ALU.subtract).then_inc(wlo, 1)

            def gu_lo(L, e, s):
                for p in range(4):
                    ve.wait_ge(ghi, (NE * L + e) * 4 + (p + 1))
                    ve.tensor_tensor(pair(gul[s], p), pair(wgu[s], p), eh[p][:, :].bitcast(F32), ALU.subtract).then_inc(glo, 1)

            def dn_lo(L, e, s):
                for k in range(2):
                    ve.wait_ge(dhi, (NE * L + e) * 2 + (k + 1))
                    ve.tensor_tensor(dnl[s][:, k, :], wdn[s][:, k, :], eh[4 + k][:, :].bitcast(F32), ALU.subtract).then_inc(dlo, 1)

            def rows_lo(L, e):
                for half in range(2):
                    ve.wait_ge(hg_hi, (NE * L + e) * 2 + (half + 1))
                    ks = slice(4 * half, 4 * half + 4)
                    ve.tensor_tensor(hgTl[:, ks, :], ps[1 + half][:, :].rearrange("p (k c) -> p k c", k=4), hgTh[:, ks, :].bitcast(F32),
                                     ALU.subtract).then_inc(hg_lo, 1)

            def y_evac(L, e, s, n):
                ve.wait_ge(dpe, (NE * L + e) * 2 + 2)
                if L or not (isinstance(n, int) and n == 0):
                    ve.wait_ge(y_sc[s], (used(L, s, n) - 1) * 16)
                ve.tensor_copy(y[s][:, 512:D], ps[4][:, :]).then_inc(yV, 1)

            def expert(L, e, s, n):
                X = NE * L + e
                if not first(e):
                    dn_lo(L, e - 1, (s + 2) % 3)
                if not final(e):
                    gu_lo(L, e + 1, (s + 1) % 3)
                ve.wait_ge(silu_done, X + 1)
                ve.tensor_tensor(act[:, :], act[:, :], ps[0][:, F:2 * F], ALU.mult).then_inc(act_done, 1)
                if not final(e):
                    rows_lo(L, e + 1)
                if not first(e):
                    y_evac(L, e - 1, (s + 2) % 3, n[0])
                ve.wait_ge(at_hi, X + 1)
                ve.tensor_tensor(actTl[:, :, :], ps[5][:, 0:F].rearrange("p (k c) -> p k c", k=2), actTh[:, :, :].bitcast(F32),
                                 ALU.subtract).then_inc(at_lo, 1)

            ve.memset(x[NSAMP:P, LAST, :], 0.0).then_inc(ready0, 1)
            for L in range(NL):
                if L == 0:
                    ve.wait_ge(cst_ld, 48)
                    ve.wait_ge(ready0, 5)
                norm_rows(2 * L)
                for s in range(WIN_STEPS):
                    w_lo(L, s)
                    if s % KC == 3 and s > KC:
                        g = s // KC - 1
                        for t in (1, 3):
                            m = 5 * g + t
                            ve.wait_ge(zmm, 25 * L + m + 1)
                            dst = unat[:, t, :] if g == 0 else z[:, t, g - 1, :]
                            ve.tensor_copy(dst, ps[m % 8][:, :]).then_inc(zfree[m % 8], 1)
                for s in range(WIN_STEPS, WIN_STEPS + SPL):
                    w_lo(L, s)
                ve.wait_ge(small_ld, 128 * (L + 1))
                link(ve.tensor_copy(wrh[:, :, :], wr[:, :, :]))
                ve.tensor_tensor(wrl[:, :, :], wr[:, :, :], wrh[:, :, :].bitcast(F32), ALU.subtract).then_inc(wr_lo, 1)
                w = 0
                for g in range(NH):
                    w += g + 1
                    ve.wait_ge(win_done, 10 * L + w)
                    if g or L:
                        ve.wait_ge(yp_done, NH * L + g)
                    win = (winA, winB)[g % 2]
                    inv = 1.0 / (2 << g)
                    link(ve.tensor_tensor(edge[:, :], win[:, 16:32], c("inv", NH)[:, g, :], ALU.mult))
                    ve.tensor_tensor(dT[:, 0:16], edge[:, :], uT[:, 16:32], ALU.subtract)
                    ve.scalar_tensor_tensor(out=dT[:, 16:SEQ], in0=win[:, 32:16 + SEQ], scalar=inv, in1=uT[:, 32:16 + SEQ],
                                            op0=ALU.mult, op1=ALU.subtract)
                    ws = win[:, 16 + SEQ:].rearrange("p (b w) -> p b w", b=DECB)[:, :, 16:24]
                    us = uT[:, 16 + SEQ:].rearrange("p (b w) -> p b w", b=DECB)[:, :, 16:24]
                    ve.scalar_tensor_tensor(out=dT[:, SEQ:SEQ + NSAMP].rearrange("p (b s) -> p b s", b=DECB), in0=ws, scalar=inv, in1=us,
                                            op0=ALU.mult, op1=ALU.subtract).then_inc(d_done, 1)
                    ve.wait_ge(phi, 8 * L + 2 * g + 1)
                    ve.scalar_tensor_tensor(out=lT[:, g, 0:SEQ], in0=ps[4][:, :], scalar=pscale[:, g:g + 1], in1=hT[:, g, 0:SEQ].bitcast(F32),
                                            op0=ALU.mult, op1=ALU.subtract).then_inc(plo, 1)
                    ve.wait_ge(phi, 8 * L + 2 * g + 2)
                    ve.scalar_tensor_tensor(out=lT[:, g, SEQ:TOK], in0=ps[5][:, 0:P], scalar=pscale[:, g:g + 1], in1=hT[:, g, SEQ:TOK].bitcast(F32),
                                            op0=ALU.mult, op1=ALU.subtract).then_inc(plo, 1)
                for t in range(NT):
                    z_there(ve, L, 4, t)
                    last = ve.tensor_tensor(z[:, t, 3, :], z[:, t, 3, :], gnrow[:, :], ALU.mult)
                last.then_inc(sg_done, 1)
                ve.wait_ge(sg_done, L + 1)
                ve.wait_ge(upool_st, 32 * (L + 1))
                for t in range(NT):
                    T = NT * L + t
                    kind = 1 if t == LAST else 0
                    ve.wait_ge(rope, T + 1)
                    if 1 <= t:
                        ve.wait_ge(kv_mm, 4 * L + t)
                    ve.tensor_tensor(kd[:, :, :], heads(zq(t, "k")), c("kdec", 2)[:, kind, :].unsqueeze(2).to_broadcast([P, NH, P]),
                                     ALU.mult).then_inc(kd_done, 1)
                    ve.wait_ge(qk_ev, 2 * T + 1)
                    if t:
                        ve.wait_ge(o_mm, T)
                    ve.tensor_tensor(qdT[:, :, :], heads(ps[0][:, :]), c("qdec", 2, NH)[:, kind, :, :], ALU.mult).then_inc(qd_done, 1)
                    if t:
                        o_lo(ve, L, t - 1)
                    ve.wait_ge(sc_mm, T + 1)
                    ve.tensor_tensor(scT[:, :, :], heads(ps[2][:, :]), c("decay", 2, NH)[:, kind, :, :], ALU.mult).then_inc(sc_ev, 1)
                    if t < LAST:
                        ve.wait_ge(kv_mm, 4 * L + t + 1)
                        if t == 0 and L:
                            ve.wait_ge(st_st, 16 * L)
                        for h in range(NH):
                            if t == 0:
                                last = ve.tensor_copy(st[:, h, :], ps[4][:, h * P:(h + 1) * P])
                            else:
                                last = ve.scalar_tensor_tensor(out=st[:, h, :], in0=st[:, h, :], scalar=float(chunk_decay[0][h]),
                                                               in1=ps[4][:, h * P:(h + 1) * P], op0=ALU.mult, op1=ALU.add)
                        last.then_inc(st_ready, 1)
                        ve.wait_ge(st_ready, 4 * L + t + 1)
                    else:
                        for h in range(NH):
                            if h:
                                ve.wait_ge(skv_mm, NH * L + h)
                            ve.tensor_tensor(vb[:, :, :], over(zq(t, "v")[:, h * P:(h + 1) * P], DECB),
                                             c("seqm").unsqueeze(2).to_broadcast([P, DECB, P]), ALU.mult).then_inc(vb_done, 1)
                            ve.wait_ge(skv_mm, NH * L + h + 1)
                            for n in range(2):
                                v = s0[h % 2][:, 4 * n:4 * n + 4, :]
                                last = ve.scalar_tensor_tensor(out=v, in0=v, scalar=float(chunk_decay[1][h]),
                                                               in1=ps[4 + n][:, :].rearrange("p (b e) -> p b e", b=4), op0=ALU.mult, op1=ALU.add)
                            last.then_inc(s_new, 1)
                        ve.wait_ge(o_back, L + 1)
                    ve.wait_ge(o_mm, T + 1)
                    for h in range(NH):
                        last = ve.bn_stats(bnst[:, h, :], ps[3][:, h * P:(h + 1) * P])
                    link(last)
                    for h in range(NH):
                        last = ve.bn_aggr(mv[:, h, :], bnst[:, h, :])
                    last.then_inc(gn_st, 1)
                    ve.wait_ge(gn_rt, T + 1)
                    link(ve.reciprocal(gnrs[:, :], gnrt[:, :]))
                    if t:
                        ve.wait_ge(on_tr, T)
                    for h in range(NH):
                        last = ve.tensor_scalar(on[:, h, :], ps[3][:, h * P:(h + 1) * P], mv[:, h, 0:1], gnrs[:, h:h + 1], ALU.subtract, ALU.mult)
                    last.then_inc(gn_free, 1)
                    ve.wait_ge(gn_free, T + 1)
                    ve.tensor_tensor(on[:, :, :], on[:, :, :], heads(zq(t, "g")), ALU.mult).then_inc(on_done, 1)
                o_lo(ve, L, LAST)
                for s in range(WIN_STEPS + SPL, W_STEPS):
                    w_lo(L, s)
                    if s == WIN_STEPS + KC + 3:
                        for t in range(NT):
                            x_add(ve, L, 0, t)
                for t in range(NT):
                    x_add(ve, L, 1, t)
                norm_rows(2 * L + 1)
                routing(ve, L, link, gu_lo)
                rows_lo(L, 0)
                experts(ve, lambda e, s, n: expert(L, e, s, n))
                dn_lo(L, NE - 1, (NE - 1) % 3)
                y_evac(L, NE - 1, (NE - 1) % 3, (NE - 1) // 3)
                v = ov[L]
                ve.wait_ge(most_done, L + 1)
                n = ve.value_load(most[0:1, 0:1], min_val=0, max_val=2 * TOK)
                with ve.If(n > P):
                    with ve.Fori(1, (NT - 1) * NE + 1) as i:
                        ve.wait_ge(v["s"], i)
                        ve.tensor_tensor(act[:, :], act[:, :], ps[0][:, F:2 * F], ALU.mult).then_inc(v["a"], 1)
                with ve.Else():
                    ve.wait_ge(dpe, 2 * NE * (L + 1))
                for i in range(2 * NT):
                    k, t = divmod(i, NT)
                    n = P if t < LAST else NSAMP
                    per = 2 if i % 9 == 0 else 1
                    ve.wait_ge(comb_ld[i % 9], 16 * (per * L + i // 9 + 1))
                    if k:
                        ve.wait_ge(comb, 10 * L + t + 1)
                    ve.scalar_tensor_tensor(out=x[0:n, t, :], in0=back[i % 9][0:n, :], scalar=pgate[0:n, k, t:t + 1], in1=x[0:n, t, :],
                                            op0=ALU.mult, op1=ALU.add).then_inc(comb, 1)
            norm_rows(2 * NL, lo=False)



_INS = ["x_prompt", "x_sample", "cache_pool", "state_ret", "norm_mix", "w_in", "w_pool", "pool_scale", "ret_gn", "w_out",
        "norm_ffn", "w_router_group", "b_router_group", "w_router_expert", "b_router_expert", "w_gate", "w_up", "w_down",
        "norm_final"]
_OUTS = [("y_prompt", (1, SEQ, D)), ("y_sample", (DECB, DECS, D)), ("new_pool_prompt", (NL, 1, BUF, PW)),
         ("new_ret_prompt", (NL, 1, NH, P, P)), ("new_pool_sample", (NL, DECB, BUF, PW)), ("new_ret_sample", (NL, DECB, NH, P, P))]


def kernel(**inputs):
    import concourse.bacc as bacc
    from concourse.bass_utils import run_bass_kernel_spmd as run
    import ml_dtypes

    nc = bacc.Bacc("TRN2", target_bir_lowering=False, num_devices=1)
    arrays, aps = {}, {}
    _, cst, tri, ints, _ = constant_tables()
    host = {k: np.ascontiguousarray(inputs[k]) for k in _INS}
    host.update(cst=cst, tri=tri.astype(ml_dtypes.bfloat16), ints=ints)
    for k, v in host.items():
        arrays[f"in_{k}"] = v
        aps[k] = nc.dram_tensor(f"in_{k}", v.shape, mybir.dt.from_np(v.dtype), kind="ExternalInput").ap()
    outs = {k: nc.dram_tensor(f"out_{k}", s, F32, kind="ExternalOutput").ap() for k, s in _OUTS}
    build(nc, aps, outs)
    r = run(nc, [arrays], core_ids=[0])
    return tuple(r.results[0][f"out_{k}"] for k, _ in _OUTS)
```

```python
from contextlib import ExitStack

import numpy as np

import concourse.bass as bass
from concourse import mybir

ALU = mybir.AluOpType
ACT = mybir.ActivationFunctionType
AX = mybir.AxisListType
F32 = mybir.dt.float32
F32R = mybir.dt.float32r
BF16 = mybir.dt.bfloat16
I32 = mybir.dt.int32
U32 = mybir.dt.uint32

P = 128
D = 1024
SEQ, DECB, DECS, PAST = 512, 8, 8, 4096
NL = 2
KC = D // P
NT = 5
LAST = NT - 1
NSAMP = DECB * DECS
TOK = NT * P
PW = 512
NH = 4
HALF = 64
BUF = 15
NE, NG, EPG = 16, 4, 4
F = 256
UW = 16 + SEQ + DECB * 24
WIN_STEPS, WOUT_STEPS = 5 * KC, 2 * KC
W_STEPS = WIN_STEPS + WOUT_STEPS
ZB = 6
RAW, SPL = 3, 4
LOOP0, LOOP1 = 5, 14
AHEAD = 3
EPS_RMS, EPS_GN = 1e-6, 1e-5
OUT_OF_RANGE = 1000000.0


def constant_tables():
    f = np.float32
    p = np.arange(P)
    pos = np.zeros((P, NT), f)
    for t in range(LAST):
        pos[:, t] = t * P + p
    pos[:, LAST] = PAST + p % DECS
    inv = f(10000.0) ** (-(np.arange(HALF, dtype=f)) / f(HALF))
    ang = (pos[:, :, None] * inv.astype(f)[None, None, :]).astype(f)
    log_g = np.log(f(1.0) - f(2.0) ** (-5.0 - np.arange(NH, dtype=f))).astype(f)
    scale = f(P) ** f(-0.5)

    def decay(chunk):
        i, j = p[None, :], p[:, None]
        same = (i // chunk == j // chunk) & (i >= j)
        e = np.exp(np.maximum(i - j, 0).astype(f)[:, None, :] * log_g[None, :, None])
        return np.where(same[:, None, :], e, 0).astype(f) * scale

    def qdecay(chunk):
        row = np.exp(((p % chunk) + 1.0).astype(f)[None, :] * log_g[:, None])
        return np.broadcast_to(row[None], (P, NH, P))

    def kdecay(chunk):
        return np.exp((chunk - 1.0 - (p % chunk)).astype(f)[:, None] * log_g[None]) * scale

    invc = np.zeros((NH, 16), f)
    for g, w in enumerate((2, 4, 8, 16)):
        invc[g] = 1.0 / np.minimum(w, np.arange(16) + 1)
    seq_mask = (p[:, None] // DECS == np.arange(DECB)[None]) & (p[:, None] < NSAMP)
    valid = np.ones((P, NT), f)
    valid[NSAMP:, LAST] = 0
    parts = {
        "ident": np.eye(P),
        "cos": np.cos(ang), "sin": np.sin(ang), "nsin": -np.sin(ang),
        "decay": np.stack([decay(P), decay(DECS)], 1),
        "qdec": np.stack([qdecay(P), qdecay(DECS)], 1),
        "kdec": np.stack([kdecay(P), kdecay(DECS)], 1),
        "seqm": seq_mask, "inv": np.broadcast_to(invc[None], (P, NH, 16)),
        "rank4": np.broadcast_to(np.array([4, 3, 2, 1], f), (P, NT, 4)),
        "before": np.broadcast_to(np.arange(P, dtype=f) - P, (P, P)),
        "turn": np.broadcast_to(np.arange(NT, dtype=f) * P, (P, 2 * NT, NT)),
        "nth": np.broadcast_to(np.arange(NT, dtype=f) + 1, (P, 2 * NT, NT)),
        "pair": np.stack([np.broadcast_to(p[:, None], (P, 2 * NT)), np.broadcast_to(np.arange(2 * NT) + 1, (P, 2 * NT))], 2)
        * np.tile(valid, 2)[:, :, None],
        "valid": valid,
    }
    at, cols, n = {}, [], 0
    for k, a in parts.items():
        a = np.asarray(a, f).reshape(P, -1)
        at[k] = (n, n + a.shape[1])
        n += a.shape[1]
        cols.append(a)
    tri = np.concatenate([(p[:, None] < p[None, :]), np.ones((P, P))], 1)
    chunk = np.exp(f(P) * log_g), np.exp(f(DECS) * log_g)
    return at, np.concatenate(cols, 1).astype(f), tri.astype(f), chunk


def build(nc, a, o):
    at, _, _, chunk_decay = constant_tables()
    ncst = max(v[1] for v in at.values())
    ctx = ExitStack()
    with ctx:
        top = [((nc.sbuf_base + 63) // 64) * 64]

        def place(nbytes):
            off = top[0]
            top[0] += (nbytes + 31) // 32 * 32
            assert top[0] <= nc.SBUF_PARTITION_SIZE_BYTES, top[0]
            return off

        def tile(name, shape, dt=F32, off=None):
            size = int(np.prod(shape[1:])) * (2 if dt == BF16 else 4)
            return nc.alloc_sbuf_tensor_at(name, shape, dt, offset=place(size) if off is None else off)

        cst = tile("cst", [P, ncst])
        tri = tile("tri", [P, 2 * P], BF16)
        x = tile("x", [P, NT, D])
        gain = tile("gain", [P, D])
        wpool = tile("wpool", [P, NH, P])
        pscale = tile("pscale", [P, NH])
        gn_at = place(4096)
        gnrow = tile("gnrow", [P, PW], off=gn_at)
        cpn = tile("cpn", [DECB * BUF, PW], off=gn_at + 2048)
        wr = tile("wr", [P, KC, 20])
        wrs = tile("wrs", [P, KC, 40], F32R)
        rbias = tile("rbias", [P, 20])
        wring = place(4096 * SPL)
        wh = [tile(f"wh{i}", [P, PW], F32R, off=wring + 2048 * i) for i in range(SPL)]
        wl = [tile(f"wl{i}", [P, PW], F32R, off=wring + 2048 * (SPL + i)) for i in range(SPL)]
        e0 = place(24 * 1024)
        shared = place(48 * 1024)
        slot_at = [e0, shared, shared + 24 * 1024]
        wgu = [tile(f"wgu{s}", [P, KC, 2 * F], off=slot_at[s]) for s in range(3)]
        wdn = [tile(f"wdn{s}", [P, 2, D], off=slot_at[s] + 16 * 1024) for s in range(3)]
        gul = [tile(f"gul{s}", [P, KC, 2 * F], F32R, off=slot_at[s]) for s in range(3)]
        dnl = [tile(f"dnl{s}", [P, 2, D], F32R, off=slot_at[s] + 16 * 1024) for s in range(3)]
        z = tile("z", [P, NT, 4, PW], off=shared)
        raw = [tile(f"raw{i}", [P, PW], off=shared + 40 * 1024 + 2048 * i) for i in range(RAW)]
        region = place(40 * 1024)
        hT = tile("hT", [P, KC, TOK], F32R, off=region)
        lT = tile("lT", [P, KC, TOK], F32R, off=region + 20 * 1024)
        hg = [tile(f"hg{i}", [P, D], off=region + 4096 * i) for i in range(3)]
        y = [tile(f"y{i}", [P, D], off=region + 4096 * (3 + i)) for i in range(3)]
        hgTh = tile("hgTh", [P, KC, P], F32R, off=region + 4096 * 6)
        hgTl = tile("hgTl", [P, KC, P], F32R, off=region + 4096 * 7)
        act = tile("act", [P, F], off=region + 4096 * 9)
        actTh = tile("actTh", [P, 2, P], F32R, off=region + 4096 * 9 + 1024)
        actTl = tile("actTl", [P, 2, P], F32R, off=region + 4096 * 9 + 2048)
        pidx = tile("pidx", [P, NT * NE], U32, off=region + 4096 * 9 + 3072)
        tidx = tile("tidx", [P, NT * NE], U32, off=region + 4096 * 9 + 3072 + 320)
        tmpf = tile("tmpf", [P, NT * NE], off=region + 4096 * 9 + 3072 + 640)
        tab = region + 4096 * 3
        atslot = tile("atslot", [P, 2 * NT, P], BF16, off=tab)
        spread = tile("spread", [P, 2 * NT, NT * 2 * NE], BF16, off=tab + 2560)
        named = tile("named", [P, 2 * NT, 2 * NE], off=tab + 5760)
        place_of = tile("place_of", [P, 2 * NT], off=tab + 7040)
        turn1 = tile("turn1", [P, 2 * NT], off=tab + 7104)
        in_turn = tile("in_turn", [P, 2 * NT], off=tab + 7168)
        reached = tile("reached", [P, 2 * NT, NT], off=tab + 7232)
        hotturn = tile("hotturn", [P, 2 * NT, NT], off=tab + 7456)
        small_tab = tile("small_tab", [P, NT * NE], off=tab + 7680)
        hgT = tile("hgT", [P, KC, P], off=region + 4096 * 6)
        actT = tile("actT", [P, 2, P], off=region + 4096 * 9 + 1024)
        back = [tile(f"back{i}", [P, D], off=shared + 4096 * i) for i in range(2 * NT)]
        r12 = place(12 * 1024)
        eh = [tile(f"eh{i}", [P, 2 * PW], F32R, off=wring + 4096 * i if i < 4 else r12 + 4096 * (i - 4)) for i in range(6)]
        unat = tile("unat", [P, NT, PW], off=r12)
        def twice(name, i, at1):
            return [tile(f"{name}0", [P, NH, P], off=r12 + 2048 * i), tile(f"{name}1", [P, NH, P], off=region + at1)]

        qT = twice("qT", 0, 8 * 1024)
        kT, qdT, scT, kd, on = (twice(name, 1 + i, 20 * 1024 + 2048 * i) for i, name in enumerate(("kT", "qdT", "scT", "kd", "on")))
        rt = [r12 + 8192]

        def route(name, shape, dt=F32):
            off = rt[0]
            rt[0] += (int(np.prod(shape[1:])) * (2 if dt == BF16 else 4) + 31) // 32 * 32
            assert rt[0] <= r12 + 12 * 1024
            return tile(name, shape, dt, off)

        lg = route("lg", [P, NT, 20])
        gd = route("gd", [P, NT, 4])
        gex = route("gex", [P, NT, 4])
        key = route("key", [P, NT, 4])
        ohg = route("ohg", [P, NT, 4])
        prod = route("prod", [P, NT, NG, EPG])
        ing = route("ing", [P, NT, EPG])
        oh = [route(f"oh{k}", [P, NT, EPG]) for k in range(2)]
        both = route("both", [P, 2, NT, NE])
        taken = route("taken", [P, NT, NE], BF16)
        picked = route("picked", [P, 2, NT, NE])
        small = route("small", [P, 16, NT])
        pgate = tile("pgate", [P, 2, NT])
        gidx = tile("gidx", [P, 1], U32)
        sidx = tile("sidx", [P, 1], U32)
        most_f = tile("most_f", [P, 1])
        most = tile("most", [P, 1], I32)
        ss = tile("ss", [P, NT])
        rms = tile("rms", [P, NT])
        rstd = tile("rstd", [P, NT])
        bnst = tile("bnst", [P, NH, 6])
        mv = tile("mv", [P, NH, 2])
        gnrt = tile("gnrt", [P, NH])
        gnrs = tile("gnrs", [P, NH])
        eps = tile("eps", [P, 2])
        warm = tile("warm", [P, 1])
        s0_at = [place(4096) for i in range(2)]
        s0 = [tile(f"s0{h}", [P, DECB, P], off=(s0_at + [region, region + 4096])[h]) for h in range(NH)]
        st = tile("st", [P, NH, P])
        d_at = place(4 * (TOK + 16 + 2 * UW))
        xn = [[tile(f"xm{t}", [P, D], off=e0 + 4096 * t) for t in range(NT)],
              [tile(f"xf{t}", [P, D], off=(r12, r12 + 4096, d_at, s0_at[0], s0_at[1])[t]) for t in range(NT)]]
        hP = tile("hP", [P, NH, TOK], F32R, off=e0)
        lP = tile("lP", [P, NH, TOK], F32R, off=e0 + 10 * 1024)
        uT = tile("uT", [P, UW])
        dT = tile("dT", [P, TOK], off=d_at)
        edge = tile("edge", [P, 16], off=d_at + 4 * TOK)
        wa = d_at + 4 * (TOK + 16)
        winA = tile("winA", [P, UW], off=wa)
        winB = tile("winB", [P, UW], off=wa + UW * 4)
        ropA = tile("ropA", [P, NH, 2, HALF], off=wa)
        ropB = tile("ropB", [P, NH, 2, HALF], off=wa + 2048)
        lgT = tile("lgT", [P, TOK], off=d_at + 4096 + 64)
        vb = [tile(f"vb{i}", [P, DECB, P], off=(wa, e0 + 20 * 1024)[i]) for i in range(2)]

        gu3_at, dn3_at = (s0_at[0], d_at), (gn_at, region + 4096 * 8)
        wgu3 = [tile(f"wgu3_{h}", [P, KC // 2, 2 * F], off=gu3_at[h]) for h in range(2)]
        gul3 = [tile(f"gul3_{h}", [P, KC // 2, 2 * F], F32R, off=gu3_at[h]) for h in range(2)]
        wdn3 = [tile(f"wdn3_{k}", [P, D], off=dn3_at[k]) for k in range(2)]
        dnl3 = [tile(f"dnl3_{k}", [P, D], F32R, off=dn3_at[k]) for k in range(2)]

        ps = [ctx.enter_context(nc.psum_tensor(f"ps{i}", [P, 512], F32)) for i in range(8)]
        xn_d = nc.dram_tensor("xn_d", (TOK, D), F32).ap()
        y_d = nc.dram_tensor("y_d", (2 * TOK, D), F32).ap()

        def sem(name):
            return ctx.enter_context(nc.semaphore(name))

        ident_ld = sem("ident_ld"); cst_ld = sem("cst_ld"); row_ld = [sem(f"row_ld{t}") for t in range(NT)]; gain_ld = sem("gain_ld")
        small_ld = sem("small_ld"); raw_ld = [sem(f"raw_ld{i}") for i in range(RAW)]
        s0_ld = [sem(f"s0_ld{h}") for h in range(NH)]; gu_ld = [[sem(f"gu_ld{s}_{h}") for h in range(2)] for s in range(3)]
        dn_ld = [[sem(f"dn_ld{s}_{k}") for k in range(2)] for s in range(3)]
        gu3_ld = [sem(f"gu3_ld{h}") for h in range(2)]; dn3_ld = [sem(f"dn3_ld{k}") for k in range(2)]
        gat = [sem(f"gat{i}") for i in range(3)]
        second_ld = sem("second_ld")
        xn_st = [sem(f"xn_st{t}") for t in range(NT)]; upool_st = sem("upool_st"); st_st = sem("st_st")
        s0_st = [sem(f"s0_st{h}") for h in range(NH)]; y_sc = [sem(f"y_sc{i}") for i in range(3)]
        out_st = sem("out_st")
        ready0 = sem("ready0"); sq_done = sem("sq_done"); rms_done = sem("rms_done"); xn_done = sem("xn_done")
        tr_done = sem("tr_done"); hi_done = sem("hi_done"); lo_done = sem("lo_done")
        whi = sem("whi"); wlo = sem("wlo"); wpe = sem("wpe"); zmm = sem("zmm")
        zfree = [sem(f"zfree{i}") for i in range(ZB)]
        xmm = sem("xmm"); xw = sem("xw"); sg_done = sem("sg_done")
        ut_done = sem("ut_done"); uT_done = sem("uT_done"); win_done = sem("win_done"); d_done = sem("d_done")
        yp_done = sem("yp_done"); phi = sem("phi"); plo = sem("plo")
        rope = sem("rope"); kd_done = sem("kd_done"); qk_tr = sem("qk_tr"); qk_ev = sem("qk_ev"); qd_done = sem("qd_done")
        sc_mm = sem("sc_mm"); sc_ev = sem("sc_ev"); o_mm = sem("o_mm"); kv_mm = sem("kv_mm");         st_ready = sem("st_ready"); o_ev = sem("o_ev"); o_back = sem("o_back"); gn_st = sem("gn_st"); gn_rt = sem("gn_rt")
        gn_free = sem("gn_free"); on_done = sem("on_done"); on_tr = sem("on_tr"); ohi = sem("ohi"); olo = sem("olo")
        vb_done = sem("vb_done"); skv_mm = sem("skv_mm"); s_new = sem("s_new")
        wr_lo = sem("wr_lo"); lg_mm = sem("lg_mm"); exp_in = sem("exp_in"); exp_out = sem("exp_out")
        taken_done = sem("taken_done"); pos_mm = sem("pos_mm")
        tab_ready = sem("tab_ready"); tab_mm = sem("tab_mm"); lgT_mm = sem("lgT_mm"); lgT_ev = sem("lgT_ev"); tidx_done = sem("tidx_done"); hg_clear = sem("hg_clear"); most_done = sem("most_done")
        ghi = sem("ghi"); glo = sem("glo"); gpe = sem("gpe")
        dhi = sem("dhi"); dlo = sem("dlo"); dpe = sem("dpe")
        t_mm = sem("t_mm"); hg_hi = sem("hg_hi"); hg_lo = sem("hg_lo"); silu_done = sem("silu_done")
        act_done = sem("act_done"); at_mm = sem("at_mm"); at_hi = sem("at_hi"); at_lo = sem("at_lo")
        yA = sem("yA"); yV = sem("yV")
        comb = sem("comb")
        ov = [{k: sem(f"ov{L}_{k}") for k in ("ld", "g", "t", "h", "gu", "s", "a", "at", "aT", "d", "y", "sc")}
              for L in range(NL)]
        dve_chain = sem("dve_chain"); pool_chain = sem("pool_chain")

        def c(name, *shape):
            v = cst[:, at[name][0]:at[name][1]]
            if len(shape) == 1:
                return v.rearrange("p (a b) -> p a b", a=shape[0])
            if len(shape) == 2:
                return v.rearrange("p (a b c) -> p a b c", a=shape[0], b=shape[1])
            return v

        ident = c("ident")
        OFFS = {"q": 0, "k": 1, "v": 2, "g": 3}

        def zq(t, name):
            return z[:, t, OFFS[name], :]

        def heads(ap):
            return ap.rearrange("p (h d) -> p h d", h=NH)

        def over(ap, n, dim=1):
            v = ap.unsqueeze(dim)
            shape = list(v.shape)
            shape[dim] = n
            return v.to_broadcast(shape)

        ZUSES = [len(range(b, 5 * NT, ZB)) for b in range(ZB)]
        EUSES = [len(range(s, NE, 3)) for s in range(3)]

        def z_there(eng, L, g, t):
            m = 5 * g + t
            eng.wait_ge(zfree[m % ZB], L * ZUSES[m % ZB] + m // ZB + 1)

        def used(L, s, n):
            return n + (L * EUSES[s] + 1)

        def ahead(e):
            return isinstance(e, int) and e == AHEAD

        def gu_half(tiles, tiles3, e, s, h):
            return tiles3[h][:, :, :] if ahead(e) else tiles[s][:, 4 * h:4 * h + 4, :]

        def gu_pair(tiles, tiles3, e, s, p):
            return gu_half(tiles, tiles3, e, s, p // 2)[:, 2 * (p % 2):2 * (p % 2) + 2, :].rearrange("p a b -> p (a b)")

        def dn_chunk(tiles, tiles3, e, s, k):
            return tiles3[k][:, :] if ahead(e) else tiles[s][:, k, :]

        def loaded(L, e, s, n):
            if ahead(e):
                return L + 1
            if s or first(e):
                return used(L, s, n) - (0 if s else L)
            return n + L * (EUSES[0] - 1)

        def experts(eng, body):
            def at(e):
                body(e, e % 3, tuple((e + d) // 3 for d in (-1, 0, 1)))
            for e in range(LOOP0):
                at(e)
            with eng.Fori(0, (LOOP1 - LOOP0) // 3) as i:
                for j in range(3):
                    body(i * 3 + (LOOP0 + j), (LOOP0 + j) % 3, tuple(i + (LOOP0 + j + d) // 3 for d in (-1, 0, 1)))
            for e in range(LOOP1, NE):
                at(e)

        def first(e):
            return isinstance(e, int) and e == 0

        def final(e):
            return isinstance(e, int) and e == NE - 1

        B_ON, B_Q, B_O, B_KV, B_OT, B_K, B_SC, B_BACK = 0, 1, (2, 3), 4, (5, 7), 6, 7, 3
        B_SKV = ((4, 2), (1, 6))
        B_W = (1, 2, 4, 5, 6, 7, 0, 3, 1, 2)

        def tr_bank(n, i):
            return ps[(4 if n % 2 else 5) + i % 3][:, :]

        def step_done(eng, S):
            L, s = divmod(S, W_STEPS)
            g, k = divmod(s, KC)
            if k < KC - 1:
                eng.wait_ge(wpe, (W_STEPS * L // KC + g) * (KC - 1) + k + 1)
            elif g < 5:
                eng.wait_ge(zmm, 5 * NT * L + NT * (g + 1))
            else:
                eng.wait_ge(xmm, 2 * NT * L + NT * (g - 4))

        block = ctx.enter_context(nc.Block())

        @block.sync
        def _(sp):
            def load_x(t):
                if t < LAST:
                    sp.dma_start(x[:, t, :], a["x_prompt"][0, t * P:(t + 1) * P, :]).then_inc(row_ld[t], 16)
                else:
                    sp.dma_start(x[0:NSAMP, LAST, :], a["x_sample"].rearrange("b s d -> (b s) d")).then_inc(row_ld[LAST], 16)

            def load_gain(n):
                if n:
                    sp.wait_ge(xn_done, 5 * n)
                src = a["norm_final"] if n == 2 * NL else a[("norm_mix", "norm_ffn")[n % 2]][n // 2]
                sp.dma_start(gain[:, :], src.partition_broadcast(P)).then_inc(gain_ld, 16)

            def load_raw(L, s):
                S = W_STEPS * L + s
                if S >= RAW:
                    sp.wait_ge(wlo, S - RAW + 1)
                if s < RAW and L:
                    sp.wait_ge(dpe, 2 * (NE * L - 1))
                if s < WIN_STEPS:
                    g, k = divmod(s, KC)
                    src = a["w_in"][L, k * P:(k + 1) * P, g * PW:(g + 1) * PW]
                else:
                    n, k = divmod(s - WIN_STEPS, KC)
                    src = a["w_out"][L, k * P:(k + 1) * P, n * PW:(n + 1) * PW]
                sp.dma_start(raw[S % RAW][:, :], src).then_inc(raw_ld[S % RAW], 16)

            def load_gu(L, e, s, after=None):
                for h in range(2):
                    if after is not None:
                        sp.wait_ge(gpe, after * 4 + (4 * NE * L + 2 * h + 2))
                    dst, ld = gu_half(wgu, wgu3, e, s, h), (gu3_ld if ahead(e) else gu_ld[s])[h]
                    rows = slice(4 * h * P, (4 * h + 4) * P)
                    sp.dma_start(dst[:, :, 0:F], a["w_gate"][L, e, rows].rearrange("(k p) f -> p k f", p=P)).then_inc(ld, 16)
                    sp.dma_start(dst[:, :, F:2 * F], a["w_up"][L, e, rows].rearrange("(k p) f -> p k f", p=P)).then_inc(ld, 16)

            def load_dn(L, e, s, after=None):
                for k in range(2):
                    if after is not None:
                        sp.wait_ge(dpe, after * 2 + (2 * NE * L + k + 1))
                    sp.dma_start(dn_chunk(wdn, wdn3, e, s, k), a["w_down"][L, e, k * P:(k + 1) * P]).then_inc((dn3_ld if ahead(e) else dn_ld[s])[k], 16)

            def overflow(L):
                v = ov[L]
                sp.wait_ge(most_done, L + 1)
                n = sp.value_load(most[0:1, 0:1], min_val=0, max_val=2 * TOK)
                with sp.If(n > P):
                    sp.wait_ge(dpe, 2 * NE * (L + 1))
                    sp.sem_inc(v["d"], 1)
                    with sp.Fori(1, NT) as turn:
                        with sp.Fori(0, NE) as e:
                            sp.wait_ge(v["d"], turn * NE + e - NE + 1)
                            sp.dma_start(wgu[0][:, :, 0:F], a["w_gate"][L, e].rearrange("(k p) f -> p k f", p=P)).then_inc(v["ld"], 16)
                            sp.dma_start(wgu[0][:, :, F:2 * F], a["w_up"][L, e].rearrange("(k p) f -> p k f", p=P)).then_inc(v["ld"], 16)
                            sp.dma_start(wdn[0][:, :, :], a["w_down"][L, e].rearrange("(k p) d -> p k d", p=P)).then_inc(v["ld"], 16)
                    sp.wait_ge(v["sc"], 16 * (NT - 1) * NE)
                with sp.Else():
                    sp.wait_ge(most_done, L + 1)

            def small_tables(L):
                if L:
                    sp.wait_ge(comb, 2 * NT * L)
                sp.dma_start(cpn[:, :], a["cache_pool"][L].rearrange("b r c -> (b r) c")).then_inc(small_ld, 16)
                sp.dma_start(wpool[:, :, :], a["w_pool"][L].rearrange("g c e -> c g e")).then_inc(small_ld, 16)
                sp.dma_start(pscale[:, :], a["pool_scale"][L].rearrange("(g e) -> e g", g=NH),
                             allow_slow_non_contiguous=True).then_inc(small_ld, 16)
                sp.dma_start(gnrow[:, :], a["ret_gn"][L].partition_broadcast(P)).then_inc(small_ld, 16)
                sp.dma_start(wr[:, :, 0:4], a["w_router_group"][L].rearrange("(k p) n -> p k n", p=P)).then_inc(small_ld, 16)
                sp.dma_start(wr[:, :, 4:20], a["w_router_expert"][L].rearrange("(k p) n -> p k n", p=P)).then_inc(small_ld, 16)
                sp.dma_start(rbias[:, 0:4], a["b_router_group"][L].partition_broadcast(P)).then_inc(small_ld, 16)
                sp.dma_start(rbias[:, 4:20], a["b_router_expert"][L].partition_broadcast(P)).then_inc(small_ld, 16)
                sp.dma_start(o["new_pool_sample"][L, :, 0:BUF - DECS, :], a["cache_pool"][L, :, DECS:BUF, :]).then_inc(out_st, 16)

            sp.dma_start(cst[:, 0:P], a["cst"][:, 0:P]).then_inc(ident_ld, 16)
            load_x(0)
            load_gain(0)
            for t in range(1, NT):
                load_x(t)
                if t - 1 < RAW:
                    load_raw(0, t - 1)
            sp.dma_start(cst[:, P:], a["cst"][:, P:]).then_inc(cst_ld, 16)
            sp.dma_start(tri[:, :], a["tri"]).then_inc(cst_ld, 16)
            for L in range(NL):
                for s in range(RAW, WIN_STEPS):
                    load_raw(L, s)
                    if s == 6:
                        small_tables(L)
                    if s == 10:
                        load_gain(2 * L + 1)
                    if s == 20:
                        for t in (3, LAST):
                            z_there(sp, L, 0, t)
                        sp.dma_start(o["new_pool_prompt"][L, 0], unat[P - BUF:P, 3, :]).then_inc(upool_st, 16)
                        sp.dma_start(o["new_pool_sample"][L, :, BUF - DECS:BUF, :], unat[0:NSAMP, LAST, :]).then_inc(upool_st, 16)
                for s in range(WIN_STEPS, W_STEPS):
                    load_raw(L, s)
                    if s == WIN_STEPS + KC:
                        sp.wait_ge(on_tr, NT * (L + 1))
                        load_gu(L, 1, 1)
                    if s == WIN_STEPS + KC + 2:
                        load_dn(L, 1, 1)
                    if s == WIN_STEPS + KC + 4:
                        load_gu(L, 2, 2)
                step_done(sp, W_STEPS * (L + 1) - 1)
                load_gu(L, 0, 0)
                load_dn(L, 0, 0)
                load_dn(L, 2, 2)
                load_gain(2 * L + 2)
                for t in (2, 3, LAST):
                    sp.wait_ge(xn_st[t], 16 * (L + 1))
                sp.wait_ge(lg_mm, L + 1)
                load_gu(L, AHEAD, 0)
                load_dn(L, AHEAD, 0)
                load_gu(L, 6, 0, after=0)
                load_gu(L, 4, 1, after=1)
                load_dn(L, 6, 0, after=0)
                load_gu(L, 5, 2, after=2)
                load_dn(L, 4, 1, after=1)
                load_dn(L, 5, 2, after=2)
                load_gu(L, 7, 1, after=4)
                with sp.Fori(0, 2) as i:
                    for j in range(3):
                        load_gu(L, i * 3 + (8 + j), (2 + j) % 3, after=i * 3 + (5 + j))
                        load_dn(L, i * 3 + (7 + j), (1 + j) % 3, after=i * 3 + (4 + j))
                for e in (14, 15):
                    load_gu(L, e, e % 3, after=e - 3)
                    load_dn(L, e - 1, (e - 1) % 3, after=e - 4)
                load_dn(L, NE - 1, 0, after=NE - 4)
                if L + 1 < NL:
                    for s in range(RAW):
                        load_raw(L + 1, s)
                overflow(L)
                for s in range(3):
                    sp.wait_ge(y_sc[s], 16 * EUSES[s] * (L + 1))
                for i in range(2 * NT):
                    t, k = divmod(i, 2)
                    n = P if t < LAST else NSAMP
                    sp.dma_start(back[i][0:n, :], y_d[k * TOK + t * P:k * TOK + t * P + n, :]).then_inc(second_ld if i == 1 else row_ld[t], 16)
            sp.wait_ge(out_st, 16 * NL)
            sp.wait_ge(upool_st, 32 * NL)
            sp.wait_ge(st_st, 16 * NL)
            for h in range(NH):
                sp.wait_ge(s0_st[h], 16 * NL)

        @block.gpsimd
        def _(pool):
            chain = [0]

            def link(ins):
                chain[0] += 1
                ins.then_inc(pool_chain, 1)
                pool.wait_ge(pool_chain, chain[0])

            pool.memset(eps[:, 0:1], EPS_RMS).then_inc(ready0, 1)
            pool.memset(eps[:, 1:2], EPS_GN).then_inc(ready0, 1)
            pool.memset(uT[:, :], 0.0).then_inc(ready0, 1)
            pool.memset(dT[:, SEQ + NSAMP:TOK], 0.0).then_inc(ready0, 1)
            pool.wait_ge(cst_ld, 32)

            def rope_tile(L, t):
                for qk in (0, 1):
                    z_there(pool, L, 1 + qk, t)
                    v = z[:, t, qk, :].rearrange("p (h s d) -> p h s d", h=NH, s=2)
                    cs, sn, ns = (c(n, NT)[:, t, :] for n in ("cos", "sin", "nsin"))
                    cosb = cs.unsqueeze(1).unsqueeze(1).to_broadcast([P, NH, 2, HALF])
                    pool.tensor_tensor(ropA[:, :, :, :], v, cosb, ALU.mult)
                    pool.tensor_tensor(ropB[:, :, 0, :], v[:, :, 1, :], over(ns, NH), ALU.mult)
                    link(pool.tensor_tensor(ropB[:, :, 1, :], v[:, :, 0, :], over(sn, NH), ALU.mult))
                    last = pool.tensor_tensor(v, ropA[:, :, :, :], ropB[:, :, :, :], ALU.add)
                    if qk == 0:
                        link(last)
                last.then_inc(rope, 1)
                pool.wait_ge(rope, NT * L + t + 1)

            def load_s0(L, h):
                pool.dma_start(s0[h][:, :, :], a["state_ret"][L, :, h].rearrange("b d e -> d b e")).then_inc(s0_ld[h], 16)

            def gate_gain(L, t):
                z_there(pool, L, 4, t)
                pool.tensor_tensor(z[:, t, 3, :], z[:, t, 3, :], gnrow[:, :], ALU.mult).then_inc(sg_done, 1)

            def gather(e):
                s = e % 3
                pool.indirect_dma_start(out=hg[s][:, :], out_offset=None, in_=xn_d,
                                        in_offset=bass.IndirectOffsetOnAxis(ap=tidx[:, e:e + 1], axis=0),
                                        bounds_check=TOK - 1, oob_is_err=False).then_inc(gat[s], 16)

            def scatter(L, e):
                s = e % 3
                pool.wait_ge(yA, NE * L + e + 1)
                pool.wait_ge(yV, NE * L + e + 1)
                pool.indirect_dma_start(out=y_d, out_offset=bass.IndirectOffsetOnAxis(ap=pidx[:, e:e + 1], axis=0),
                                        in_=y[s][:, :], in_offset=None,
                                        bounds_check=2 * TOK - 1, oob_is_err=False).then_inc(y_sc[s], 16)

            for L in range(NL):
                for h in range(2):
                    if L:
                        pool.wait_ge(comb, 2 * NT * L)
                    load_s0(L, h)
                w = 0
                for g in range(NH):
                    if g or L:
                        pool.wait_ge(d_done, NH * L + g)
                    if g == NH - 1:
                        for t in range(2):
                            rope_tile(L, t)
                    pool.wait_ge(uT_done, 3 * (NH * L + g + 1))
                    src = uT
                    for r in range(g + 1):
                        dst = (winA, winB)[r % 2]
                        n = 1 << r
                        lo = 2 * n - 1
                        pool.tensor_tensor(dst[:, lo:UW], src[:, lo:UW], src[:, lo - n:UW - n], ALU.add).then_inc(win_done, 1)
                        w += 1
                        pool.wait_ge(win_done, 10 * L + w)
                        src = dst
                pool.wait_ge(d_done, NH * (L + 1))
                rope_tile(L, 2)
                rope_tile(L, 3)
                gate_gain(L, 0)
                gate_gain(L, 1)
                rope_tile(L, LAST)
                pool.wait_ge(zmm, 5 * NT * (L + 1))
                for h in range(2, NH):
                    load_s0(L, h)
                gate_gain(L, 2)
                for h in range(NH):
                    if h >= 2:
                        pool.wait_ge(skv_mm, NH * L + h - 1)
                    pool.tensor_tensor(vb[h % 2][:, :, :], over(zq(LAST, "v")[:, h * P:(h + 1) * P], DECB),
                                       c("seqm").unsqueeze(2).to_broadcast([P, DECB, P]), ALU.mult).then_inc(vb_done, 1)
                    if h < 2:
                        gate_gain(L, 3 + h)
                for h in range(NH):
                    pool.wait_ge(s_new, NH * L + h + 1)
                    pool.dma_start(o["new_ret_sample"][L, :, h].rearrange("b d e -> d b e"), s0[h][:, :, :]).then_inc(s0_st[h], 16)
                pool.wait_ge(lg_mm, L + 1)
                for s in range(3):
                    pool.memset(hg[s][:, :], 0.0).then_inc(hg_clear, 1)
                pool.wait_ge(tidx_done, L + 1)
                pool.wait_ge(hg_clear, 3 * (L + 1))
                for t in range(NT):
                    pool.wait_ge(xn_st[t], 16 * (L + 1))
                for e in range(3):
                    gather(e)
                for e in range(NE):
                    if e + 3 < NE:
                        pool.wait_ge(t_mm, NE * L + e + 1)
                        gather(e + 3)
                    if e >= 2:
                        scatter(L, e - 2)
                scatter(L, NE - 2)
                scatter(L, NE - 1)
                v = ov[L]
                pool.wait_ge(most_done, L + 1)
                n = pool.value_load(most[0:1, 0:1], min_val=0, max_val=2 * TOK)
                with pool.If(n > P):
                    pool.wait_ge(t_mm, NE * (L + 1))
                    for s in range(3):
                        pool.wait_ge(y_sc[s], 16 * EUSES[s] * (L + 1))
                    with pool.Fori(1, NT) as turn:
                        with pool.Fori(0, NE) as e:
                            col = turn * NE + e
                            pool.tensor_copy(gidx[:, :], tidx[:, bass.ds(col, 1)])
                            pool.drain()
                            pool.indirect_dma_start(out=hg[0][:, :], out_offset=None, in_=xn_d,
                                                    in_offset=bass.IndirectOffsetOnAxis(ap=gidx[:, 0:1], axis=0),
                                                    bounds_check=TOK - 1, oob_is_err=False).then_inc(v["g"], 16)
                            pool.wait_ge(v["y"], col - NE + 1)
                            pool.tensor_copy(sidx[:, :], pidx[:, bass.ds(col, 1)])
                            pool.drain()
                            pool.indirect_dma_start(out=y_d, out_offset=bass.IndirectOffsetOnAxis(ap=sidx[:, 0:1], axis=0),
                                                    in_=y[0][:, :], in_offset=None,
                                                    bounds_check=2 * TOK - 1, oob_is_err=False).then_inc(v["sc"], 16)
                            pool.wait_ge(v["sc"], 16 * (col - NE + 1))
                with pool.Else():
                    pool.wait_ge(t_mm, NE * (L + 1))
                pool.wait_ge(t_mm, NE * (L + 1))

        def o_hi(eng, L, t):
            eng.wait_ge(on_tr, NT * L + t + 1)
            eng.activation(hT[:, NH:KC, t * P:(t + 1) * P], heads(ps[B_ON][:, :]), ACT.Copy).then_inc(ohi, 1)

        @block.scalar
        def _(sc):

            def table(func):
                sc.activation(warm[:, :], eps[:, 0:1], func)

            def norm_root(n, t):
                if n == 0:
                    sc.wait_ge(row_ld[t], 16)
                    sc.wait_ge(ready0, 5)
                elif n % 2:
                    sc.wait_ge(xw, 10 * (n // 2) + NT + t + 1)
                    if t >= 3:
                        sc.wait_ge(s0_st[t - 3], 8 * (n + 1))
                else:
                    sc.wait_ge(comb, 10 * (n // 2 - 1) + 2 * (t + 1))
                sc.activation(xn[n % 2][t][:, :], x[:, t, :], ACT.Square, accum_out=ss[:, t:t + 1]).then_inc(sq_done, 1)
                sc.wait_ge(sq_done, NT * n + t + 1)
                sc.activation(rms[:, t:t + 1], ss[:, t:t + 1], ACT.Sqrt, bias=eps[:, 0:1], scale=1.0 / D).then_inc(rms_done, 1)

            def norm_hi(n, t):
                if n % 2:
                    sc.wait_ge(xn_done, NT * n + t + 1)
                    sc.dma_start(xn_d[t * P:(t + 1) * P, :], xn[1][t][:, :]).then_inc(xn_st[t], 16)
                    if t == 0:
                        for h in range(2, NH):
                            sc.wait_ge(s0_st[h], 8 * (n + 1))
                for half in range(2):
                    i = 2 * t + half
                    sc.wait_ge(tr_done, 10 * n + i + 1)
                    sc.activation(hT[:, 4 * half:4 * half + 4, t * P:(t + 1) * P], tr_bank(n, i).rearrange("p (k c) -> p k c", k=4),
                                  ACT.Copy).then_inc(hi_done, 1)

            def norm(n):
                if n == 0:
                    sc.wait_ge(ready0, 5)
                table(ACT.Sqrt)
                norm_root(n, 0)
                for t in range(NT):
                    if t + 1 < NT:
                        norm_root(n, t + 1)
                    if n == 0 and t == 1:
                        for s in range(RAW):
                            w_hi(0, s)
                    norm_hi(n, t)

            def w_hi(L, s):
                S = W_STEPS * L + s
                sc.wait_ge(raw_ld[S % RAW], 16 * (S // RAW + 1))
                if S >= SPL:
                    step_done(sc, S - SPL)
                sc.activation(wh[S % SPL][:, :], raw[S % RAW][:, :], ACT.Copy).then_inc(whi, 1)

            def z_evac(L, g, tiles):
                for t in tiles:
                    m = 5 * g + t
                    sc.wait_ge(zmm, 25 * L + m + 1)
                    dst = unat[:, t, :] if g == 0 else z[:, t, g - 1, :]
                    sc.activation(dst, ps[m % ZB][:, :], ACT.Silu if g == 4 else ACT.Copy).then_inc(zfree[m % ZB], 1)

            def gu_hi(L, e, s, n, pairs=range(4)):
                X = NE * L + e
                for p in pairs:
                    if p % 2 == 0:
                        sc.wait_ge((gu3_ld if ahead(e) else gu_ld[s])[p // 2], loaded(L, e, s, n) * 32)
                    if not first(e):
                        sc.wait_ge(gpe, X * 4 + (p - 3))
                    sc.activation(eh[p][:, :], gu_pair(wgu, wgu3, e, s, p), ACT.Copy).then_inc(ghi, 1)

            def dn_hi(L, e, s, n):
                X = NE * L + e
                for k in range(2):
                    sc.wait_ge((dn3_ld if ahead(e) else dn_ld[s])[k], loaded(L, e, s, n) * 16)
                    if not first(e):
                        sc.wait_ge(dpe, X * 2 + (k - 1))
                    sc.activation(eh[4 + k][:, :], dn_chunk(wdn, wdn3, e, s, k), ACT.Copy).then_inc(dhi, 1)

            def rows_hi(L, e):
                for half in range(2):
                    sc.wait_ge(t_mm, NE * L + e + 1)
                    sc.activation(hgTh[:, 4 * half:4 * half + 4, :], ps[1 + half][:, :].rearrange("p (k c) -> p k c", k=4), ACT.Copy).then_inc(hg_hi, 1)

            def y_evac(L, e, s, n):
                sc.wait_ge(dpe, (NE * L + e) * 2 + 2)
                if L or not (isinstance(n, int) and n == 0):
                    sc.wait_ge(y_sc[s], (used(L, s, n) - 1) * 16)
                sc.activation(y[s][:, 0:512], ps[3][:, :], ACT.Copy).then_inc(yA, 1)

            def expert(L, e, s, n):
                X = NE * L + e
                if not first(e):
                    dn_hi(L, e - 1, (s + 2) % 3, n[0])
                if not final(e):
                    gu_hi(L, e + 1, (s + 1) % 3, n[2], range(3))
                sc.wait_ge(gpe, X * 4 + 4)
                sc.activation(act[:, :], ps[0][:, 0:F], ACT.Silu).then_inc(silu_done, 1)
                if not final(e):
                    rows_hi(L, e + 1)
                    gu_hi(L, e + 1, (s + 1) % 3, n[2], (3,))
                if not first(e):
                    y_evac(L, e - 1, (s + 2) % 3, n[0])
                sc.wait_ge(at_mm, X + 1)
                sc.activation(actTh[:, :, :], ps[5][:, 0:F].rearrange("p (k c) -> p k c", k=2), ACT.Copy).then_inc(at_hi, 1)

            def pool_u(L, g):
                if g or L:
                    sc.wait_ge(d_done, NH * L + g)
                sc.wait_ge(ut_done, NH * L + g + 1)
                samp = uT[:, 16 + SEQ:].rearrange("p (b w) -> p b w", b=DECB)
                sc.activation(uT[:, 16:16 + SEQ], ps[6][:, :], ACT.Copy).then_inc(uT_done, 1)
                sc.activation(samp[:, :, 16:24], ps[7][:, 0:NSAMP].rearrange("p (b s) -> p b s", b=DECB), ACT.Copy).then_inc(uT_done, 1)
                sc.activation(samp[:, :, 1:16], ps[7][:, P:P + DECB * BUF].rearrange("p (b s) -> p b s", b=DECB), ACT.Copy).then_inc(uT_done, 1)

            def pool_hi(L, g):
                sc.wait_ge(small_ld, 128 * (L + 1))
                sc.wait_ge(yp_done, NH * L + g + 1)
                sc.activation(hP[:, g, 0:SEQ], ps[6][:, :], ACT.Copy, scale=pscale[:, g:g + 1]).then_inc(phi, 1)
                sc.activation(hP[:, g, SEQ:TOK], ps[7][:, 0:P], ACT.Copy, scale=pscale[:, g:g + 1]).then_inc(phi, 1)

            def qk_evac(L, t):
                if t == 0:
                    sc.wait_ge(upool_st, 32 * (L + 1))
                sc.wait_ge(qk_tr, NT * L + t + 1)
                sc.activation(qT[t % 2][:, :, :], heads(ps[B_Q][:, :]), ACT.Copy).then_inc(qk_ev, 1)
                sc.activation(kT[t % 2][:, :, :], heads(ps[B_K][:, :]), ACT.Copy).then_inc(qk_ev, 1)

            def key_decay(L, t):
                sc.wait_ge(rope, NT * L + t + 1)
                if t >= 2:
                    sc.wait_ge(kv_mm, LAST * L + t - 1)
                for h in range(NH):
                    last = sc.activation(kd[t % 2][:, h, :], zq(t, "k")[:, h * P:(h + 1) * P], ACT.Copy,
                                         scale=c("kdec", 2)[:, int(t == LAST), h:h + 1])
                last.then_inc(kd_done, 1)

            for L in range(NL):
                if L:
                    for s in range(RAW):
                        w_hi(L, s)
                norm(2 * L)
                for s in range(RAW, WIN_STEPS + SPL):
                    w_hi(L, s)
                    g, k = divmod(s, KC)
                    if s == WIN_STEPS:
                        table(ACT.Silu)
                    if k == 5 and g:
                        pool_u(L, g - 1)
                    if k == 1 and g >= 2:
                        pool_hi(L, g - 2)
                    if k == 2 and g:
                        if g == 5:
                            qk_evac(L, 0)
                        z_evac(L, g - 1, (0, 2, 4) if g < 5 else range(NT))
                table(ACT.Sqrt)
                sc.wait_ge(cst_ld, 32)
                key_decay(L, 0)
                for t in range(NT):
                    if t >= 2:
                        o_hi(sc, L, t - 2)
                    if t < LAST:
                        qk_evac(L, t + 1)
                        key_decay(L, t + 1)
                    else:
                        sc.wait_ge(st_ready, LAST * (L + 1))
                        sc.dma_start(o["new_ret_prompt"][L, 0].rearrange("h d e -> d h e"), st[:, :, :]).then_inc(st_st, 16)
                        o_hi(sc, L, t - 1)
                        for h in range(2):
                            sc.wait_ge(o_mm, (NT + 1) * L + LAST + h + 1)
                            sc.activation(scT[1][:, 2 * h:2 * h + 2, :], heads(ps[B_OT[h]][:, :])[:, 2 * h:2 * h + 2, :], ACT.Copy).then_inc(o_ev, 1)
                    sc.wait_ge(gn_st, NT * L + t + 1)
                    sc.activation(gnrt[:, :], mv[:, :, 1], ACT.Sqrt, bias=eps[:, 1:2], scale=1.0).then_inc(gn_rt, 1)
                for s in range(WIN_STEPS + SPL, W_STEPS):
                    if s == WIN_STEPS + SPL + 3:
                        o_hi(sc, L, LAST)
                    w_hi(L, s)
                norm(2 * L + 1)
                table(ACT.Exp)
                sc.wait_ge(lgT_mm, 2 * L + 1)
                sc.activation(lgT[0:40, 0:TOK // 2], ps[7][0:40, 0:TOK // 2], ACT.Copy).then_inc(lgT_ev, 1)
                sc.wait_ge(exp_in, 2 * L + 1)
                sc.activation(gex[:, :, :], gd[:, :, :], ACT.Exp).then_inc(exp_out, 1)
                sc.wait_ge(exp_in, 2 * L + 2)
                sc.activation(small[:, 5, :], small[:, 4, :], ACT.Exp).then_inc(exp_out, 1)
                table(ACT.Silu)
                gu_hi(L, 0, 0, 0)
                for t in range(2):
                    sc.wait_ge(xn_st[t], 16 * (L + 1))
                rows_hi(L, 0)
                experts(sc, lambda e, s, n: expert(L, e, s, n))
                dn_hi(L, NE - 1, (NE - 1) % 3, (NE - 1) // 3)
                y_evac(L, NE - 1, (NE - 1) % 3, (NE - 1) // 3)
                v = ov[L]
                sc.wait_ge(most_done, L + 1)
                n = sc.value_load(most[0:1, 0:1], min_val=0, max_val=2 * TOK)
                with sc.If(n > P):
                    with sc.Fori(1, (NT - 1) * NE + 1) as i:
                        sc.wait_ge(v["t"], i)
                        for half in range(2):
                            sc.activation(hgT[:, 4 * half:4 * half + 4, :], ps[1 + half][:, :].rearrange("p (k c) -> p k c", k=4), ACT.Copy).then_inc(v["h"], 1)
                        sc.wait_ge(v["gu"], i)
                        sc.activation(act[:, :], ps[0][:, 0:F], ACT.Silu).then_inc(v["s"], 1)
                        sc.wait_ge(v["at"], i)
                        sc.activation(actT[:, :, :], ps[5][:, 0:F].rearrange("p (k c) -> p k c", k=2), ACT.Copy).then_inc(v["aT"], 1)
                        sc.wait_ge(v["d"], i + 1)
                        sc.activation(y[0][:, 0:512], ps[3][:, :], ACT.Copy)
                        sc.activation(y[0][:, 512:D], ps[4][:, :], ACT.Copy).then_inc(v["y"], 1)
                with sc.Else():
                    sc.wait_ge(dpe, 2 * NE * (L + 1))
                sc.wait_ge(dpe, 2 * NE * (L + 1))
            table(ACT.Sqrt)
            norm_root(2 * NL, 0)
            for t in range(NT):
                if t + 1 < NT:
                    norm_root(2 * NL, t + 1)
                sc.wait_ge(xn_done, NT * 2 * NL + t + 1)
                if t < LAST:
                    sc.dma_start(o["y_prompt"][0, t * P:(t + 1) * P, :], xn[0][t][:, :]).then_inc(xn_st[t], 16)
                else:
                    sc.dma_start(o["y_sample"].rearrange("b s d -> (b s) d"), xn[0][t][0:NSAMP, :]).then_inc(xn_st[t], 16)
            for t in range(NT):
                sc.wait_ge(xn_st[t], 16 * (NL + 1))

        def pool_mix(pe, L, g):
            pe.wait_ge(d_done, NH * L + g + 1)
            pe.matmul(ps[6][:, :], wpool[:, g, :], dT[:, 0:SEQ], start=True, stop=True)
            pe.matmul(ps[7][:, 0:P], wpool[:, g, :], dT[:, SEQ:TOK], start=True, stop=True).then_inc(yp_done, 1)

        def on_t(pe, L, t):
            pe.wait_ge(on_done, NT * L + t + 1)
            if t:
                pe.wait_ge(olo, NT * L + t)
            for h in range(NH):
                last = pe.transpose(ps[B_ON][:, h * P:(h + 1) * P], on[t % 2][:, h, :], ident)
            last.then_inc(on_tr, 1)

        @block.tensor
        def _(pe):
            def transposes(n, t):
                pe.wait_ge(ident_ld, 16)
                pe.wait_ge(xn_done, NT * n + t + 1)
                for half in range(2):
                    i = 2 * t + half
                    if i >= 3:
                        pe.wait_ge(lo_done, 10 * n + i - 2)
                    for k in range(4):
                        last = pe.transpose(tr_bank(n, i)[:, k * P:(k + 1) * P], xn[n % 2][t][:, (4 * half + k) * P:(4 * half + k + 1) * P], ident)
                    last.then_inc(tr_done, 1)

            def three(out, hi_l, lo_l, hi_r, lo_r, first, final):
                pe.matmul(out, hi_l, hi_r, start=first, stop=False)
                pe.matmul(out, hi_l, lo_r, start=False, stop=False)
                return pe.matmul(out, lo_l, hi_r, start=False, stop=final)

            def rows_t(s):
                for k in range(KC):
                    last = pe.transpose(ps[1 + k // 4][:, (k % 4) * P:(k % 4 + 1) * P], hg[s][:, k * P:(k + 1) * P], ident)
                return last

            def act_t():
                for k in range(2):
                    last = pe.transpose(ps[5][:, k * P:(k + 1) * P], act[:, k * P:(k + 1) * P], ident)
                return last

            def expert(L, e, s, n):
                X = NE * L + e
                pe.wait_ge(hg_lo, X * 2 + 2)
                if not first(e):
                    pe.wait_ge(act_done, X)
                for p in range(4):
                    pe.wait_ge(glo, X * 4 + (p + 1))
                    for k in (2 * p, 2 * p + 1):
                        half = slice((k % 2) * PW, (k % 2 + 1) * PW)
                        last = three(ps[0][:, :], hgTh[:, k, :], hgTl[:, k, :], eh[p][:, half], gu_half(gul, gul3, e, s, k // 4)[:, k % 4, :],
                                     k == 0, k == KC - 1)
                    last.then_inc(gpe, 1)
                if not final(e):
                    q = (s + 1) % 3
                    pe.wait_ge(gat[q], used(L, q, n[2]) * 16)
                    rows_t(q).then_inc(t_mm, 1)
                if not first(e):
                    down(L, e - 1, (s + 2) % 3)
                pe.wait_ge(act_done, X + 1)
                act_t().then_inc(at_mm, 1)

            def down(L, e, s):
                X = NE * L + e
                pe.wait_ge(at_lo, X + 1)
                if not first(e):
                    pe.wait_ge(yA, X)
                    pe.wait_ge(yV, X)
                for k in range(2):
                    pe.wait_ge(dlo, X * 2 + (k + 1))
                    for m in range(2):
                        cols = slice(m * 512, (m + 1) * 512)
                        last = three(ps[3 + m][:, :], actTh[:, k, :], actTl[:, k, :], eh[4 + k][:, cols],
                                     dn_chunk(dnl, dnl3, e, s, k)[:, cols], k == 0, k == 1)
                    last.then_inc(dpe, 1)

            def win_mm(L, s, t):
                g, k = divmod(s, KC)
                S, m = W_STEPS * L + s, 5 * g + t
                pe.wait_ge(wlo, S + 1)
                if k == 0 and m >= ZB:
                    z_there(pe, L, (m - ZB) // 5, (m - ZB) % 5)
                last = three(ps[m % ZB][:, :], hT[:, k, t * P:(t + 1) * P], lT[:, k, t * P:(t + 1) * P],
                             wh[S % SPL][:, :], wl[S % SPL][:, :], k == 0, k == KC - 1)
                if k == KC - 1:
                    last.then_inc(zmm, 1)
                elif t == LAST:
                    last.then_inc(wpe, 1)

            def wout_mm(L, s, t):
                n, k = divmod(s, KC)
                S, m = W_STEPS * L + WIN_STEPS + s, 5 * n + t
                pe.wait_ge(wlo, S + 1)
                if k == 0 and m >= 8:
                    pe.wait_ge(xw, 10 * L + m - 7)
                h, l = (hP, lP) if k < NH else (hT, lT)
                last = three(ps[B_W[m]][:, :], h[:, k, t * P:(t + 1) * P], l[:, k, t * P:(t + 1) * P],
                             wh[S % SPL][:, :], wl[S % SPL][:, :], k == 0, k == KC - 1)
                if k == KC - 1:
                    last.then_inc(xmm, 1)
                elif t == LAST:
                    last.then_inc(wpe, 1)

            def logits(L, i):
                pe.wait_ge(wr_lo, L + 1)
                pe.wait_ge(lo_done, 10 * (2 * L + 1) + (6, 10)[i])
                cols = slice(i * TOK // 2, (i + 1) * TOK // 2)
                out = ps[(7, 0)[i]]
                for k in range(KC):
                    if k:
                        pe.matmul(out[0:20, 0:TOK // 2], wrs[:, k, 0:20], lT[:, k, cols], start=False, stop=False)
                    last = pe.matmul(out[0:40, 0:TOK // 2], wrs[:, k, :], hT[:, k, cols], start=(k == 0), stop=(k == KC - 1))
                    if k == 0:
                        pe.matmul(out[0:20, 0:TOK // 2], wrs[:, k, 0:20], lT[:, k, cols], start=False, stop=False)
                last.then_inc(lgT_mm, 1)

            def qk_t(L, t):
                T = NT * L + t
                pe.wait_ge(rope, T + 1)
                if t:
                    pe.wait_ge(qk_ev, 2 * T)
                    pe.wait_ge(qd_done, T)
                for h in range(NH):
                    pe.transpose(ps[B_Q][:, h * P:(h + 1) * P], zq(t, "q")[:, h * P:(h + 1) * P], ident)
                for h in range(NH):
                    last = pe.transpose(ps[B_K][:, h * P:(h + 1) * P], zq(t, "k")[:, h * P:(h + 1) * P], ident)
                last.then_inc(qk_tr, 1)

            def back(L, i):
                pe.wait_ge(o_ev, 2 * L + i + 1)
                for h in (2 * i, 2 * i + 1):
                    last = pe.transpose(ps[B_BACK][:, h * P:(h + 1) * P], scT[1][:, h, :], ident)
                if i:
                    last.then_inc(o_back, 1)

            for L in range(NL):
                transposes(2 * L, 0)
                for t in range(NT):
                    if t + 1 < NT:
                        transposes(2 * L, t + 1)
                    pe.wait_ge(lo_done, 10 * 2 * L + 2 * (t + 1))
                    for s in range(RAW):
                        win_mm(L, s, t)
                for s in range(RAW, WIN_STEPS):
                    for t in range(NT):
                        win_mm(L, s, t)
                    g, k = divmod(s, KC)
                    if g and k == 1:
                        if g == 1:
                            for t in range(NT):
                                z_there(pe, L, 0, t)
                            pe.wait_ge(small_ld, 128 * (L + 1))
                            pe.wait_ge(cst_ld, 32)
                        else:
                            pe.wait_ge(plo, 8 * L + 2 * (g - 1))
                        for t in range(LAST):
                            pe.transpose(ps[6][:, t * P:(t + 1) * P], unat[:, t, (g - 1) * P:g * P], ident)
                        pe.transpose(ps[7][:, 0:P], unat[:, LAST, (g - 1) * P:g * P], ident)
                        pe.transpose(ps[7][:, P:P + DECB * BUF], cpn[:, (g - 1) * P:g * P], ident[0:DECB * BUF, 0:DECB * BUF]).then_inc(ut_done, 1)
                    if g and k == 5:
                        pool_mix(pe, L, g - 1)
                    if g == 4 and k == 6:
                        z_there(pe, L, 3, LAST)
                        pe.wait_ge(plo, 8 * (L + 1))
                        qk_t(L, 0)
                for t in range(NT):
                    T = NT * L + t
                    pe.wait_ge(qk_ev, 2 * T + 2)
                    if t:
                        pe.wait_ge(sc_ev, T)
                    for h in range(NH):
                        last = pe.matmul(ps[B_SC][:, h * P:(h + 1) * P], kT[t % 2][:, h, :], qT[t % 2][:, h, :], start=True, stop=True)
                    last.then_inc(sc_mm, 1)
                    if t < LAST:
                        qk_t(L, t + 1)
                    if t == 0:
                        for tile_t in range(NT):
                            z_there(pe, L, 3, tile_t)
                        z_there(pe, L, 4, 0)
                    if t == 1:
                        for tile_t in (1, 3, 4):
                            z_there(pe, L, 4, tile_t)
                    pe.wait_ge(sc_ev, T + 1)
                    pe.wait_ge(qd_done, T + 1)
                    if t < LAST:
                        if t >= 2:
                            pe.wait_ge(gn_free, T - 1)
                        if t:
                            pe.wait_ge(st_ready, 4 * L + t)
                        for h in range(NH):
                            out = ps[B_O[t % 2]][:, h * P:(h + 1) * P]
                            last = pe.matmul(out, scT[t % 2][:, h, :], zq(t, "v")[:, h * P:(h + 1) * P], start=True, stop=(t == 0))
                            if t:
                                last = pe.matmul(out, qdT[t % 2][:, h, :], st[:, h, :], start=False, stop=True)
                        last.then_inc(o_mm, 1)
                        pe.wait_ge(kd_done, T + 1)
                        if t == 0:
                            z_there(pe, L, 4, 2)
                        for h in range(NH):
                            last = pe.matmul(ps[B_KV][:, h * P:(h + 1) * P], kd[t % 2][:, h, :], zq(t, "v")[:, h * P:(h + 1) * P], start=True, stop=True)
                        last.then_inc(kv_mm, 1)
                        if t:
                            on_t(pe, L, t - 1)
                    else:
                        for h in range(NH):
                            out = ps[B_OT[h // 2]][:, h * P:(h + 1) * P]
                            pe.wait_ge(s0_ld[h], 16 * (L + 1))
                            pe.matmul(out, zq(t, "v")[:, h * P:(h + 1) * P], scT[0][:, h, :], start=True, stop=False)
                            for b in range(DECB):
                                last = pe.matmul(out[:, b * DECS:(b + 1) * DECS], s0[h][:, b, :], qdT[0][:, h, b * DECS:(b + 1) * DECS],
                                                 start=False, stop=(b == DECB - 1))
                            if h % 2:
                                last.then_inc(o_mm, 1)
                            pe.wait_ge(vb_done, NH * L + h + 1)
                            if h >= 2:
                                pe.wait_ge(s_new, NH * L + h - 1)
                            elif h == 0:
                                pe.wait_ge(st_ready, 4 * L + 4)
                                pe.wait_ge(kd_done, T + 1)
                                pe.wait_ge(gn_free, T - 1)
                            for n in range(2):
                                last = pe.matmul(ps[B_SKV[h % 2][n]][:, :], kd[0][:, h, :], vb[h % 2][:, 4 * n:4 * n + 4, :], start=True, stop=True)
                            last.then_inc(skv_mm, 1)
                            if h == 0:
                                on_t(pe, L, t - 1)
                            if h == 2:
                                pe.wait_ge(gn_free, T)
                                back(L, 0)
                        back(L, 1)
                pe.wait_ge(phi, 8 * (L + 1))
                pe.wait_ge(s_new, NH * (L + 1))
                for s in range(2 * KC - SPL):
                    if s == 3:
                        on_t(pe, L, LAST)
                    if s == NH:
                        pe.wait_ge(olo, NT * (L + 1))
                    for t in range(NT):
                        wout_mm(L, s, t)
                for t in range(NT + 2):
                    if t < NT:
                        for s in range(2 * KC - SPL, 2 * KC):
                            wout_mm(L, s, t)
                    if t == NT + 1:
                        logits(L, 0)
                    if t >= 2:
                        transposes(2 * L + 1, t - 2)
                logits(L, 1)
                pe.wait_ge(lgT_ev, 2 * (L + 1))
                for t in range(NT):
                    last = pe.transpose(ps[3][:, 40 * t:40 * t + 40], lgT[0:40, t * P:(t + 1) * P], ident[0:40, 0:40])
                last.then_inc(lg_mm, 1)
                pe.wait_ge(taken_done, L + 1)
                for t in range(NT):
                    for u in range(t + 1):
                        pe.matmul(ps[1][:, t * NE:(t + 1) * NE], tri[:, 0:P] if u == t else tri[:, P:2 * P], taken[:, u, :],
                                  start=(u == 0), stop=(u == t))
                for u in range(NT):
                    last = pe.matmul(ps[1][:, 96:96 + NE], tri[:, P:2 * P], taken[:, u, :], start=(u == 0), stop=(u == NT - 1))
                last.then_inc(pos_mm, 1)
                pe.wait_ge(tab_ready, L + 1)
                for i in range(2 * NT):
                    last = pe.matmul(ps[2][:, 0:NT * 2 * NE], atslot[:, i, :], spread[:, i, :], start=(i == 0), stop=(i == 2 * NT - 1))
                last.then_inc(tab_mm, 1)
                pe.wait_ge(gat[0], 16 * used(L, 0, 0))
                rows_t(0).then_inc(t_mm, 1)
                experts(pe, lambda e, s, n: expert(L, e, s, n))
                down(L, NE - 1, (NE - 1) % 3)
                v = ov[L]
                pe.wait_ge(most_done, L + 1)
                n = pe.value_load(most[0:1, 0:1], min_val=0, max_val=2 * TOK)
                with pe.If(n > P):
                    pe.wait_ge(yA, NE * (L + 1))
                    pe.wait_ge(yV, NE * (L + 1))
                    with pe.Fori(1, (NT - 1) * NE + 1) as i:
                        pe.wait_ge(v["g"], 16 * i)
                        rows_t(0).then_inc(v["t"], 1)
                        pe.wait_ge(v["h"], 2 * i)
                        pe.wait_ge(v["ld"], 48 * i)
                        for k in range(KC):
                            last = pe.matmul(ps[0][:, :], hgT[:, k, :], wgu[0][:, k, :], start=(k == 0), stop=(k == KC - 1))
                        last.then_inc(v["gu"], 1)
                        pe.wait_ge(v["a"], i)
                        act_t().then_inc(v["at"], 1)
                        pe.wait_ge(v["aT"], i)
                        for m in range(2):
                            for k in range(2):
                                last = pe.matmul(ps[3 + m][:, :], actT[:, k, :], wdn[0][:, k, m * 512:(m + 1) * 512], start=(k == 0), stop=(k == 1))
                        last.then_inc(v["d"], 1)
                        pe.wait_ge(v["y"], i)
                with pe.Else():
                    pe.wait_ge(yA, NE * (L + 1))
                pe.wait_ge(yV, NE * (L + 1))

        def o_lo(ve, L, t):
            ve.wait_ge(ohi, NT * L + t + 1)
            dst = (slice(None), slice(NH, KC), slice(t * P, (t + 1) * P))
            ve.tensor_tensor(lT[dst], heads(ps[B_ON][:, :]), hT[dst].bitcast(F32), ALU.subtract).then_inc(olo, 1)

        def x_add(ve, L, n, t):
            m = 5 * n + t
            ve.wait_ge(xmm, 10 * L + m + 1)
            v = x[:, t, n * 512:(n + 1) * 512]
            ve.tensor_tensor(v, v, ps[B_W[m]][:, :], ALU.add).then_inc(xw, 1)

        def routing(ve, L, link, gu_lo):
            def col(i):
                return small[:, i, :]

            def wide(ap, n):
                return ap.unsqueeze(2).to_broadcast([P, NT, n])

            def first_of(vals, best, hot):
                link(ve.tensor_tensor(key[:, :, :], vals, wide(best, 4), ALU.is_ge))
                link(ve.tensor_tensor(key[:, :, :], key[:, :, :], c("rank4", NT), ALU.mult))
                link(ve.tensor_reduce(col(9), key[:, :, :], AX.X, ALU.max))
                link(ve.tensor_tensor(hot, key[:, :, :], wide(col(9), 4), ALU.is_equal))

            ve.wait_ge(lgT_mm, 2 * L + 2)
            ve.tensor_copy(lgT[0:40, TOK // 2:TOK], ps[0][0:40, 0:TOK // 2]).then_inc(lgT_ev, 1)
            ve.wait_ge(lg_mm, L + 1)
            parts = ps[3][:, 0:40 * NT].rearrange("p (t n) -> p t n", t=NT)
            link(ve.tensor_tensor(lg[:, :, :], parts[:, :, 0:20], over(rbias[:, :], NT), ALU.add))
            link(ve.tensor_tensor(lg[:, :, :], lg[:, :, :], parts[:, :, 20:40], ALU.add))
            G = lg[:, :, 0:4]
            link(ve.tensor_reduce(col(0), G, AX.X, ALU.max))
            ve.tensor_tensor(gd[:, :, :], G, wide(col(0), 4), ALU.subtract).then_inc(exp_in, 1)
            first_of(G, col(0), ohg[:, :, :])
            link(ve.tensor_tensor(prod[:, :, :, :], lg[:, :, 4:20].rearrange("p t (g j) -> p t g j", g=NG),
                                  ohg[:, :, :].unsqueeze(3).to_broadcast([P, NT, NG, EPG]), ALU.mult))
            link(ve.tensor_reduce(ing[:, :, :], prod[:, :, :, :].rearrange("p t g j -> p t j g"), AX.X, ALU.add))
            link(ve.tensor_reduce(col(1), ing[:, :, :], AX.X, ALU.max))
            first_of(ing[:, :, :], col(1), oh[0][:, :, :])
            link(ve.scalar_tensor_tensor(out=ing[:, :, :], in0=oh[0][:, :, :], scalar=-3.0e38, in1=ing[:, :, :], op0=ALU.mult, op1=ALU.add))
            link(ve.tensor_reduce(col(2), ing[:, :, :], AX.X, ALU.max))
            ve.tensor_tensor(col(4), col(2), col(1), ALU.subtract).then_inc(exp_in, 1)
            first_of(ing[:, :, :], col(2), oh[1][:, :, :])
            for k in range(2):
                last = ve.tensor_tensor(both[:, k, :, :].rearrange("p t (g j) -> p t g j", g=NG),
                                        ohg[:, :, :].unsqueeze(3).to_broadcast([P, NT, NG, EPG]),
                                        over(oh[k][:, :, :], NG, 2), ALU.mult)
            link(last)
            link(ve.tensor_tensor(picked[:, 0, :, :], both[:, 0, :, :], both[:, 1, :, :], ALU.add))
            ve.tensor_tensor(taken[:, :, :], picked[:, 0, :, :], wide(c("valid"), NE), ALU.mult).then_inc(taken_done, 1)
            one = both[:, :, :, :].rearrange("p k t e -> p (k t) e")
            ve.tensor_tensor(named[:, :, :].rearrange("p i (w e) -> p i w e", w=2), over(one, 2, 2),
                             c("pair", 2 * NT).unsqueeze(3).to_broadcast([P, 2 * NT, 2, NE]), ALU.mult)
            ve.wait_ge(exp_out, 2 * L + 1)
            link(ve.tensor_reduce(col(6), gex[:, :, :], AX.X, ALU.add))
            ve.wait_ge(exp_out, 2 * L + 2)
            link(ve.tensor_scalar(col(7), col(5), 1.0, None, ALU.add))
            link(ve.tensor_tensor(col(8), col(6), col(7), ALU.mult))
            link(ve.reciprocal(pgate[:, 0, :], col(8)))
            link(ve.tensor_tensor(pgate[:, 1, :], pgate[:, 0, :], col(5), ALU.mult))
            ve.wait_ge(pos_mm, L + 1)
            link(ve.tensor_tensor(picked[:, :, :, :], both[:, :, :, :], over(ps[1][:, 0:NT * NE].rearrange("p (t e) -> p t e", t=NT), 2), ALU.mult))
            link(ve.tensor_reduce(place_of[:, :], picked[:, :, :, :].rearrange("p k t e -> p (k t) e"), AX.X, ALU.add))
            link(ve.tensor_tensor(reached[:, :, :], place_of[:, :].unsqueeze(2).to_broadcast([P, 2 * NT, NT]), c("turn", 2 * NT), ALU.is_ge))
            link(ve.tensor_reduce(turn1[:, :], reached[:, :, :], AX.X, ALU.add))
            link(ve.scalar_tensor_tensor(out=in_turn[:, :], in0=turn1[:, :], scalar=-float(P), in1=place_of[:, :], op0=ALU.mult, op1=ALU.add))
            link(ve.tensor_tensor(hotturn[:, :, :], turn1[:, :].unsqueeze(2).to_broadcast([P, 2 * NT, NT]), c("nth", 2 * NT), ALU.is_equal))
            ve.tensor_tensor(atslot[:, :, :], over(c("before"), 2 * NT), in_turn[:, :].unsqueeze(2).to_broadcast([P, 2 * NT, P]), ALU.is_equal)
            ve.tensor_tensor(spread[:, :, :].rearrange("p i (j w) -> p i j w", j=NT),
                             hotturn[:, :, :].unsqueeze(3).to_broadcast([P, 2 * NT, NT, 2 * NE]), over(named[:, :, :], NT, 2),
                             ALU.mult).then_inc(tab_ready, 1)
            link(ve.tensor_reduce(most_f[:, :], ps[1][:, 96:96 + NE], AX.X, ALU.max))
            ve.tensor_copy(most[:, :], most_f[:, :]).then_inc(most_done, 1)
            ve.wait_ge(tab_mm, L + 1)
            byslot = ps[2][:, 0:NT * 2 * NE].rearrange("p (j w e) -> p j w e", j=NT, w=2)
            rows = tmpf[:, :].rearrange("p (j e) -> p j e", j=NT)
            empty = small_tab[:, :].rearrange("p (j e) -> p j e", j=NT)
            ve.tensor_scalar(empty, byslot[:, :, 1, :], 0.0, OUT_OF_RANGE, ALU.is_equal, ALU.mult)
            link(ve.tensor_copy(rows, byslot[:, :, 0, :]))
            link(ve.scalar_tensor_tensor(out=rows, in0=byslot[:, :, 1, :], scalar=float(P), in1=rows, op0=ALU.mult, op1=ALU.add))
            link(ve.scalar_tensor_tensor(out=rows, in0=rows, scalar=-float(P), in1=empty, op0=ALU.add, op1=ALU.add))
            ve.tensor_copy(pidx[:, :], tmpf[:, :])
            link(ve.tensor_scalar(small_tab[:, :], tmpf[:, :], float(TOK), -float(TOK), ALU.is_ge, ALU.mult))
            ve.tensor_tensor(tidx[:, :], small_tab[:, :], tmpf[:, :], ALU.add).then_inc(tidx_done, 1)
            gu_lo(L, 0, 0)

        @block.vector
        def _(ve):
            chain = [0]

            def link(ins):
                chain[0] += 1
                ins.then_inc(dve_chain, 1)
                ve.wait_ge(dve_chain, chain[0])

            def norm_lo(n, t):
                for half in range(2):
                    i = 2 * t + half
                    ve.wait_ge(hi_done, 10 * n + i + 1)
                    dst = (slice(None), slice(4 * half, 4 * half + 4), slice(t * P, (t + 1) * P))
                    ve.tensor_tensor(lT[dst], tr_bank(n, i).rearrange("p (k c) -> p k c", k=4), hT[dst].bitcast(F32),
                                     ALU.subtract).then_inc(lo_done, 1)

            def norm(n, add=None):
                if add:
                    add(0, 0)
                    add(0, 1)
                ve.wait_ge(gain_ld, 16 * (n + 1))
                for t in range(NT):
                    if add and t + 1 < NT:
                        add(t + 1, 0)
                    ve.wait_ge(rms_done, NT * n + t + 1)
                    link(ve.reciprocal(rstd[:, t:t + 1], rms[:, t:t + 1]))
                    ve.scalar_tensor_tensor(out=xn[n % 2][t][:, :], in0=x[:, t, :], scalar=rstd[:, t:t + 1], in1=gain[:, :],
                                            op0=ALU.mult, op1=ALU.mult).then_inc(xn_done, 1)
                    if add and t + 1 < NT:
                        add(t + 1, 1)
                    if t and n < 2 * NL:
                        norm_lo(n, t - 1)
                    if n == 0 and t == 1:
                        for s in range(RAW):
                            w_lo(0, s)
                if n < 2 * NL:
                    norm_lo(n, LAST)

            def w_lo(L, s):
                S = W_STEPS * L + s
                ve.wait_ge(whi, S + 1)
                ve.tensor_tensor(wl[S % SPL][:, :], raw[S % RAW][:, :], wh[S % SPL][:, :].bitcast(F32), ALU.subtract).then_inc(wlo, 1)

            def gu_lo(L, e, s, pairs=range(4)):
                for p in pairs:
                    ve.wait_ge(ghi, (NE * L + e) * 4 + (p + 1))
                    ve.tensor_tensor(gu_pair(gul, gul3, e, s, p), gu_pair(wgu, wgu3, e, s, p), eh[p][:, :].bitcast(F32), ALU.subtract).then_inc(glo, 1)

            def dn_lo(L, e, s):
                for k in range(2):
                    ve.wait_ge(dhi, (NE * L + e) * 2 + (k + 1))
                    ve.tensor_tensor(dn_chunk(dnl, dnl3, e, s, k), dn_chunk(wdn, wdn3, e, s, k), eh[4 + k][:, :].bitcast(F32), ALU.subtract).then_inc(dlo, 1)

            def rows_lo(L, e):
                for half in range(2):
                    ve.wait_ge(hg_hi, (NE * L + e) * 2 + (half + 1))
                    ks = slice(4 * half, 4 * half + 4)
                    ve.tensor_tensor(hgTl[:, ks, :], ps[1 + half][:, :].rearrange("p (k c) -> p k c", k=4), hgTh[:, ks, :].bitcast(F32),
                                     ALU.subtract).then_inc(hg_lo, 1)

            def y_evac(L, e, s, n):
                ve.wait_ge(dpe, (NE * L + e) * 2 + 2)
                if L or not (isinstance(n, int) and n == 0):
                    ve.wait_ge(y_sc[s], (used(L, s, n) - 1) * 16)
                ve.tensor_copy(y[s][:, 512:D], ps[4][:, :]).then_inc(yV, 1)

            def expert(L, e, s, n):
                X = NE * L + e
                if not first(e):
                    dn_lo(L, e - 1, (s + 2) % 3)
                if not final(e):
                    gu_lo(L, e + 1, (s + 1) % 3, range(3))
                ve.wait_ge(silu_done, X + 1)
                ve.tensor_tensor(act[:, :], act[:, :], ps[0][:, F:2 * F], ALU.mult).then_inc(act_done, 1)
                if not final(e):
                    rows_lo(L, e + 1)
                    gu_lo(L, e + 1, (s + 1) % 3, (3,))
                if not first(e):
                    y_evac(L, e - 1, (s + 2) % 3, n[0])
                ve.wait_ge(at_hi, X + 1)
                ve.tensor_tensor(actTl[:, :, :], ps[5][:, 0:F].rearrange("p (k c) -> p k c", k=2), actTh[:, :, :].bitcast(F32),
                                 ALU.subtract).then_inc(at_lo, 1)

            ve.memset(x[NSAMP:P, LAST, :], 0.0).then_inc(ready0, 1)
            def pool_d(L, g):
                ve.wait_ge(win_done, 10 * L + (g + 1) * (g + 2) // 2)
                if g or L:
                    ve.wait_ge(yp_done, NH * L + g)
                win = (winA, winB)[g % 2]
                inv = 1.0 / (2 << g)
                link(ve.tensor_tensor(edge[:, :], win[:, 16:32], c("inv", NH)[:, g, :], ALU.mult))
                if g == 0 and L:
                    ve.memset(dT[:, SEQ + NSAMP:TOK], 0.0)
                ve.tensor_tensor(dT[:, 0:16], edge[:, :], uT[:, 16:32], ALU.subtract)
                ve.scalar_tensor_tensor(out=dT[:, 16:SEQ], in0=win[:, 32:16 + SEQ], scalar=inv, in1=uT[:, 32:16 + SEQ],
                                        op0=ALU.mult, op1=ALU.subtract)
                ws = win[:, 16 + SEQ:].rearrange("p (b w) -> p b w", b=DECB)[:, :, 16:24]
                us = uT[:, 16 + SEQ:].rearrange("p (b w) -> p b w", b=DECB)[:, :, 16:24]
                ve.scalar_tensor_tensor(out=dT[:, SEQ:SEQ + NSAMP].rearrange("p (b s) -> p b s", b=DECB), in0=ws, scalar=inv, in1=us,
                                        op0=ALU.mult, op1=ALU.subtract).then_inc(d_done, 1)

            def pool_lo(L, g):
                ve.wait_ge(phi, 8 * L + 2 * g + 1)
                ve.scalar_tensor_tensor(out=lP[:, g, 0:SEQ], in0=ps[6][:, :], scalar=pscale[:, g:g + 1], in1=hP[:, g, 0:SEQ].bitcast(F32),
                                        op0=ALU.mult, op1=ALU.subtract).then_inc(plo, 1)
                ve.wait_ge(phi, 8 * L + 2 * g + 2)
                ve.scalar_tensor_tensor(out=lP[:, g, SEQ:TOK], in0=ps[7][:, 0:P], scalar=pscale[:, g:g + 1], in1=hP[:, g, SEQ:TOK].bitcast(F32),
                                        op0=ALU.mult, op1=ALU.subtract).then_inc(plo, 1)

            def combine(L, t, k):
                i = 2 * t + k
                n = P if t < LAST else NSAMP
                if i == 1:
                    ve.wait_ge(second_ld, 16 * (L + 1))
                elif k == 0:
                    ve.wait_ge(row_ld[t], 16 + (32 if t else 16) * (L + 1))
                if k:
                    ve.wait_ge(comb, 2 * NT * L + 2 * t + 1)
                ve.scalar_tensor_tensor(out=x[0:n, t, :], in0=back[i][0:n, :], scalar=pgate[0:n, k, t:t + 1], in1=x[0:n, t, :],
                                        op0=ALU.mult, op1=ALU.add).then_inc(comb, 1)

            def q_decay(L, t):
                T = NT * L + t
                ve.wait_ge(qk_ev, 2 * T + 1)
                ve.tensor_tensor(qdT[t % 2][:, :, :], heads(ps[B_Q][:, :]), c("qdec", 2, NH)[:, int(t == LAST), :, :], ALU.mult).then_inc(qd_done, 1)

            def o_bank(t):
                return ps[B_O[t % 2] if t < LAST else B_BACK]

            def group_stats(L, t):
                if t < LAST:
                    ve.wait_ge(o_mm, (NT + 1) * L + t + 1)
                for h in range(NH):
                    last = ve.bn_stats(bnst[:, h, :], o_bank(t)[:, h * P:(h + 1) * P])
                link(last)
                for h in range(NH):
                    last = ve.bn_aggr(mv[:, h, :], bnst[:, h, :])
                last.then_inc(gn_st, 1)

            def group_norm(L, t):
                T = NT * L + t
                ve.wait_ge(gn_rt, T + 1)
                link(ve.reciprocal(gnrs[:, :], gnrt[:, :]))
                if t >= 2:
                    ve.wait_ge(on_tr, T - 1)
                for h in range(NH):
                    last = ve.tensor_scalar(on[t % 2][:, h, :], o_bank(t)[:, h * P:(h + 1) * P], mv[:, h, 0:1], gnrs[:, h:h + 1], ALU.subtract, ALU.mult)
                last.then_inc(gn_free, 1)
                ve.wait_ge(gn_free, T + 1)
                ve.wait_ge(sg_done, T + 1)
                ve.tensor_tensor(on[t % 2][:, :, :], on[t % 2][:, :, :], heads(zq(t, "g")), ALU.mult).then_inc(on_done, 1)

            ve.wait_ge(ready0, 5)
            for L in range(NL):
                if L:
                    for s in range(RAW):
                        w_lo(L, s)
                    norm(2 * L, lambda t, k: combine(L - 1, t, k))
                else:
                    norm(0)
                    ve.wait_ge(cst_ld, 32)
                for s in range(RAW, WIN_STEPS + SPL):
                    w_lo(L, s)
                    g, k = divmod(s, KC)
                    if k == 1 and g >= 2:
                        pool_lo(L, g - 2)
                    if s == WIN_STEPS + 2:
                        ve.wait_ge(upool_st, 32 * (L + 1))
                        q_decay(L, 0)
                    if k == 2 and 0 < g < 5:
                        for t in (1, 3):
                            m = 5 * (g - 1) + t
                            ve.wait_ge(zmm, 25 * L + m + 1)
                            dst = unat[:, t, :] if g == 1 else z[:, t, g - 2, :]
                            ve.tensor_copy(dst, ps[m % ZB][:, :]).then_inc(zfree[m % ZB], 1)
                    if k == 0 and g >= 2:
                        pool_d(L, g - 2)
                for t in range(NT):
                    T = NT * L + t
                    kind = int(t == LAST)
                    ve.wait_ge(sc_mm, T + 1)
                    ve.tensor_tensor(scT[t % 2][:, :, :], heads(ps[B_SC][:, :]), c("decay", 2, NH)[:, kind, :, :], ALU.mult).then_inc(sc_ev, 1)
                    if t:
                        group_norm(L, t - 1)
                    if t >= 2:
                        o_lo(ve, L, t - 2)
                    if t < LAST:
                        q_decay(L, t + 1)
                        group_stats(L, t)
                        ve.wait_ge(kv_mm, 4 * L + t + 1)
                        if t == 0 and L:
                            ve.wait_ge(st_st, 16 * L)
                        for h in range(NH):
                            if t == 0:
                                last = ve.tensor_copy(st[:, h, :], ps[B_KV][:, h * P:(h + 1) * P])
                            else:
                                last = ve.scalar_tensor_tensor(out=st[:, h, :], in0=st[:, h, :], scalar=float(chunk_decay[0][h]),
                                                               in1=ps[B_KV][:, h * P:(h + 1) * P], op0=ALU.mult, op1=ALU.add)
                        last.then_inc(st_ready, 1)
                        ve.wait_ge(st_ready, 4 * L + t + 1)
                    else:
                        o_lo(ve, L, t - 1)
                        for h in range(NH):
                            ve.wait_ge(skv_mm, NH * L + h + 1)
                            for n in range(2):
                                v = s0[h][:, 4 * n:4 * n + 4, :]
                                last = ve.scalar_tensor_tensor(out=v, in0=v, scalar=float(chunk_decay[1][h]),
                                                               in1=ps[B_SKV[h % 2][n]][:, :].rearrange("p (b e) -> p b e", b=4), op0=ALU.mult, op1=ALU.add)
                            last.then_inc(s_new, 1)
                        ve.wait_ge(o_back, L + 1)
                        group_stats(L, t)
                        group_norm(L, t)
                        link(ve.tensor_copy(wrs[:, :, 0:20], wr[:, :, :]))
                        ve.tensor_tensor(wrs[:, :, 20:40], wr[:, :, :], wrs[:, :, 0:20].bitcast(F32), ALU.subtract).then_inc(wr_lo, 1)
                for s in range(WIN_STEPS + SPL, W_STEPS):
                    if s == WIN_STEPS + SPL + 3:
                        o_lo(ve, L, LAST)
                    w_lo(L, s)
                    if s == WIN_STEPS + KC + 3:
                        for t in range(NT):
                            x_add(ve, L, 0, t)
                norm(2 * L + 1, lambda t, k: None if k else x_add(ve, L, 1, t))
                routing(ve, L, link, gu_lo)
                rows_lo(L, 0)
                experts(ve, lambda e, s, n: expert(L, e, s, n))
                dn_lo(L, NE - 1, (NE - 1) % 3)
                y_evac(L, NE - 1, (NE - 1) % 3, (NE - 1) // 3)
                v = ov[L]
                ve.wait_ge(most_done, L + 1)
                n = ve.value_load(most[0:1, 0:1], min_val=0, max_val=2 * TOK)
                with ve.If(n > P):
                    with ve.Fori(1, (NT - 1) * NE + 1) as i:
                        ve.wait_ge(v["s"], i)
                        ve.tensor_tensor(act[:, :], act[:, :], ps[0][:, F:2 * F], ALU.mult).then_inc(v["a"], 1)
                with ve.Else():
                    ve.wait_ge(dpe, 2 * NE * (L + 1))
            norm(2 * NL, lambda t, k: combine(NL - 1, t, k))



_INS = ["x_prompt", "x_sample", "cache_pool", "state_ret", "norm_mix", "w_in", "w_pool", "pool_scale", "ret_gn", "w_out",
        "norm_ffn", "w_router_group", "b_router_group", "w_router_expert", "b_router_expert", "w_gate", "w_up", "w_down",
        "norm_final"]
_OUTS = [("y_prompt", (1, SEQ, D)), ("y_sample", (DECB, DECS, D)), ("new_pool_prompt", (NL, 1, BUF, PW)),
         ("new_ret_prompt", (NL, 1, NH, P, P)), ("new_pool_sample", (NL, DECB, BUF, PW)), ("new_ret_sample", (NL, DECB, NH, P, P))]


def kernel(**inputs):
    import concourse.bacc as bacc
    from concourse.bass_utils import run_bass_kernel_spmd as run
    import ml_dtypes

    nc = bacc.Bacc("TRN2", target_bir_lowering=False, num_devices=1)
    arrays, aps = {}, {}
    _, cst, tri, _ = constant_tables()
    host = {k: np.ascontiguousarray(inputs[k]) for k in _INS}
    host.update(cst=cst, tri=tri.astype(ml_dtypes.bfloat16))
    for k, v in host.items():
        arrays[f"in_{k}"] = v
        aps[k] = nc.dram_tensor(f"in_{k}", v.shape, mybir.dt.from_np(v.dtype), kind="ExternalInput").ap()
    outs = {k: nc.dram_tensor(f"out_{k}", s, F32, kind="ExternalOutput").ap() for k, s in _OUTS}
    build(nc, aps, outs)
    r = run(nc, [arrays], core_ids=[0])
    return tuple(r.results[0][f"out_{k}"] for k, _ in _OUTS)
```
